# Optimizing a Trainium2 kernel written in Bass

```python
import math
import jax
import jax.numpy as jnp
from jax import lax
import numpy as np

D_MODEL = 1024
BATCH = 1
SEQ = 256
DEPTH = 1

N_HEADS = 8
HEAD_DIM = 64
ATTN_WIDTH = N_HEADS * HEAD_DIM
ROPE_THETA = 10000.0
MOBA_BLOCK = 256
MOBA_TOPK = 3
Q_CHUNK = 64
SSM_GROUP_SIZE = 16
SSM_GROUPS = 32
SSM_WIDTH = SSM_GROUPS * SSM_GROUP_SIZE
SSM_STATE = 64
DT_MIN = 0.001
DT_MAX = 0.1
IN_WIDTH = SSM_WIDTH + 3 * ATTN_WIDTH + 2 * D_MODEL
N_EXPERTS = 32
TOP_K = 4
D_FF = D_MODEL
SWIGLU_ALPHA = 1.702
SWIGLU_LIMIT = 7.0
MOE_BLOCK = 128
NORM_EPS = 1e-6
NEG_INF = -1e30


def rms_norm(t, g):
    tf = t.astype(jnp.float32)
    tf = tf * lax.rsqrt(jnp.mean(tf * tf, axis=-1, keepdims=True) + NORM_EPS)
    return tf * g.astype(jnp.float32)

def apply_rope(t, positions):
    half = HEAD_DIM // 2
    inv_freq = ROPE_THETA ** (-jnp.arange(half, dtype=jnp.float32) / half)
    ang = positions.astype(jnp.float32)[..., None] * inv_freq
    cos = jnp.cos(ang)[:, :, None, :]
    sin = jnp.sin(ang)[:, :, None, :]
    tf = t.astype(jnp.float32)
    t1, t2 = tf[..., :half], tf[..., half:]
    return jnp.concatenate([t1 * cos - t2 * sin, t2 * cos + t1 * sin], axis=-1)

def _linear_recurrence(left, right):
    a_l, b_l = left
    a_r, b_r = right
    return a_r * a_l, a_r * b_l + b_r

def s5_mixer(u, lam_re, lam_im, log_dt, b_re, b_im, c_re, c_im, d_skip, w_glu):
    bsz, seq, _ = u.shape
    uf = u.astype(jnp.float32)
    ug = uf.reshape(bsz, seq, SSM_GROUPS, SSM_GROUP_SIZE)
    lam = lax.complex(lam_re.astype(jnp.float32), lam_im.astype(jnp.float32))
    dt = jnp.exp(log_dt.astype(jnp.float32))[:, None]
    lam_bar = jnp.exp(lam * dt)
    b_mat = lax.complex(b_re.astype(jnp.float32), b_im.astype(jnp.float32))
    c_mat = lax.complex(c_re.astype(jnp.float32), c_im.astype(jnp.float32))
    b_bar = ((lam_bar - 1.0) / lam)[..., None] * b_mat
    bu = jnp.einsum('gpc,bsgc->bsgp', b_bar, ug.astype(jnp.complex64))
    a = jnp.broadcast_to(lam_bar, bu.shape)
    _, states = lax.associative_scan(_linear_recurrence, (a, bu), axis=1)
    y = jnp.einsum('gcp,bsgp->bsgc', c_mat, states).real.reshape(bsz, seq, SSM_WIDTH)
    y = y + d_skip.astype(jnp.float32) * uf
    y = jax.nn.gelu(y)
    y = y * jax.nn.sigmoid(y @ w_glu.astype(jnp.float32))
    return y

def moba_attention(q, k, v):
    bsz, nh, seq, hd = q.shape
    qf, kf, vf = q.astype(jnp.float32), k.astype(jnp.float32), v.astype(jnp.float32)
    nb = -(-seq // MOBA_BLOCK)
    pad = nb * MOBA_BLOCK - seq
    kb = jnp.pad(kf, ((0, 0), (0, 0), (0, pad), (0, 0))).reshape(bsz, nh, nb, MOBA_BLOCK, hd)
    vb = jnp.pad(vf, ((0, 0), (0, 0), (0, pad), (0, 0))).reshape(bsz, nh, nb, MOBA_BLOCK, hd)
    k_mean = jnp.mean(kb, axis=3)
    n_sel = min(MOBA_TOPK, nb)
    scale = HEAD_DIM ** -0.5
    n_chunks = seq // Q_CHUNK
    q_chunks = qf.reshape(bsz, nh, n_chunks, Q_CHUNK, hd).transpose(2, 0, 1, 3, 4)
    gather_blocks = jax.vmap(jax.vmap(lambda blocks, idx: blocks[idx]))
    block_ids = jnp.arange(nb)
    offs = jnp.arange(MOBA_BLOCK)

    def chunk_attend(args):
        ci, qi = args
        q_pos = ci * Q_CHUNK + jnp.arange(Q_CHUNK)
        q_blk = q_pos // MOBA_BLOCK
        own = (ci * Q_CHUNK) // MOBA_BLOCK
        gate = jnp.einsum('bhqd,bhnd->bhqn', qi, k_mean)
        gate = jnp.where(block_ids[None, :] < q_blk[:, None], gate, NEG_INF)
        _, sel = lax.top_k(gate, n_sel)
        sel_ok = sel < q_blk[:, None]
        k_sel = gather_blocks(kb, sel)
        v_sel = gather_blocks(vb, sel)
        s_sel = jnp.einsum('bhqd,bhqnld->bhqnl', qi, k_sel) * scale
        s_sel = jnp.where(sel_ok[..., None], s_sel, NEG_INF).reshape(bsz, nh, Q_CHUNK, n_sel * MOBA_BLOCK)
        k_own = lax.dynamic_index_in_dim(kb, own, axis=2, keepdims=False)
        v_own = lax.dynamic_index_in_dim(vb, own, axis=2, keepdims=False)
        s_own = jnp.einsum('bhqd,bhld->bhql', qi, k_own) * scale
        k_pos = own * MOBA_BLOCK + offs
        s_own = jnp.where(k_pos[None, :] <= q_pos[:, None], s_own, NEG_INF)
        p = jax.nn.softmax(jnp.concatenate([s_sel, s_own], axis=-1), axis=-1)
        p_sel = p[..., :n_sel * MOBA_BLOCK].reshape(bsz, nh, Q_CHUNK, n_sel, MOBA_BLOCK)
        p_own = p[..., n_sel * MOBA_BLOCK:]
        return (jnp.einsum('bhqnl,bhqnld->bhqd', p_sel, v_sel)
                + jnp.einsum('bhql,bhld->bhqd', p_own, v_own))

    out = lax.map(chunk_attend, (jnp.arange(n_chunks), q_chunks))
    return out.transpose(1, 2, 0, 3, 4).reshape(bsz, nh, seq, hd)

def moe_ffn(h, router_w, router_b, w_gate, b_gate, w_up, b_up, w_down, b_down):
    bsz, seq, d = h.shape
    n_tok = bsz * seq
    hf = h.reshape(n_tok, d).astype(jnp.float32)
    logits = hf @ router_w.astype(jnp.float32) + router_b.astype(jnp.float32)
    top_val, top_idx = lax.top_k(logits, TOP_K)
    top_w = jax.nn.softmax(top_val, axis=-1)
    n_assign = n_tok * TOP_K
    eid = top_idx.reshape(n_assign)
    order = jnp.argsort(eid)
    s_eid = eid[order]
    s_tok = order // TOP_K
    s_w = top_w.reshape(n_assign)[order]
    counts = jnp.bincount(eid, length=N_EXPERTS)
    starts = jnp.cumsum(counts) - counts
    padded = (counts + MOE_BLOCK - 1) // MOE_BLOCK * MOE_BLOCK
    p_ends = jnp.cumsum(padded)
    p_starts = p_ends - padded
    dest = p_starts[s_eid] + jnp.arange(n_assign) - starts[s_eid]
    n_blocks = -(-n_assign // MOE_BLOCK) + N_EXPERTS
    n_rows = n_blocks * MOE_BLOCK
    row_tok = jnp.full((n_rows,), n_tok, dtype=jnp.int32).at[dest].set(s_tok.astype(jnp.int32))
    row_w = jnp.zeros((n_rows,), jnp.float32).at[dest].set(s_w)
    blk_exp = jnp.minimum(jnp.searchsorted(p_ends, jnp.arange(n_blocks) * MOE_BLOCK, side='right'),
                          N_EXPERTS - 1)
    h_pad = jnp.concatenate([hf, jnp.zeros((1, d), jnp.float32)], axis=0)
    xs = h_pad[row_tok].reshape(n_blocks, MOE_BLOCK, d)

    def expert_block(args):
        xb, e = args
        g = xb @ w_gate[e].astype(jnp.float32) + b_gate[e].astype(jnp.float32)
        u = xb @ w_up[e].astype(jnp.float32) + b_up[e].astype(jnp.float32)
        g = jnp.minimum(g, SWIGLU_LIMIT)
        u = jnp.clip(u, -SWIGLU_LIMIT, SWIGLU_LIMIT)
        act = g * jax.nn.sigmoid(SWIGLU_ALPHA * g) * (u + 1.0)
        return act @ w_down[e].astype(jnp.float32) + b_down[e].astype(jnp.float32)

    yb = lax.map(expert_block, (xs, blk_exp)).reshape(n_rows, d)
    y = jnp.zeros((n_tok + 1, d), jnp.float32).at[row_tok].add(yb * row_w[:, None])
    return y[:n_tok].reshape(bsz, seq, d)

def first_inputs(seed: int = 0) -> dict:
    key = jax.random.key(seed)
    ks = jax.random.split(key, 32)
    f32 = jnp.float32
    nrm = lambda k, shape, s: jax.random.normal(k, shape, f32) * s
    L, D, G, P, HG, E, F = DEPTH, D_MODEL, SSM_GROUPS, SSM_STATE, SSM_GROUP_SIZE, N_EXPERTS, D_FF
    x = jax.random.normal(ks[0], (BATCH, SEQ, D), f32)
    c = jax.random.normal(ks[1], (BATCH, D), f32)
    offset = jax.random.randint(ks[2], (BATCH, 1), 0, 1024, dtype=jnp.int32)
    positions = (jnp.arange(SEQ, dtype=jnp.int32)[None, :] + offset).astype(jnp.int32)
    lam_im0 = jnp.pi * jnp.arange(P, dtype=f32)
    return {
        'x': x,
        'c': c,
        'positions': positions,
        'ada_w': nrm(ks[3], (L, D, 6 * D), 0.5 * D ** -0.5),
        'ada_b': nrm(ks[4], (L, 6 * D), 0.01),
        'mix_pre_g': 1.0 + nrm(ks[5], (L, D), 0.05),
        'mix_post_g': 1.0 + nrm(ks[6], (L, D), 0.05),
        'ffn_pre_g': 1.0 + nrm(ks[7], (L, D), 0.05),
        'ffn_post_g': 1.0 + nrm(ks[8], (L, D), 0.05),
        'w_in': nrm(ks[9], (L, D, IN_WIDTH), D ** -0.5),
        'ssm_lam_re': -0.5 + nrm(ks[10], (L, G, P), 0.01),
        'ssm_lam_im': lam_im0 + nrm(ks[11], (L, G, P), 0.01),
        'ssm_log_dt': jax.random.uniform(ks[12], (L, G), f32, math.log(DT_MIN), math.log(DT_MAX)),
        'ssm_b_re': nrm(ks[13], (L, G, P, HG), (2 * HG) ** -0.5),
        'ssm_b_im': nrm(ks[14], (L, G, P, HG), (2 * HG) ** -0.5),
        'ssm_c_re': nrm(ks[15], (L, G, HG, P), (2 * P) ** -0.5),
        'ssm_c_im': nrm(ks[16], (L, G, HG, P), (2 * P) ** -0.5),
        'ssm_d': nrm(ks[17], (L, SSM_WIDTH), 1.0),
        'ssm_w_glu': nrm(ks[18], (L, SSM_WIDTH, SSM_WIDTH), SSM_WIDTH ** -0.5),
        'w_ssm_branch': nrm(ks[19], (L, SSM_WIDTH, D), SSM_WIDTH ** -0.5),
        'w_attn_branch': nrm(ks[20], (L, ATTN_WIDTH, D), ATTN_WIDTH ** -0.5),
        'w_out': nrm(ks[21], (L, D, D), D ** -0.5),
        'router_w': nrm(ks[22], (L, D, E), D ** -0.5),
        'router_b': nrm(ks[23], (L, E), 0.01),
        'w_gate': nrm(ks[24], (L, E, D, F), D ** -0.5),
        'b_gate': nrm(ks[25], (L, E, F), 0.01),
        'w_up': nrm(ks[26], (L, E, D, F), D ** -0.5),
        'b_up': nrm(ks[27], (L, E, F), 0.01),
        'w_down': nrm(ks[28], (L, E, F, D), F ** -0.5),
        'b_down': nrm(ks[29], (L, E, D), 0.01),
    }

def first_block(x, c, positions, ada_w, ada_b, mix_pre_g, mix_post_g, ffn_pre_g, ffn_post_g,
              w_in, ssm_lam_re, ssm_lam_im, ssm_log_dt, ssm_b_re, ssm_b_im, ssm_c_re, ssm_c_im,
              ssm_d, ssm_w_glu, w_ssm_branch, w_attn_branch, w_out,
              router_w, router_b, w_gate, b_gate, w_up, b_up, w_down, b_down):
    bsz, seq, _ = x.shape
    dtype = x.dtype
    cond = jax.nn.silu(c.astype(jnp.float32))
    splits = [SSM_WIDTH, SSM_WIDTH + ATTN_WIDTH, SSM_WIDTH + 2 * ATTN_WIDTH,
              SSM_WIDTH + 3 * ATTN_WIDTH, SSM_WIDTH + 3 * ATTN_WIDTH + D_MODEL]
    for l in range(DEPTH):
        ada = cond @ ada_w[l].astype(jnp.float32) + ada_b[l].astype(jnp.float32)
        sh_m, sc_m, gt_m, sh_f, sc_f, gt_f = [a[:, None, :] for a in jnp.split(ada, 6, axis=-1)]

        h = (rms_norm(x, mix_pre_g[l]) * (1.0 + sc_m) + sh_m).astype(dtype)
        proj = h @ w_in[l]
        u_s, q, k, v, g_s, g_a = jnp.split(proj, splits, axis=-1)
        y_s = s5_mixer(u_s, ssm_lam_re[l], ssm_lam_im[l], ssm_log_dt[l], ssm_b_re[l], ssm_b_im[l],
                       ssm_c_re[l], ssm_c_im[l], ssm_d[l], ssm_w_glu[l])
        q = apply_rope(q.reshape(bsz, seq, N_HEADS, HEAD_DIM), positions).transpose(0, 2, 1, 3)
        k = apply_rope(k.reshape(bsz, seq, N_HEADS, HEAD_DIM), positions).transpose(0, 2, 1, 3)
        v = v.reshape(bsz, seq, N_HEADS, HEAD_DIM).transpose(0, 2, 1, 3)
        y_a = moba_attention(q, k, v).transpose(0, 2, 1, 3).reshape(bsz, seq, ATTN_WIDTH)
        merged = (jax.nn.sigmoid(g_s.astype(jnp.float32)) * (y_s @ w_ssm_branch[l].astype(jnp.float32))
                  + jax.nn.sigmoid(g_a.astype(jnp.float32)) * (y_a @ w_attn_branch[l].astype(jnp.float32)))
        mix = merged @ w_out[l].astype(jnp.float32)
        x = (x.astype(jnp.float32) + gt_m * rms_norm(mix, mix_post_g[l])).astype(dtype)

        h2 = (rms_norm(x, ffn_pre_g[l]) * (1.0 + sc_f) + sh_f).astype(dtype)
        ff = moe_ffn(h2, router_w[l], router_b[l], w_gate[l], b_gate[l], w_up[l], b_up[l],
                     w_down[l], b_down[l])
        x = (x.astype(jnp.float32) + gt_f * rms_norm(ff, ffn_post_g[l])).astype(dtype)
    return x


DEPTH_2 = 2

NEG_INF_2 = -1e30
TINY = 1e-30
D_FF_2 = 2816
Q_BLOCK = 128

MLA_HEADS = 8
MLA_NOPE = 64
MLA_ROPE = 32
MLA_V = 64
MLA_Q_LORA = 256
MLA_KV_LORA = 128

GLA_HEADS = 4
GLA_DK = 64
GLA_DV = 128
GLA_GATE_RANK = 16
GLA_GATE_TAU = 16.0
GLA_CHUNK = 64

NSA_HEADS = 16
NSA_KV_GROUPS = 4
NSA_HEAD_DIM = 64
NSA_CMP_LEN = 32
NSA_CMP_STRIDE = 16
NSA_CMP_HIDDEN = 128
NSA_SEL_LEN = 64
NSA_TOP_N = 16
NSA_WINDOW = 512
NSA_Q_BLOCK = 64
NSA_FORCE_SCORE = 1e4

HY_SPLITS = (MLA_Q_LORA, MLA_KV_LORA, MLA_ROPE, GLA_HEADS * GLA_DK, GLA_HEADS * GLA_DK,
             GLA_HEADS * GLA_DV, GLA_GATE_RANK, GLA_HEADS * GLA_DV)
HY_IN = sum(HY_SPLITS)
HY_OUT = MLA_HEADS * MLA_V + GLA_HEADS * GLA_DV
NSA_KV_WIDTH = NSA_KV_GROUPS * NSA_HEAD_DIM
NSA_SPLITS = (NSA_HEADS * NSA_HEAD_DIM,) + (NSA_KV_WIDTH,) * 6 + (NSA_HEADS * 3,)
NSA_IN = sum(NSA_SPLITS)
NSA_OUT = NSA_HEADS * NSA_HEAD_DIM
N_EVEN = (DEPTH_2 + 1) // 2
N_ODD = DEPTH_2 // 2


def split_cols(h, sizes):
    return jnp.split(h, np.cumsum(sizes)[:-1].tolist(), axis=-1)

def rms_norm_2(x, g):
    xf = x.astype(jnp.float32)
    y = xf * lax.rsqrt(jnp.mean(xf * xf, axis=-1, keepdims=True) + NORM_EPS)
    return (y * g.astype(jnp.float32)).astype(x.dtype)

def rope(x, pos):
    d = x.shape[-1]
    inv_freq = jnp.power(ROPE_THETA, -jnp.arange(d // 2, dtype=jnp.float32) * (2.0 / d))
    ang = pos.astype(jnp.float32)[..., None] * inv_freq
    cos = jnp.cos(ang)[:, :, None, :]
    sin = jnp.sin(ang)[:, :, None, :]
    xf = x.astype(jnp.float32)
    x1, x2 = xf[..., : d // 2], xf[..., d // 2:]
    return jnp.concatenate([x1 * cos - x2 * sin, x2 * cos + x1 * sin], axis=-1).astype(x.dtype)

def masked_softmax(s, mask):
    s = jnp.where(mask, s.astype(jnp.float32), NEG_INF_2)
    m = jnp.max(s, axis=-1, keepdims=True)
    p = jnp.where(mask, jnp.exp(s - m), 0.0)
    return p / jnp.maximum(jnp.sum(p, axis=-1, keepdims=True), TINY)

def swiglu(x, w_gate, w_up, w_down):
    return (jax.nn.silu(x @ w_gate) * (x @ w_up)) @ w_down

def causal_block_attention(q, k, v, scale):
    B, S, H, Dk = q.shape
    nb = S // Q_BLOCK
    q_blocks = q.reshape(B, nb, Q_BLOCK, H, Dk).transpose(1, 0, 2, 3, 4)
    key_pos = jnp.arange(S)

    def one_block(args):
        i, qb = args
        s = jnp.einsum('bqhd,bkhd->bhqk', qb, k, preferred_element_type=jnp.float32) * scale
        q_pos = i * Q_BLOCK + jnp.arange(Q_BLOCK)
        p = masked_softmax(s, key_pos[None, :] <= q_pos[:, None])
        return jnp.einsum('bhqk,bkhd->bqhd', p.astype(v.dtype), v)

    out = lax.map(one_block, (jnp.arange(nb), q_blocks))
    return out.transpose(1, 0, 2, 3, 4).reshape(B, S, H, v.shape[-1])

def mla_heads(c_q, c_kv, k_r, positions, q_norm, w_uq, kv_norm, w_ukv):
    B, S, _ = c_q.shape
    q = (rms_norm_2(c_q, q_norm) @ w_uq).reshape(B, S, MLA_HEADS, MLA_NOPE + MLA_ROPE)
    q_nope, q_rot = q[..., :MLA_NOPE], rope(q[..., MLA_NOPE:], positions)
    kv = (rms_norm_2(c_kv, kv_norm) @ w_ukv).reshape(B, S, MLA_HEADS, MLA_NOPE + MLA_V)
    k_nope, v = kv[..., :MLA_NOPE], kv[..., MLA_NOPE:]
    k_rot = rope(k_r.reshape(B, S, 1, MLA_ROPE), positions)
    q_full = jnp.concatenate([q_nope, q_rot], axis=-1)
    k_full = jnp.concatenate([k_nope, jnp.broadcast_to(k_rot, (B, S, MLA_HEADS, MLA_ROPE))], axis=-1)
    o = causal_block_attention(q_full, k_full, v, (MLA_NOPE + MLA_ROPE) ** -0.5)
    return o.reshape(B, S, MLA_HEADS * MLA_V)

def gla_heads(h_q, h_k, h_v, h_a, h_r, w_a2, b_a, out_norm):
    B, S, _ = h_q.shape
    H, DK, DV, C = GLA_HEADS, GLA_DK, GLA_DV, GLA_CHUNK
    nc = S // C
    f32 = jnp.float32
    q = h_q.reshape(B, nc, C, H, DK).astype(f32) * DK ** -0.5
    k = h_k.reshape(B, nc, C, H, DK).astype(f32)
    v = h_v.reshape(B, nc, C, H, DV).astype(f32)
    log_a = jax.nn.log_sigmoid((h_a @ w_a2 + b_a).astype(f32)) / GLA_GATE_TAU
    b = jnp.cumsum(log_a.reshape(B, nc, C, H, DK), axis=2)
    b_last = b[:, :, -1:]
    k_dec = k * jnp.exp(b_last - b)
    q_inter = q * jnp.exp(b)
    q_intra = q * jnp.exp(b - b_last)
    causal = jnp.tril(jnp.ones((C, C), dtype=bool))
    A = jnp.where(causal, jnp.einsum('bnihd,bnjhd->bnhij', q_intra, k_dec), 0.0)
    o_intra = jnp.einsum('bnhij,bnjhv->bnihv', A, v)
    kv_chunk = jnp.einsum('bnjhd,bnjhv->nbhdv', k_dec, v)
    decay_chunk = jnp.exp(b[:, :, -1]).transpose(1, 0, 2, 3)

    def step(state, inp):
        dec, kv = inp
        return state * dec[..., None] + kv, state

    _, s_prev = lax.scan(step, jnp.zeros((B, H, DK, DV), f32), (decay_chunk, kv_chunk))
    o_inter = jnp.einsum('bnihd,nbhdv->bnihv', q_inter, s_prev)
    o = rms_norm_2((o_intra + o_inter).reshape(B, S, H, DV), out_norm)
    o = o * jax.nn.silu(h_r.reshape(B, S, H, DV).astype(f32))
    return o.reshape(B, S, H * DV).astype(h_q.dtype)

def mla_gla_mixer(u, positions, w_in, q_norm, w_uq, kv_norm, w_ukv, w_a2, b_a, out_norm, w_out):
    c_q, c_kv, k_r, g_q, g_k, g_v, g_a, g_r = split_cols(u @ w_in, HY_SPLITS)
    o_mla = mla_heads(c_q, c_kv, k_r, positions, q_norm, w_uq, kv_norm, w_ukv)
    o_gla = gla_heads(g_q, g_k, g_v, g_a, g_r, w_a2, b_a, out_norm)
    return jnp.concatenate([o_mla, o_gla.astype(o_mla.dtype)], axis=-1) @ w_out

def nsa_mixer(u, positions, w_in, pos_k, pos_v, ck_w1, ck_w2, cv_w1, cv_w2, w_out):
    B, S, _ = u.shape
    H, G, Dh = NSA_HEADS, NSA_KV_GROUPS, NSA_HEAD_DIM
    Hg = H // G
    dt = u.dtype
    q, k_c, v_c, k_s, v_s, k_w, v_w, g = split_cols(u @ w_in, NSA_SPLITS)
    q = rope(q.reshape(B, S, H, Dh), positions)
    gates = jax.nn.sigmoid(g.reshape(B, S, H, 3))

    n_cmp = (S - NSA_CMP_LEN) // NSA_CMP_STRIDE + 1
    cmp_start = np.arange(n_cmp) * NSA_CMP_STRIDE
    cmp_end = cmp_start + NSA_CMP_LEN - 1
    cmp_idx = cmp_start[:, None] + np.arange(NSA_CMP_LEN)[None, :]

    def compress(t, pos_emb, w1, w2):
        blocks = t.reshape(B, S, G, Dh)[:, cmp_idx] + pos_emb[None, None, :, None, :]
        flat = blocks.transpose(0, 1, 3, 2, 4).reshape(B, n_cmp, G, NSA_CMP_LEN * Dh)
        return jax.nn.silu(flat @ w1) @ w2

    k_cmp = rope(compress(k_c, pos_k, ck_w1, ck_w2), positions[:, cmp_end])
    v_cmp = compress(v_c, pos_v, cv_w1, cv_w2)
    cmp_end_j = jnp.asarray(cmp_end)

    n_blk = S // NSA_SEL_LEN
    n_pad = max(n_blk, NSA_TOP_N)

    def to_blocks(t):
        tb = t.reshape(B, n_blk, NSA_SEL_LEN, G, Dh).transpose(0, 3, 1, 2, 4)
        return jnp.pad(tb, ((0, 0), (0, 0), (0, n_pad - n_blk), (0, 0), (0, 0)))

    k_sel_all = to_blocks(rope(k_s.reshape(B, S, G, Dh), positions))
    v_sel_all = to_blocks(v_s.reshape(B, S, G, Dh))
    blk_start = np.arange(n_pad) * NSA_SEL_LEN
    ov = np.minimum(cmp_start[:, None] + NSA_CMP_LEN, blk_start[None, :] + NSA_SEL_LEN) - np.maximum(cmp_start[:, None], blk_start[None, :])
    overlap = jnp.asarray(np.clip(ov, 0, None) / NSA_CMP_LEN, dtype=jnp.float32)

    pad_w = ((0, 0), (NSA_WINDOW, 0), (0, 0), (0, 0))
    k_win = jnp.pad(rope(k_w.reshape(B, S, G, Dh), positions), pad_w)
    v_win = jnp.pad(v_w.reshape(B, S, G, Dh), pad_w)

    nq = S // NSA_Q_BLOCK
    q_blocks = q.reshape(B, nq, NSA_Q_BLOCK, G, Hg, Dh).transpose(1, 0, 2, 3, 4, 5)
    g_blocks = gates.reshape(B, nq, NSA_Q_BLOCK, G, Hg, 3).transpose(1, 0, 2, 3, 4, 5)
    bi = jnp.arange(B)[:, None, None, None]
    gi = jnp.arange(G)[None, :, None, None]
    scale = Dh ** -0.5
    span = NSA_Q_BLOCK + NSA_WINDOW

    def one_block(args):
        i, qb, gb = args
        t = i * NSA_Q_BLOCK + jnp.arange(NSA_Q_BLOCK)
        s_c = jnp.einsum('bqghd,bngd->bghqn', qb, k_cmp, preferred_element_type=jnp.float32) * scale
        p_c = masked_softmax(s_c, cmp_end_j[None, :] <= t[:, None])
        o_c = jnp.einsum('bghqn,bngd->bqghd', p_c.astype(dt), v_cmp)
        imp = jnp.einsum('bghqn,nm->bgqm', p_c, overlap)
        blk = jnp.arange(n_pad)[None, :]
        cur = (t // NSA_SEL_LEN)[:, None]
        forced = (blk == 0) | (blk == cur) | (blk == cur - 1)
        score = jnp.where(blk <= cur, jnp.where(forced, NSA_FORCE_SCORE, imp), NEG_INF_2)
        _, sel = lax.top_k(score, NSA_TOP_N)
        k_sel = k_sel_all[bi, gi, sel].reshape(B, G, NSA_Q_BLOCK, NSA_TOP_N * NSA_SEL_LEN, Dh)
        v_sel = v_sel_all[bi, gi, sel].reshape(B, G, NSA_Q_BLOCK, NSA_TOP_N * NSA_SEL_LEN, Dh)
        kpos = (sel[..., None] * NSA_SEL_LEN + jnp.arange(NSA_SEL_LEN)).reshape(B, G, NSA_Q_BLOCK, -1)
        s_s = jnp.einsum('bqghd,bgqmd->bghqm', qb, k_sel, preferred_element_type=jnp.float32) * scale
        p_s = masked_softmax(s_s, (kpos <= t[None, None, :, None])[:, :, None])
        o_s = jnp.einsum('bghqm,bgqmd->bqghd', p_s.astype(dt), v_sel)
        start = i * NSA_Q_BLOCK
        k_wb = lax.dynamic_slice_in_dim(k_win, start, span, axis=1)
        v_wb = lax.dynamic_slice_in_dim(v_win, start, span, axis=1)
        wpos = (start - NSA_WINDOW + jnp.arange(span))[None, :]
        m_w = (wpos <= t[:, None]) & (wpos > t[:, None] - NSA_WINDOW) & (wpos >= 0)
        s_w = jnp.einsum('bqghd,bkgd->bghqk', qb, k_wb, preferred_element_type=jnp.float32) * scale
        p_w = masked_softmax(s_w, m_w)
        o_w = jnp.einsum('bghqk,bkgd->bqghd', p_w.astype(dt), v_wb)
        return gb[..., 0:1] * o_c + gb[..., 1:2] * o_s + gb[..., 2:3] * o_w

    out = lax.map(one_block, (jnp.arange(nq), q_blocks, g_blocks))
    return out.transpose(1, 0, 2, 3, 4, 5).reshape(B, S, NSA_OUT) @ w_out

def second_inputs(seed: int = 0) -> dict:
    key = jax.random.key(seed)
    ks = iter(jax.random.split(key, 40))
    f32 = jnp.float32

    def w(shape, fan_in):
        return jax.random.normal(next(ks), shape, f32) * fan_in ** -0.5

    def gain(shape):
        return 1.0 + 0.02 * jax.random.normal(next(ks), shape, f32)

    def small(shape, s):
        return s * jax.random.normal(next(ks), shape, f32)

    x = jax.random.normal(next(ks), (BATCH, SEQ, D_MODEL), f32)
    offsets = jax.random.randint(next(ks), (BATCH, 1), 0, 1024)
    positions = (offsets + jnp.arange(SEQ)[None, :]).astype(jnp.int32)
    return {
        'x': x,
        'positions': positions,
        'ffn_norm': gain((DEPTH_2, 2, D_MODEL)),
        'ffn_w_gate': w((DEPTH_2, 2, D_MODEL, D_FF_2), D_MODEL),
        'ffn_w_up': w((DEPTH_2, 2, D_MODEL, D_FF_2), D_MODEL),
        'ffn_w_down': w((DEPTH_2, 2, D_FF_2, D_MODEL), D_FF_2),
        'mix_norm': gain((DEPTH_2, D_MODEL)),
        'hy_w_in': w((N_EVEN, D_MODEL, HY_IN), D_MODEL),
        'mla_q_norm': gain((N_EVEN, MLA_Q_LORA)),
        'mla_w_uq': w((N_EVEN, MLA_Q_LORA, MLA_HEADS * (MLA_NOPE + MLA_ROPE)), MLA_Q_LORA),
        'mla_kv_norm': gain((N_EVEN, MLA_KV_LORA)),
        'mla_w_ukv': w((N_EVEN, MLA_KV_LORA, MLA_HEADS * (MLA_NOPE + MLA_V)), MLA_KV_LORA),
        'gla_w_a2': w((N_EVEN, GLA_GATE_RANK, GLA_HEADS * GLA_DK), GLA_GATE_RANK),
        'gla_b_a': small((N_EVEN, GLA_HEADS * GLA_DK), 0.1),
        'gla_out_norm': gain((N_EVEN, GLA_DV)),
        'hy_w_out': w((N_EVEN, HY_OUT, D_MODEL), HY_OUT),
        'nsa_w_in': w((N_ODD, D_MODEL, NSA_IN), D_MODEL),
        'nsa_pos_k': small((N_ODD, NSA_CMP_LEN, NSA_HEAD_DIM), 0.1),
        'nsa_pos_v': small((N_ODD, NSA_CMP_LEN, NSA_HEAD_DIM), 0.1),
        'nsa_ck_w1': w((N_ODD, NSA_CMP_LEN * NSA_HEAD_DIM, NSA_CMP_HIDDEN), NSA_CMP_LEN * NSA_HEAD_DIM),
        'nsa_ck_w2': w((N_ODD, NSA_CMP_HIDDEN, NSA_HEAD_DIM), NSA_CMP_HIDDEN),
        'nsa_cv_w1': w((N_ODD, NSA_CMP_LEN * NSA_HEAD_DIM, NSA_CMP_HIDDEN), NSA_CMP_LEN * NSA_HEAD_DIM),
        'nsa_cv_w2': w((N_ODD, NSA_CMP_HIDDEN, NSA_HEAD_DIM), NSA_CMP_HIDDEN),
        'nsa_w_out': w((N_ODD, NSA_OUT, D_MODEL), NSA_OUT),
        'final_norm': gain((D_MODEL,)),
    }

def second_block(x, positions, ffn_norm, ffn_w_gate, ffn_w_up, ffn_w_down, mix_norm,
              hy_w_in, mla_q_norm, mla_w_uq, mla_kv_norm, mla_w_ukv, gla_w_a2, gla_b_a,
              gla_out_norm, hy_w_out, nsa_w_in, nsa_pos_k, nsa_pos_v, nsa_ck_w1, nsa_ck_w2,
              nsa_cv_w1, nsa_cv_w2, nsa_w_out, final_norm):
    h = x
    for layer in range(DEPTH_2):
        j = layer // 2
        h = h + 0.5 * swiglu(rms_norm_2(h, ffn_norm[layer, 0]), ffn_w_gate[layer, 0], ffn_w_up[layer, 0], ffn_w_down[layer, 0])
        u = rms_norm_2(h, mix_norm[layer])
        if layer % 2 == 0:
            mixed = mla_gla_mixer(u, positions, hy_w_in[j], mla_q_norm[j], mla_w_uq[j], mla_kv_norm[j],
                                  mla_w_ukv[j], gla_w_a2[j], gla_b_a[j], gla_out_norm[j], hy_w_out[j])
        else:
            mixed = nsa_mixer(u, positions, nsa_w_in[j], nsa_pos_k[j], nsa_pos_v[j], nsa_ck_w1[j],
                              nsa_ck_w2[j], nsa_cv_w1[j], nsa_cv_w2[j], nsa_w_out[j])
        h = h + mixed.astype(h.dtype)
        h = h + 0.5 * swiglu(rms_norm_2(h, ffn_norm[layer, 1]), ffn_w_gate[layer, 1], ffn_w_up[layer, 1], ffn_w_down[layer, 1])
    return rms_norm_2(h, final_norm)


def setup_inputs(seed=0):
    out = dict(first_inputs(seed))
    for name, value in second_inputs(seed + 1).items():
        if name != "x":
            out[name + "_2"] = value
    return out


def reference(
    x, c, positions, ada_w, ada_b, mix_pre_g, mix_post_g, ffn_pre_g, ffn_post_g, w_in,
    ssm_lam_re, ssm_lam_im, ssm_log_dt, ssm_b_re, ssm_b_im, ssm_c_re, ssm_c_im, ssm_d,
    ssm_w_glu, w_ssm_branch, w_attn_branch, w_out, router_w, router_b, w_gate, b_gate, w_up,
    b_up, w_down, b_down, positions_2, ffn_norm_2, ffn_w_gate_2, ffn_w_up_2, ffn_w_down_2,
    mix_norm_2, hy_w_in_2, mla_q_norm_2, mla_w_uq_2, mla_kv_norm_2, mla_w_ukv_2, gla_w_a2_2,
    gla_b_a_2, gla_out_norm_2, hy_w_out_2, nsa_w_in_2, nsa_pos_k_2, nsa_pos_v_2, nsa_ck_w1_2,
    nsa_ck_w2_2, nsa_cv_w1_2, nsa_cv_w2_2, nsa_w_out_2, final_norm_2,
):
    x = first_block(
        x, c, positions, ada_w, ada_b, mix_pre_g, mix_post_g, ffn_pre_g, ffn_post_g, w_in,
        ssm_lam_re, ssm_lam_im, ssm_log_dt, ssm_b_re, ssm_b_im, ssm_c_re, ssm_c_im, ssm_d,
        ssm_w_glu, w_ssm_branch, w_attn_branch, w_out, router_w, router_b, w_gate, b_gate, w_up,
        b_up, w_down, b_down,
    )
    return second_block(
        x, positions_2, ffn_norm_2, ffn_w_gate_2, ffn_w_up_2, ffn_w_down_2, mix_norm_2,
        hy_w_in_2, mla_q_norm_2, mla_w_uq_2, mla_kv_norm_2, mla_w_ukv_2, gla_w_a2_2, gla_b_a_2,
        gla_out_norm_2, hy_w_out_2, nsa_w_in_2, nsa_pos_k_2, nsa_pos_v_2, nsa_ck_w1_2,
        nsa_ck_w2_2, nsa_cv_w1_2, nsa_cv_w2_2, nsa_w_out_2, final_norm_2,
    )


_drawn_inputs = setup_inputs


def setup_inputs(seed=0):
    import zlib

    import numpy as np

    out = dict(_drawn_inputs(seed))
    spreads = {}
    factors = {'ffn_post_g': 3.179,
     'ssm_lam_re': 200.0,
     'b_gate': 8.0,
     'b_up': 8.0,
     'b_down': 8.0,
     'ffn_norm_2': 3.745,
     'mix_norm_2': 3.271,
     'mla_q_norm_2': 8.0,
     'mla_kv_norm_2': 8.0,
     'gla_b_a_2': 3.35,
     'gla_out_norm_2': 7.688,
     'nsa_pos_k_2': 21.42,
     'final_norm_2': 22.846,
     'nsa_pos_v_2': 23.142,
     'ssm_c_re': 4.657}
    for name, (base, spread) in spreads.items():
        noise = np.random.default_rng([zlib.crc32(name.encode()), seed]).standard_normal(out[name].shape)
        drawn = base * np.exp(spread * noise) if base else spread * noise
        out[name] = jnp.asarray(drawn.astype(out[name].dtype))
    for name, factor in factors.items():
        out[name] = (out[name] * factor).astype(out[name].dtype)
    return out
```

```python
from contextlib import ExitStack

import numpy as np

import concourse.bass as bass
from concourse import mybir

F32 = mybir.dt.float32
I32 = mybir.dt.int32
ALU = mybir.AluOpType
ACT = mybir.ActivationFunctionType
AX_X = mybir.AxisListType.X

P = 128
S = 256
TT = S // P
D = 1024
KT = D // P
EPS = 1e-6
NEG = -1e30
TINY = 1e-30

E = 32
TOP_K = 4
DFF = 1024
DFF2 = 2816
STEP_COLS = 256
STEP_TILES = STEP_COLS // P
STEP_GATE = KT * STEP_COLS
STEP_WIDTH = 2 * STEP_GATE + STEP_TILES * D
MOE_STEPS = DFF // STEP_COLS
FFN_STEPS = DFF2 // STEP_COLS
ALPHA = 1.702
LIMIT = 7.0

SSM_G, SSM_C, SSM_N = 32, 16, 64
SSM_W = SSM_G * SSM_C
SSM_TILES = SSM_G * SSM_N // P
SSM_Q = 4

HEADS, HD = 8, 64
MLA_H, MLA_NOPE, MLA_ROPE, MLA_V = 8, 64, 32, 64
MLA_QK = MLA_NOPE + MLA_ROPE
Q_LORA, KV_LORA = 256, 128
GLA_H, GLA_DK, GLA_DV, GLA_RANK, GLA_TAU, CHUNK = 4, 64, 128, 16, 16.0, 64
NCH = S // CHUNK
NSA_H, NSA_G = 16, 4
CMP_LEN, CMP_STRIDE, CMP_HID = 32, 16, 128
N_CMP = (S - CMP_LEN) // CMP_STRIDE + 1

SLOT = STEP_WIDTH
ROUND = 12582912.0
ROUND_12 = 3072.0
TWO_PI = 2 * np.pi
PI_HI = 6.28125
PI_MID = float(np.float32(np.round((TWO_PI - PI_HI) * 2 ** 21) / 2 ** 21))
PI_LO = float(np.float32(TWO_PI - PI_HI - PI_MID))
SIN_MAX = 3.1415925
TURN = 6.283185

PARAMS = [("c", KT), ("lam_re", SSM_TILES), ("lam_im", SSM_TILES), ("log_dt", SSM_TILES), ("d_skip", SSM_W // P),
          ("router_b", E), ("ffn_g", 4 * KT), ("mix_g", 2 * KT), ("q_norm", Q_LORA // P), ("kv_norm", 1),
          ("b_a", 2), ("out_norm", GLA_DV), ("w_a2", GLA_H * GLA_DK), ("pos_kv", CMP_LEN),
          ("ct_re", SSM_TILES * 32), ("ct_im", SSM_TILES * 32), ("router_w", KT * E), ("b_gu", E * 16)]
CONSTS = [("ident", P), ("causal", 3 * P), ("inv_freq_64", 32), ("inv_freq_32", 16), ("time", S),
          ("gla_mask", P), ("gla_keep", S), ("cmp_add", TT * N_CMP), ("cmp_one", TT * N_CMP)]
ANGLES = [("a0", 0, "inv_freq_64", 32), ("a1", 1, "inv_freq_64", 32), ("b0", 2, "inv_freq_64", 32),
          ("b1", 3, "inv_freq_64", 32), ("m0", 2, "inv_freq_32", 16), ("m1", 3, "inv_freq_32", 16),
          ("e", 4, "inv_freq_64", 32)]


def offsets(table):
    at, out = 0, {}
    for name, width in table:
        out[name] = (at, at + width)
        at += width
    return out, at


PARAM_AT, PARAM_W = offsets(PARAMS)
CONST_AT, CONST_W = offsets(CONSTS)
ANGLE_AT, ANGLE_W = offsets([(n, w) for n, _, _, w in ANGLES])

ADA_COLS = 768
ADA_UNITS = 16
ADA_N = ADA_COLS // 2
HYA = Q_LORA + KV_LORA + MLA_ROPE + GLA_RANK

SIGNALS = """small_loaded rows_loaded step_dve step_act step_pool phase_end
 cond_sig cond_ready ada_ready ada_act ada_dve
 sumsq meansq root xn_ready xT_ready hT_act hT_dve x_ready
 proj_ready proj_act proj_dve rope_dve rope_pool
 ssm_prep_act ssm_prep_dve trig_arg trig_done table_free bu_ready bu_read rotated ssm_y_ready ssm_y_read gelu_in gelu_done glu_ready glu_sig ys_ready
 heads_T heads_T_act heads_T_dve score_ready masked negmax exp_done p_norm pT_ready pT_copied o_ready o_copied
 merge_ready merge_sig merged
 mix_square moe_square post_mean post_root
 router_ready router_exp router_in weights_ready weights_T weights_T_done y_init tie_loaded
 gu_ready gu_drained gate_ready sig_ready swi_step act_ready down_done y_drained
 angles_ready lora_ready lora_act lora_dve lora_sq lora_mean lora_root lora_n mla_dve mla_pool
 gla_pre gla_abs gla_soft gla_arg gla_exp gla_ready gla_kdec gla_kdec_read gla_kv gla_state gla_A gla_A_read gla_o gla_sq gla_mean gla_root gla_silu gla_out
 nsa_dve nsa_pool gate_in gate_sig cmp_blk cmp_h cmp_sig cmp_hid cmp_kv cmp_k cmp_kT cmp_kT_read cmp_score cmp_arg cmp_exp cmp_p
 out_ready out_read final_loaded stored arena_free""".split()


class Steps:

    def __init__(self, engine, sem):
        self.engine, self.sem, self.n = engine, sem, 0

    def mark(self, instruction):
        instruction.then_inc(self.sem, 1)
        self.n += 1
        return instruction

    def wait(self):
        self.engine.wait_ge(self.sem, self.n)


class Item:

    def __init__(self, src, width, slot, free, landed):
        self.src, self.width, self.slot, self.free, self.landed = src, width, slot, free, landed


class Unit:

    def __init__(self, kind, first, last, at, dv, gate=None, q=None, k=None, v=None, p=None, out=None):
        self.kind, self.first, self.last, self.at, self.dv, self.gate = kind, first, last, at, dv, gate
        self.q, self.k, self.v, self.p, self.out = q, k, v, p, out
        self.all = self.full = self.head = None


def plan_ring(sig):
    freed = [None] * 4
    landed = [0] * 4
    plan, order = {}, []
    turn = 0

    def item(name, src, width, done):
        nonlocal turn
        slot = turn % 3
        turn += 1
        landed[slot] += 16
        plan[name] = Item(src, width, slot, freed[slot], landed[slot])
        order.append(plan[name])
        freed[slot] = done

    for j in range(8):
        item(f"ada{j}", ("ada", j), SLOT, (sig["ada_ready"], 2 * j + 2))
    item("w_u", ("w_in", 0), 4096, (sig["proj_ready"], 2))
    for j in range(3):
        item(f"w_qkv{j}", ("w_in", 1 + j), 4096, (sig["proj_ready"], 4 + 2 * j))
    item("ssm_b", ("ssm_b", 0), 4096, (sig["bu_ready"], SSM_TILES))
    item("w_glu", ("w_glu", 0), 2048, (sig["glu_ready"], 2))
    for j in range(4):
        item(f"merge{j}", ("merge", j), SLOT, (sig["merge_ready"], 2 * j + 2))
    for j in range(2):
        item(f"w_out{j}", ("w_out", j), 4096, (sig["out_ready"], 2 * j + 2))
    before = list(order)
    moe = Item("moe", SLOT, None, [freed[0], freed[1], freed[2], (sig["arena_free"], 1)], [x + 16 for x in landed])
    for s in range(4):
        landed[s] += 16 * E
        freed[s] = (sig["down_done"], 2 + 4 * (E - 1) + s + 1)
    order.clear()
    turn = 0

    def ffn(q):
        base = 2 + E * MOE_STEPS + FFN_STEPS * q
        for m in range(FFN_STEPS):
            item(f"ffn{q}_{m}", ("ffn", q * FFN_STEPS + m), SLOT, (sig["down_done"], base + m + 1))

    ffn(0)
    for j in range(4):
        item(f"hy{j}", ("hy_in", j), HYA * KT if j == 0 else 4096, (sig["proj_ready"], 8 + 2 * j + 2))
    item("lora", ("lora", 0), 2 * 768 + 1024, (sig["lora_ready"], 8))
    for j in range(2):
        item(f"hy_out{j}", ("hy_out", j), 4096, (sig["out_ready"], 4 + 2 * j + 2))
    ffn(1)
    ffn(2)
    for j in range(5):
        item(f"nsa{j}", ("nsa_in", j), 4096, (sig["proj_ready"], 16 + 2 * j + 2))
    item("nsa_c", ("nsa_c", 0), 4096 + 384 + 128, (sig["cmp_kv"], 2))
    for j in range(2):
        item(f"nsa_out{j}", ("nsa_out", j), 4096, (sig["out_ready"], 8 + 2 * j + 2))
    ffn(3)
    return plan, before, moe, order


def par(k, name, a=None, b=None):
    lo, hi = PARAM_AT[name]
    return k["params"][:, lo + (a or 0):(lo + b if b is not None else hi)]


def con(k, name, a=None, b=None):
    lo, hi = CONST_AT[name]
    return k["consts"][:, lo + (a or 0):(lo + b if b is not None else hi)]


def spread(ap, n):
    return ap.unsqueeze(1).to_broadcast([ap.shape[0], n, ap.shape[1]])


def spread_last(ap, n):
    return ap.unsqueeze(2).to_broadcast([ap.shape[0], ap.shape[1], n])


def end_phase(k, eng, n):
    eng.drain().then_inc(k["sig"]["phase_end"], 1)
    eng.wait_ge(k["sig"]["phase_end"], 4 * n)




def ada_scalar(k, act):
    s = k["sig"]
    act.wait_ge(s["small_loaded"], 64)
    act.activation(k["cond"][:, 0:KT], par(k, "c"), ACT.Sigmoid).then_inc(s["cond_sig"], 1)
    for u in range(0, ADA_UNITS, 2):
        act.wait_ge(s["ada_ready"], u + 1)
        act.activation(k["rows"][:, u * ADA_N:(u + 1) * ADA_N], k["ps"][u % 4][:, 0:ADA_N], ACT.Copy).then_inc(s["ada_act"], 1)


def ada_vector(k, dve):
    s = k["sig"]
    dve.wait_ge(s["small_loaded"], 64)
    dve.wait_ge(s["cond_sig"], 1)
    k["vs"].mark(dve.tensor_tensor(k["cond"][:, KT:2 * KT], k["cond"][:, 0:KT], par(k, "c"), ALU.mult))
    k["vs"].mark(dve.memset(k["one_row"][:, :], 1.0))
    k["vs"].mark(dve.memset(k["quarter"][:, :], float(np.float32(TURN * 0.25))))
    k["vs"].wait()
    dve.tensor_copy(k["cond_wide"][:, :, :], spread_last(k["cond"][:, KT:2 * KT], P)).then_inc(s["cond_ready"], 1)
    dve.drain().then_inc(s["gu_drained"], 2)
    dve.drain().then_inc(s["act_ready"], 1)
    for u in range(1, ADA_UNITS, 2):
        dve.wait_ge(s["ada_ready"], u + 1)
        dve.tensor_copy(k["rows"][:, u * ADA_N:(u + 1) * ADA_N], k["ps"][u % 4][:, 0:ADA_N]).then_inc(s["ada_dve"], 1)
    dve.wait_ge(s["ada_dve"], 8)
    dve.wait_ge(s["ada_act"], 8)
    dve.wait_ge(s["rows_loaded"], 32)
    for row, gain, plus in ((1, 0, True), (4, 2, True), (2, 1, False), (5, 3, False)):
        r = k["rows"][:, row * D:(row + 1) * D]
        g = k["gains"][:, gain, :]
        if plus:
            k["vs"].mark(dve.scalar_tensor_tensor(out=r, in0=r, scalar=1.0, in1=g, op0=ALU.add, op1=ALU.mult))
        else:
            k["vs"].mark(dve.tensor_tensor(r, r, g, ALU.mult))
    k["vs"].wait()
    dve.drain().then_inc(s["x_ready"], 1)


def ada_tensor(k, pe):
    s = k["sig"]
    pe.wait_ge(s["cond_ready"], 1)
    pe.wait_ge(s["rows_loaded"], 32)
    for u in range(ADA_UNITS):
        j, half = divmod(u, 2)
        it = k["plan"][f"ada{j}"]
        if half == 0:
            pe.wait_ge(k["landed"][it.slot], it.landed)
        if u >= 4:
            pe.wait_ge(s["ada_act"] if u % 2 == 0 else s["ada_dve"], (u - 4) // 2 + 1)
        bank = k["ps"][u % 4][:, 0:ADA_N]
        pe.matmul(bank, k["one_row"][0:1, :], k["ada_b"][0:1, u * ADA_N:(u + 1) * ADA_N], start=True, stop=False)
        for kt in range(KT):
            at = kt * ADA_COLS + half * ADA_N
            mm = pe.matmul(bank, k["cond_wide"][:, kt, :], k["ring"][it.slot][:, at:at + ADA_N], start=False, stop=kt == KT - 1)
        mm.then_inc(s["ada_ready"], 1)




def angles_vector(k, dve):
    s = k["sig"]
    vs = k["vs"]
    vs.mark(dve.tensor_copy(k["posf"][:, :], k["posi"][:, :]))
    vs.wait()
    ang, turns, tmp = k["rope"][:, 0, :], k["rope"][:, 1, :], k["rope"][:, 2, :]
    for name, col, freq, w in ANGLES:
        lo, hi = ANGLE_AT[name]
        vs.mark(dve.tensor_scalar(ang[:, lo:hi], con(k, freq), k["posf"][:, col:col + 1], None, ALU.mult))
    vs.wait()
    reduce_angle(dve, vs, ang, turns)
    fold_quarter(dve, vs, ang, tmp, turns)
    dve.drain().then_inc(s["angles_ready"], 1)


def reduce_angle(dve, vs, ang, turns):
    vs.mark(dve.tensor_scalar(turns, ang, 1.0 / TWO_PI, ROUND, ALU.mult, ALU.add))
    vs.wait()
    vs.mark(dve.tensor_scalar(turns, turns, ROUND, None, ALU.subtract))
    vs.wait()
    for part in (PI_HI, PI_MID, PI_LO):
        vs.mark(dve.scalar_tensor_tensor(out=ang, in0=turns, scalar=-part, in1=ang, op0=ALU.mult, op1=ALU.add))
        vs.wait()


def fold_quarter(dve, vs, ang, out, tmp):
    vs.mark(dve.tensor_scalar(out, ang, float(np.pi / 2), None, ALU.add))
    vs.wait()
    vs.mark(dve.tensor_scalar(tmp, out, float(np.pi), -TWO_PI, ALU.is_gt, ALU.mult))
    vs.wait()
    vs.mark(dve.tensor_tensor(out, out, tmp, ALU.add))
    vs.wait()
    vs.mark(dve.tensor_scalar(out, out, SIN_MAX, -SIN_MAX, ALU.min, ALU.max))
    vs.mark(dve.tensor_scalar(ang, ang, SIN_MAX, -SIN_MAX, ALU.min, ALU.max))
    vs.wait()


def angles_scalar(k, act):
    act.wait_ge(k["sig"]["angles_ready"], 1)
    k["acs"].mark(act.activation(k["sin"][:, :], k["rope"][:, 0, :], ACT.Sin))
    k["acs"].mark(act.activation(k["cos"][:, :], k["rope"][:, 2, :], ACT.Sin))




def norm_scalar(k, act, i, gain):
    s = k["sig"]
    act.wait_ge(s["x_ready"], i + 1)
    for t in range(TT):
        act.activation(k["xn"][:, t, :], k["x"][:, t, :], ACT.Square, accum_out=k["ss"][:, t:t + 1]).then_inc(s["sumsq"], 1)
    act.wait_ge(s["meansq"], i + 1)
    act.activation(k["ss"][:, 2:4], k["ss"][:, 2:4], ACT.Sqrt).then_inc(s["root"], 1)
    for b in range(2):
        act.wait_ge(s["xT_ready"], 4 * i + b + 1)
        for kk in range(2):
            kt = 2 * b + kk
            src = k["ps"][b][:, kk * S:(kk + 1) * S]
            if gain is None:
                ins = act.activation(k["hT"][:, kt, :], src, ACT.Copy)
            else:
                ins = act.activation(k["hT"][:, kt, :], src, ACT.Copy, scale=gain[:, kt:kt + 1])
        ins.then_inc(s["hT_act"], 1)


def norm_vector(k, dve, i, gain, rows=None):
    s = k["sig"]
    vs = k["vs"]
    dve.wait_ge(s["sumsq"], 2 * i + 2)
    dve.tensor_scalar(k["ss"][:, 2:4], k["ss"][:, 0:2], 1.0 / D, EPS, ALU.mult, ALU.add).then_inc(s["meansq"], 1)
    dve.wait_ge(s["root"], i + 1)
    vs.mark(dve.reciprocal(k["ss"][:, 4:6], k["ss"][:, 2:4]))
    vs.wait()
    for t in range(TT):
        r = k["ss"][:, 4 + t:5 + t]
        if rows is None:
            dve.tensor_scalar(k["xn"][:, t, :], k["x"][:, t, :], r, None, ALU.mult).then_inc(s["xn_ready"], 1)
        else:
            g, sh = rows
            vs.mark(dve.scalar_tensor_tensor(out=k["xn"][:, t, :], in0=k["x"][:, t, :], scalar=r, in1=g, op0=ALU.mult, op1=ALU.mult))
            vs.wait()
            dve.tensor_tensor(k["xn"][:, t, :], k["xn"][:, t, :], sh, ALU.add).then_inc(s["xn_ready"], 1)
    for b in range(2, 4):
        dve.wait_ge(s["xT_ready"], 4 * i + b + 1)
        if gain is None:
            ins = dve.tensor_copy(k["hT"][:, 2 * b:2 * b + 2, :].rearrange("p a b -> p (a b)"), k["ps"][b][:, :])
        else:
            for kk in range(2):
                kt = 2 * b + kk
                ins = dve.tensor_scalar(k["hT"][:, kt, :], k["ps"][b][:, kk * S:(kk + 1) * S], gain[:, kt:kt + 1], None, ALU.mult)
        ins.then_inc(s["hT_dve"], 1)


def norm_tensor(k, pe, i):
    s = k["sig"]
    pe.wait_ge(s["xn_ready"], 2 * i + 2)
    for b in range(4):
        for kk in range(2):
            for t in range(TT):
                kt = 2 * b + kk
                mm = pe.transpose(k["ps"][b][:, (kk * 2 + t) * P:(kk * 2 + t + 1) * P], k["xn"][:, t, kt * P:(kt + 1) * P], con(k, "ident"))
        mm.then_inc(s["xT_ready"], 1)
    pe.wait_ge(s["hT_act"], 2 * i + 2)
    pe.wait_ge(s["hT_dve"], 2 * i + 2)




def project_tensor(k, pe, names, base, ncols, src, kts, start):
    s = k["sig"]
    for j, name in enumerate(names):
        it = k["plan"][name]
        n = ncols[j]
        pe.wait_ge(k["landed"][it.slot], it.landed)
        for t in range(TT):
            u = base + 2 * j + t
            if u - 4 >= start:
                pe.wait_ge(s["proj_act"] if t == 0 else s["proj_dve"], (u - 4) // 2 + 1)
            bank = k["ps"][u % 4][:, 0:n]
            for kt in range(kts):
                mm = pe.matmul(bank, src[:, kt, t * P:(t + 1) * P], k["ring"][it.slot][:, kt * n:(kt + 1) * n], start=kt == 0, stop=kt == kts - 1)
            mm.then_inc(s["proj_ready"], 1)


def project_read(k, eng, t, base, dsts):
    s = k["sig"]
    for j, dst in enumerate(dsts):
        u = base + 2 * j + t
        eng.wait_ge(s["proj_ready"], u + 1)
        d = dst[:, t, :]
        bank = k["ps"][u % 4][:, 0:d.shape[1]]
        if t == 0:
            eng.activation(d, bank, ACT.Copy).then_inc(s["proj_act"], 1)
        else:
            eng.tensor_copy(d, bank).then_inc(s["proj_dve"], 1)


def u_tensor(k, pe):
    s = k["sig"]
    it = k["plan"]["w_u"]
    pe.wait_ge(k["landed"][it.slot], it.landed)
    for b in range(2):
        for ff in range(2):
            f = 2 * b + ff
            for kt in range(KT):
                at = kt * SSM_W + f * P
                mm = pe.matmul(k["ps"][b][:, ff * S:(ff + 1) * S], k["ring"][it.slot][:, at:at + P], k["hT"][:, kt, :], start=kt == 0, stop=kt == KT - 1)
        mm.then_inc(s["proj_ready"], 1)


def rope_rotate(eng, steps, dst, src, nh, half, cos, sin, tmp):
    p = cos.shape[0]
    a, b, c, d = (tmp[0:p, i, 0:nh * half].rearrange("p (h x) -> p h x", h=nh) for i in range(4))
    cb, sb = spread(cos, nh), spread(sin, nh)
    lo, hi = src[:, :, 0:half], src[:, :, half:2 * half]
    steps.mark(eng.tensor_tensor(a, lo, cb, ALU.mult))
    steps.mark(eng.tensor_tensor(b, hi, sb, ALU.mult))
    steps.mark(eng.tensor_tensor(c, hi, cb, ALU.mult))
    steps.mark(eng.tensor_tensor(d, lo, sb, ALU.mult))
    steps.wait()
    steps.mark(eng.tensor_tensor(dst[:, :, 0:half], a, b, ALU.subtract))
    steps.mark(eng.tensor_tensor(dst[:, :, half:2 * half], c, d, ALU.add))
    steps.wait()


def angle(k, table, name, p=P):
    lo, hi = ANGLE_AT[name]
    return table[0:p, lo:hi]




def ssm_prep_vector(k, dve):
    s, vs, w = k["sig"], k["vs"], k["ssm_small"]
    n = SSM_TILES

    def c(i):
        return w[:, i * n:(i + 1) * n]

    dt, re, theta, r, sn, cs, thi, tlo, t0, t1, t2, t3, sarg, carg = (c(i) for i in range(14))
    dve.wait_ge(s["ssm_prep_act"], 1)
    vs.mark(dve.tensor_tensor(re, par(k, "lam_re"), dt, ALU.mult))
    vs.mark(dve.tensor_tensor(theta, par(k, "lam_im"), dt, ALU.mult))
    vs.wait()
    reduce_angle(dve, vs, theta, t0)
    vs.mark(dve.tensor_scalar(t1, theta, 1.0 / TWO_PI, None, ALU.mult))
    vs.wait()
    vs.mark(dve.tensor_scalar(thi, t1, ROUND_12, None, ALU.add))
    vs.wait()
    vs.mark(dve.tensor_scalar(thi, thi, ROUND_12, None, ALU.subtract))
    vs.wait()
    vs.mark(dve.tensor_tensor(tlo, t1, thi, ALU.subtract))
    vs.mark(dve.tensor_copy(sarg, theta))
    vs.wait()
    fold_quarter(dve, vs, sarg, carg, t0)
    dve.drain().then_inc(s["ssm_prep_dve"], 1)
    dve.wait_ge(s["ssm_prep_act"], 4)
    lr, li = par(k, "lam_re"), par(k, "lam_im")
    vs.mark(dve.tensor_tensor(t0, r, cs, ALU.mult))
    vs.mark(dve.tensor_tensor(t1, r, sn, ALU.mult))
    vs.mark(dve.tensor_tensor(t2, lr, lr, ALU.mult))
    vs.mark(dve.tensor_tensor(t3, li, li, ALU.mult))
    vs.wait()
    vs.mark(dve.tensor_scalar(t0, t0, 1.0, None, ALU.subtract))
    vs.mark(dve.tensor_tensor(t2, t2, t3, ALU.add))
    vs.wait()
    vs.mark(dve.reciprocal(t3, t2))
    vs.mark(dve.tensor_tensor(sarg, t0, lr, ALU.mult))
    vs.mark(dve.tensor_tensor(carg, t1, li, ALU.mult))
    vs.wait()
    vs.mark(dve.tensor_tensor(sarg, sarg, carg, ALU.add))
    vs.mark(dve.tensor_tensor(t1, t1, lr, ALU.mult))
    vs.mark(dve.tensor_tensor(t0, t0, li, ALU.mult))
    vs.wait()
    vs.mark(dve.tensor_tensor(t1, t1, t0, ALU.subtract))
    vs.wait()
    vs.mark(dve.tensor_tensor(sarg, sarg, t3, ALU.mult))
    vs.mark(dve.tensor_tensor(t1, t1, t3, ALU.mult))
    vs.wait()
    cr, ci = spread_last(sarg, 32), spread_last(t1, 32)
    re3 = par(k, "ct_re").rearrange("p (j c) -> p j c", j=n)
    im3 = par(k, "ct_im").rearrange("p (j c) -> p j c", j=n)
    plus, minus, neg_im, tmp = (k["c_mix"][:, i, :].rearrange("p (j c) -> p j c", j=n) for i in range(4))
    vs.mark(dve.tensor_tensor(plus, re3, cr, ALU.mult))
    vs.mark(dve.tensor_tensor(tmp, im3, ci, ALU.mult))
    vs.mark(dve.tensor_tensor(neg_im, re3, ci, ALU.mult))
    vs.mark(dve.tensor_tensor(minus, im3, cr, ALU.mult))
    vs.wait()
    vs.mark(dve.tensor_tensor(plus, plus, tmp, ALU.subtract))
    vs.mark(dve.tensor_tensor(neg_im, neg_im, minus, ALU.add))
    vs.wait()
    vs.mark(dve.tensor_scalar(minus, plus, -1.0, None, ALU.mult))
    vs.mark(dve.tensor_scalar(neg_im, neg_im, -1.0, None, ALU.mult))
    vs.wait()


def ssm_prep_scalar(k, act):
    s = k["sig"]
    n = SSM_TILES
    act.wait_ge(s["small_loaded"], 64)
    act.activation(k["ssm_small"][:, 0:n], par(k, "log_dt"), ACT.Exp).then_inc(s["ssm_prep_act"], 1)
    act.wait_ge(s["ssm_prep_dve"], 1)
    act.activation(k["ssm_small"][:, 3 * n:4 * n], k["ssm_small"][:, n:2 * n], ACT.Exp).then_inc(s["ssm_prep_act"], 1)
    act.activation(k["ssm_small"][:, 4 * n:5 * n], k["ssm_small"][:, 12 * n:13 * n], ACT.Sin).then_inc(s["ssm_prep_act"], 1)
    act.activation(k["ssm_small"][:, 5 * n:6 * n], k["ssm_small"][:, 13 * n:14 * n], ACT.Sin).then_inc(s["ssm_prep_act"], 1)


def ssm_tables_pool(k, pool):
    s, po = k["sig"], k["pos"]
    n = SSM_TILES
    pool.wait_ge(s["ssm_prep_dve"], 1)
    time = spread(con(k, "time"), SSM_Q)
    for q in range(4):
        if q >= 1:
            pool.wait_ge(s["trig_done"], 2 * q)
        a, b = k["trig"][:, 0, :, :], k["trig"][:, 1, :, :]
        hi = spread_last(k["ssm_small"][:, 6 * n + q * SSM_Q:6 * n + (q + 1) * SSM_Q], S)
        lo = spread_last(k["ssm_small"][:, 7 * n + q * SSM_Q:7 * n + (q + 1) * SSM_Q], S)
        po.mark(pool.tensor_tensor(a, time, hi, ALU.mult))
        po.wait()
        po.mark(pool.tensor_scalar(b, a, ROUND, ROUND, ALU.add, ALU.subtract))
        po.wait()
        po.mark(pool.tensor_tensor(a, a, b, ALU.subtract))
        po.wait()
        po.mark(pool.tensor_tensor(b, time, lo, ALU.mult))
        po.wait()
        po.mark(pool.tensor_tensor(a, a, b, ALU.add))
        po.wait()
        po.mark(pool.tensor_scalar(b, a, ROUND, ROUND, ALU.add, ALU.subtract))
        po.wait()
        po.mark(pool.tensor_tensor(a, a, b, ALU.subtract))
        po.wait()
        po.mark(pool.tensor_scalar(b, a, 0.25, ROUND, ALU.add, ALU.add))
        po.wait()
        po.mark(pool.tensor_scalar(b, b, ROUND, None, ALU.subtract))
        po.wait()
        pool.tensor_tensor(b, a, b, ALU.subtract).then_inc(s["trig_arg"], 1)
        pool.wait_ge(s["trig_arg"], q + 1)


def ssm_trig_scalar(k, act, q):
    s = k["sig"]
    act.wait_ge(s["trig_arg"], q + 1)
    if q >= 2:
        act.wait_ge(s["table_free"], q - 1)
    act.activation(k["table"][:, q % 2, 1, :, :], k["trig"][:, 0, :, :], ACT.Sin, scale=TURN).then_inc(s["trig_done"], 1)
    act.activation(k["table"][:, q % 2, 0, :, :], k["trig"][:, 1, :, :], ACT.Sin, scale=TURN, bias=k["quarter"][:, 0:1]).then_inc(s["trig_done"], 1)


def ssm_vector(k, dve):
    s, vs = k["sig"], k["vs"]
    n = SSM_TILES
    A, B = k["ssm_a"], k["ssm_b"]
    for j in range(SSM_TILES):
        q, jj = divmod(j, SSM_Q)
        if jj == 0:
            dve.wait_ge(s["trig_done"], 2 * q + 2)
        cosb = spread(k["table"][:, q % 2, 0, jj, :], 2)
        sinb = spread(k["table"][:, q % 2, 1, jj, :], 2)
        bu = k["ps"][4 + j % 2][:, :].rearrange("p (a b) -> p a b", a=2)
        dve.wait_ge(s["bu_ready"], j + 1)
        vs.mark(dve.tensor_tensor(A[:, :, :], bu, cosb, ALU.mult))
        dve.tensor_tensor(B[:, :, :], bu, sinb, ALU.mult).then_inc(s["bu_read"], 1)
        vs.wait()
        dve.wait_ge(s["bu_read"], j + 1)
        vs.mark(dve.tensor_tensor(A[:, 0, :], A[:, 0, :], B[:, 1, :], ALU.add))
        vs.mark(dve.tensor_tensor(A[:, 1, :], A[:, 1, :], B[:, 0, :], ALU.subtract))
        vs.wait()
        decay = k["ssm_small"][:, 3 * n + j:3 * n + j + 1].to_broadcast([P, S])
        for c in range(2):
            vs.mark(dve.tensor_tensor_scan(B[:, c, :], decay, A[:, c, :], 0.0, ALU.mult, ALU.add))
        vs.wait()
        if j >= 2:
            dve.wait_ge(s["ssm_y_ready"], j - 1)
        R = k["ssm_r"][:, j % 2, :, :, :]
        vs.mark(dve.tensor_tensor(R[:, 0, :, :], B[:, :, :], cosb, ALU.mult))
        dve.tensor_tensor(R[:, 1, :, :], B[:, :, :], sinb, ALU.mult).then_inc(s["rotated"], 1)
        vs.wait()
        dve.wait_ge(s["rotated"], j + 1)
        if jj == SSM_Q - 1:
            dve.drain().then_inc(s["table_free"], 1)
        if jj == 1 and q >= 1:
            ssm_skip(k, dve, q - 1)
    ssm_skip(k, dve, 3)


def ssm_skip(k, dve, q):
    s = k["sig"]
    dve.wait_ge(s["ssm_y_ready"], 4 * q + 4)
    lo = PARAM_AT["d_skip"][0]
    dve.scalar_tensor_tensor(out=k["ysT"][:, q, :], in0=k["uT"][:, q, :], scalar=k["params"][:, lo + q:lo + q + 1],
                             in1=k["ps"][6 + q % 2][:, 0:S], op0=ALU.mult, op1=ALU.add).then_inc(s["gelu_in"], 1)


def ssm_tensor(k, pe):
    s = k["sig"]
    it = k["plan"]["ssm_b"]
    pe.wait_ge(k["landed"][it.slot], it.landed)
    pe.wait_ge(s["proj_act"], 1)
    pe.wait_ge(s["proj_dve"], 1)
    pe.wait_ge(s["ssm_prep_dve"], 2)

    def inputs(j):
        if j >= 2:
            pe.wait_ge(s["bu_read"], j - 1)
        for c in range(2):
            at = (c * SSM_TILES + j) * P
            mm = pe.matmul(k["ps"][4 + j % 2][:, c * S:(c + 1) * S], k["ring"][it.slot][:, at:at + P], k["uT"][:, j // SSM_Q, :], start=True, stop=True)
        mm.then_inc(s["bu_ready"], 1)

    def outputs(j):
        q, jj = divmod(j, SSM_Q)
        if jj == 0 and q >= 2:
            pe.wait_ge(s["gelu_in"], q - 1)
        pe.wait_ge(s["rotated"], j + 1)
        out = k["ps"][6 + q % 2][32 * jj:32 * jj + 32, 0:S]
        R = k["ssm_r"][:, j % 2, :, :, :]
        for n_, (c, trig, part) in enumerate(((0, 0, 0), (1, 1, 1), (2, 0, 1), (2, 1, 0))):
            mm = pe.matmul(out, k["c_mix"][:, c, 32 * j:32 * j + 32], R[:, trig, part, :], start=n_ == 0, stop=n_ == 3)
        mm.then_inc(s["ssm_y_ready"], 1)

    inputs(0)
    for j in range(SSM_TILES):
        if j + 1 < SSM_TILES:
            inputs(j + 1)
        outputs(j)
    it = k["plan"]["w_glu"]
    pe.wait_ge(k["landed"][it.slot], it.landed)
    pe.wait_ge(s["gelu_done"], 4)
    for b in range(2):
        for ff in range(2):
            f = 2 * b + ff
            for kt in range(4):
                at = kt * SSM_W + f * P
                mm = pe.matmul(k["ps"][b][:, ff * S:(ff + 1) * S], k["ring"][it.slot][:, at:at + P], k["ysT"][:, kt, :], start=kt == 0, stop=kt == 3)
        mm.then_inc(s["glu_ready"], 1)


def ssm_scalar(k, act):
    s = k["sig"]
    for q in range(4):
        ssm_trig_scalar(k, act, q)
    for q in range(4):
        act.wait_ge(s["gelu_in"], q + 1)
        act.activation(k["ysT"][:, q, :], k["ysT"][:, q, :], ACT.Gelu_apprx_tanh).then_inc(s["gelu_done"], 1)
    act.wait_ge(s["rope_pool"], 1)
    for b in range(2):
        act.wait_ge(s["glu_ready"], b + 1)
        act.activation(k["ssm_sig"][:, b, :], k["ps"][b][:, :], ACT.Sigmoid).then_inc(s["glu_sig"], 1)


def ssm_gate_vector(k, dve):
    s = k["sig"]
    dve.wait_ge(s["glu_ready"], 2)
    for b in range(2):
        dve.wait_ge(s["glu_sig"], b + 1)
        y = k["ysT"][:, 2 * b:2 * b + 2, :].rearrange("p a b -> p (a b)")
        k["vs"].mark(dve.tensor_tensor(y, y, k["ssm_sig"][:, b, :], ALU.mult))
    k["vs"].wait()




def turn_tensor(k, pe, jobs, base):
    s = k["sig"]
    for j, pieces in enumerate(jobs):
        b = base + j
        if j >= 4:
            pe.wait_ge(s["heads_T_act"] if b % 2 == 0 else s["heads_T_dve"], (b - 4) // 2 + 1)
        for src, n, col in pieces:
            p = src.shape[0]
            mm = pe.transpose(k["ps"][b % 4][0:n, col:col + p], src, con(k, "ident")[0:p, 0:p])
        mm.then_inc(s["heads_T"], 1)


def turn_read(k, eng, jobs, base, parity):
    s = k["sig"]
    for j, (dst, n, cols, *gain) in enumerate(jobs):
        b = base + j
        if b % 2 != parity:
            continue
        eng.wait_ge(s["heads_T"], b + 1)
        src = k["ps"][b % 4][0:n, 0:cols]
        if parity == 0:
            eng.activation(dst, src, ACT.Copy, scale=gain[0] if gain else 1.0).then_inc(s["heads_T_act"], 1)
        elif gain:
            eng.tensor_scalar(dst, src, gain[0], None, ALU.mult).then_inc(s["heads_T_dve"], 1)
        else:
            eng.tensor_copy(dst, src).then_inc(s["heads_T_dve"], 1)


def turned(k, eng, total):
    eng.wait_ge(k["sig"]["heads_T_act"], total // 2)
    eng.wait_ge(k["sig"]["heads_T_dve"], total // 2)




def attend_units(units, base_full, base_all, base_heads):
    full, heads = base_full, base_heads
    for n, u in enumerate(units):
        u.all = base_all + n
        u.full = None
        if u.kind == "full":
            u.full = full
            full += 1
        u.head = heads
        if u.last:
            heads += 1
    return units


def attend_tensor(k, pe, units):
    s = k["sig"]
    fulls = [u for u in units if u.full is not None]
    first_full, first_all, first_head = fulls[0].full, units[0].all, units[0].head

    def score(u):
        if u.full - first_full >= 2:
            pe.wait_ge(s["masked"], u.full - 1)
        bank = k["ps"][u.full % 2]
        pe.matmul(bank[:, 0:P], u.q(0), u.k(0, P), start=True, stop=True)
        pe.matmul(bank[:, P:3 * P], u.q(1), u.k(0, S), start=True, stop=True).then_inc(s["score_ready"], 1)

    def turn(u):
        if u.all - first_all >= 2:
            pe.wait_ge(s["pT_copied"], u.all - 1)
        bank = k["ps"][2 + u.all % 2]
        if u.kind == "full":
            pe.wait_ge(s["p_norm"], u.full + 1)
            for b in range(3):
                mm = pe.transpose(bank[:, b * P:(b + 1) * P], k["prob"][:, u.full % 2, b * P:(b + 1) * P], con(k, "ident"))
        else:
            for t in range(TT):
                mm = pe.transpose(bank[0:N_CMP, t * P:(t + 1) * P], u.p(t), con(k, "ident"))
        mm.then_inc(s["pT_ready"], 1)

    def weigh(u):
        pe.wait_ge(s["pT_copied"], u.all + 1)
        if u.first and u.head - first_head >= 2:
            pe.wait_ge(s["o_copied"], u.head - 1)
        o = k["ps"][4 + u.head % 2][u.at:u.at + u.dv, 0:S]
        pT = k["probT"][:, u.all % 2, :]
        if u.kind == "full":
            pe.matmul(o, u.v(0), pT[:, 0:S], start=u.first, stop=False)
            mm = pe.matmul(o[:, P:S], u.v(1), pT[:, S:S + P], start=False, stop=u.last)
        else:
            mm = pe.matmul(o, u.v(0), pT[0:N_CMP, 0:S], start=u.first, stop=u.last)
        if u.last:
            mm.then_inc(s["o_ready"], 1)
        return mm

    score(fulls[0])
    for n, u in enumerate(units):
        if u.full is not None and u.full - first_full + 1 < len(fulls):
            score(fulls[u.full - first_full + 1])
        if n >= 1:
            weigh(units[n - 1])
        turn(u)
    weigh(units[-1])


def attend_vector(k, dve, units, scale):
    s, vs = k["sig"], k["vs"]
    fulls = [u for u in units if u.full is not None]

    def mask_and_max(u):
        b = u.full % 2
        dve.wait_ge(s["score_ready"], u.full + 1)
        if u.full - fulls[0].full >= 2:
            dve.wait_ge(s["exp_done"], 2 * (u.full - 1))
        dve.tensor_tensor(k["masked"][:, b, :], k["ps"][b][:, 0:3 * P], con(k, "causal"), ALU.add).then_inc(s["masked"], 1)
        dve.wait_ge(s["masked"], u.full + 1)
        vs.mark(dve.tensor_reduce(k["stat"][:, b, 0:1], k["masked"][:, b, 0:P], AX_X, ALU.max))
        vs.mark(dve.tensor_reduce(k["stat"][:, b, 1:2], k["masked"][:, b, P:3 * P], AX_X, ALU.max))
        vs.wait()
        dve.tensor_scalar(k["stat"][:, b, 2:4], k["stat"][:, b, 0:2], -scale, None, ALU.mult).then_inc(s["negmax"], 1)

    def normalise(u):
        b = u.full % 2
        dve.wait_ge(s["exp_done"], 2 * (u.full + 1))
        vs.mark(dve.tensor_scalar(k["stat"][:, b, 4:6], k["stat"][:, b, 4:6], TINY, None, ALU.max))
        vs.wait()
        vs.mark(dve.reciprocal(k["stat"][:, b, 6:8], k["stat"][:, b, 4:6]))
        vs.wait()
        if u.gate is not None:
            vs.mark(dve.tensor_tensor(k["stat"][:, b, 6:8], k["stat"][:, b, 6:8], u.gate, ALU.mult))
            vs.wait()
        vs.mark(dve.tensor_scalar(k["prob"][:, b, 0:P], k["prob"][:, b, 0:P], k["stat"][:, b, 6:7], None, ALU.mult))
        dve.tensor_scalar(k["prob"][:, b, P:3 * P], k["prob"][:, b, P:3 * P], k["stat"][:, b, 7:8], None, ALU.mult).then_inc(s["p_norm"], 1)

    mask_and_max(fulls[0])
    for n, u in enumerate(fulls):
        if n + 1 < len(fulls):
            mask_and_max(fulls[n + 1])
        normalise(u)


def attend_scalar(k, act, units, scale):
    s = k["sig"]
    fulls = [u for u in units if u.full is not None]

    def exps(u):
        b = u.full % 2
        act.wait_ge(s["negmax"], u.full + 1)
        if u.full - fulls[0].full >= 2:
            act.wait_ge(s["pT_ready"], fulls[u.full - fulls[0].full - 2].all + 1)
        for t, (lo, hi) in enumerate(((0, P), (P, 3 * P))):
            act.activation(k["prob"][:, b, lo:hi], k["masked"][:, b, lo:hi], ACT.Exp, bias=k["stat"][:, b, 2 + t:3 + t], scale=scale,
                           accum_out=k["stat"][:, b, 4 + t:5 + t]).then_inc(s["exp_done"], 1)

    def out(u):
        act.wait_ge(s["o_ready"], u.head + 1)
        act.activation(u.out, k["ps"][4 + u.head % 2][u.at:u.at + u.dv, 0:S], ACT.Copy).then_inc(s["o_copied"], 1)

    exps(fulls[0])
    for n, u in enumerate(units):
        if u.full is not None and u.full - fulls[0].full + 1 < len(fulls):
            exps(fulls[u.full - fulls[0].full + 1])
        act.wait_ge(s["pT_ready"], u.all + 1)
        if u.kind == "full":
            act.activation(k["probT"][:, u.all % 2, :], k["ps"][2 + u.all % 2][:, 0:3 * P], ACT.Copy).then_inc(s["pT_copied"], 1)
        else:
            act.activation(k["probT"][0:N_CMP, u.all % 2, 0:S], k["ps"][2 + u.all % 2][0:N_CMP, 0:S], ACT.Copy).then_inc(s["pT_copied"], 1)
        if n >= 1 and units[n - 1].last:
            out(units[n - 1])
    out(units[-1])


def moba_units(k):
    us = []
    for h in range(HEADS):
        lo = HD * (h % 2)
        us.append(Unit(
            kind="full", first=True, last=True, at=lo, dv=HD, gate=None,
            q=lambda t, h=h, lo=lo: k["qT"][lo:lo + HD, h // 2, t * P:(t + 1) * P],
            k=lambda a, b, h=h, lo=lo: k["kT"][lo:lo + HD, h // 2, a:b],
            v=lambda t, h=h: k["v"][:, t, h * HD:(h + 1) * HD],
            out=k["yaT"][lo:lo + HD, h // 2, :]))
    return attend_units(us, 0, 0, 0)


def mla_units(k):
    us = []
    for h in range(MLA_H):
        lo = MLA_V * (h % 2)
        us.append(Unit(
            kind="full", first=True, last=True, at=lo, dv=MLA_V, gate=None,
            q=lambda t, h=h: k["mqT"][0:MLA_QK, h, t * P:(t + 1) * P],
            k=lambda a, b, h=h: k["mkT"][0:MLA_QK, h, a:b],
            v=lambda t, h=h: k["mkv"][:, t, h * P + MLA_NOPE:(h + 1) * P],
            out=k["catT"][lo:lo + MLA_V, h // 2, :]))
    return attend_units(us, 8, 8, 8)


def nsa_units(k):
    us = []
    for h in range(NSA_H):
        lo, g = HD * (h % 2), h // (NSA_H // NSA_G)
        for br, (kT, v) in enumerate(((k["ksT"], k["nkv"]), (k["kwT"], k["nwv"]))):
            us.append(Unit(
                kind="full", first=br == 0, last=False, at=lo, dv=HD, gate=k["gates"][:, :, 3 * h + 1 + br],
                q=lambda t, h=h, lo=lo: k["nqT"][lo:lo + HD, h // 2, t * P:(t + 1) * P],
                k=lambda a, b, g=g, lo=lo, kT=kT: kT[lo:lo + HD, g, a:b],
                v=lambda t, g=g, v=v: v[:, t, NSA_G * HD + g * HD:NSA_G * HD + (g + 1) * HD],
                out=k["catT"][lo:lo + HD, h // 2, :]))
        us.append(Unit(
            kind="cmp", first=False, last=True, at=lo, dv=HD, gate=None,
            p=lambda t, h=h: k["cp"][:, t, h, :],
            v=lambda t, g=g: k["vcmp"][0:N_CMP, g, :],
            out=k["catT"][lo:lo + HD, h // 2, :]))
    return attend_units(us, 16, 16, 16)




def merge_tensor(k, pe):
    s = k["sig"]
    pe.wait_ge(s["o_copied"], HEADS)
    for m in range(4):
        it = k["plan"][f"merge{m}"]
        w = k["ring"][it.slot]
        pe.wait_ge(k["landed"][it.slot], it.landed)
        for ff in range(2):
            u = 2 * m + ff
            if u >= 2:
                pe.wait_ge(s["merged"], u - 1)
            gate, branch = k["ps"][2 * (u % 2)], k["ps"][2 * (u % 2) + 1]
            for g in range(2):
                for kt in range(KT):
                    at = (g * KT + kt) * 256 + ff * P
                    pe.matmul(gate[:, g * S:(g + 1) * S], w[:, at:at + P], k["hT"][:, kt, :], start=kt == 0, stop=kt == KT - 1)
                for kt in range(4):
                    at = 4096 + (g * 4 + kt) * 256 + ff * P
                    src = k["yaT"] if g else k["ysT"]
                    mm = pe.matmul(branch[:, g * S:(g + 1) * S], w[:, at:at + P], src[:, kt, :], start=kt == 0, stop=kt == 3)
            mm.then_inc(s["merge_ready"], 1)


def merge_scalar(k, act):
    s = k["sig"]
    for u in range(KT):
        act.wait_ge(s["merge_ready"], u + 1)
        if u >= 2:
            act.wait_ge(s["merged"], u - 1)
        act.activation(k["msig"][:, u % 2, :], k["ps"][2 * (u % 2)][:, :], ACT.Sigmoid).then_inc(s["merge_sig"], 1)


def merge_vector(k, dve):
    s, vs = k["sig"], k["vs"]
    for u in range(KT):
        dve.wait_ge(s["merge_sig"], u + 1)
        m = k["msig"][:, u % 2, :]
        vs.mark(dve.tensor_tensor(m, m, k["ps"][2 * (u % 2) + 1][:, :], ALU.mult))
        vs.wait()
        dve.tensor_tensor(k["catT"][:, u, :], m[:, 0:S], m[:, S:2 * S], ALU.add).then_inc(s["merged"], 1)


def out_tensor(k, pe, names, base, src):
    s = k["sig"]
    for half, name in enumerate(names):
        it = k["plan"][name]
        pe.wait_ge(k["landed"][it.slot], it.landed)
        for t in range(TT):
            bank = k["ps"][4 + 2 * half + t]
            for kt in range(KT):
                mm = pe.matmul(bank[:, :], src[:, kt, t * P:(t + 1) * P], k["ring"][it.slot][:, kt * 512:(kt + 1) * 512], start=kt == 0, stop=kt == KT - 1)
            mm.then_inc(s["out_ready"], 1)


def post_norm_scalar(k, act, sem, sem_at, src, done, base):
    s = k["sig"]
    for u in range(4):
        if sem is not None:
            act.wait_ge(sem, sem_at[u])
        half, t = divmod(u, 2)
        act.activation(k["junk"][:, :], src(half, t), ACT.Square, accum_out=k["ss4"][:, t, half:half + 1]).then_inc(done, 1)
        act.wait_ge(done, u + 1)
    act.wait_ge(s["post_mean"], base + 1)
    act.activation(k["ss"][:, 2:4], k["ss"][:, 2:4], ACT.Sqrt).then_inc(s["post_root"], 1)


def post_norm_vector(k, dve, src, done, base, row):
    s, vs = k["sig"], k["vs"]
    dve.wait_ge(done, 4)
    vs.mark(dve.tensor_tensor(k["ss"][:, 0:2], k["ss4"][:, :, 0], k["ss4"][:, :, 1], ALU.add))
    vs.wait()
    dve.tensor_scalar(k["ss"][:, 2:4], k["ss"][:, 0:2], 1.0 / D, EPS, ALU.mult, ALU.add).then_inc(s["post_mean"], 1)
    dve.wait_ge(s["post_root"], base + 1)
    vs.mark(dve.reciprocal(k["ss"][:, 4:6], k["ss"][:, 2:4]))
    vs.wait()
    for u in range(4):
        half, t = divmod(u, 2)
        g = k["rows"][:, row * D + half * 512:row * D + (half + 1) * 512]
        x = k["x"][:, t, half * 512:(half + 1) * 512]
        vs.mark(dve.scalar_tensor_tensor(out=k["fold"][:, :], in0=src(half, t), scalar=k["ss"][:, 4 + t:5 + t], in1=g, op0=ALU.mult, op1=ALU.mult))
        vs.wait()
        vs.mark(dve.tensor_tensor(x, x, k["fold"][:, :], ALU.add))
        vs.wait()
    dve.drain().then_inc(s["x_ready"], 1)




def router_tensor(k, pe):
    s = k["sig"]
    lo = PARAM_AT["router_w"][0]
    for t in range(TT):
        for kt in range(KT):
            mm = pe.matmul(k["ps"][4][:, t * E:(t + 1) * E], k["hT"][:, kt, t * P:(t + 1) * P], k["params"][:, lo + kt * E:lo + (kt + 1) * E], start=kt == 0, stop=kt == KT - 1)
    mm.then_inc(s["router_ready"], 1)
    pe.wait_ge(s["weights_ready"], 1)
    for t in range(TT):
        mm = pe.transpose(k["ps"][5][0:E, t * P:(t + 1) * P], k["wtok"][:, t, :], con(k, "ident"))
    mm.then_inc(s["weights_T"], 1)
    pe.wait_ge(s["weights_T_done"], 1)
    pe.wait_ge(s["tie_loaded"], 32)
    for half in range(2):
        for t in range(TT):
            mm = pe.matmul(k["ps"][2 * half + t][:, :], k["wT"][0:E, t * P:(t + 1) * P], k["b_down"][0:E, half * 512:(half + 1) * 512], start=True, stop=True)
    mm.then_inc(s["y_init"], 1)


def router_vector(k, dve):
    s, vs = k["sig"], k["vs"]
    dve.wait_ge(s["router_ready"], 1)
    lg = k["logits"]
    for t in range(TT):
        vs.mark(dve.tensor_tensor(lg[:, t, :], k["ps"][4][:, t * E:(t + 1) * E], par(k, "router_b"), ALU.add))
    vs.wait()
    for t in range(TT):
        vs.mark(dve.tensor_reduce(k["stat"][:, 0, t:t + 1], lg[:, t, :], AX_X, ALU.max))
    vs.wait()
    dve.tensor_scalar(k["stat"][:, 0, 2:4], k["stat"][:, 0, 0:2], -1.0, None, ALU.mult).then_inc(s["router_in"], 1)
    dve.wait_ge(s["tie_loaded"], 32)
    for t in range(TT):
        mine, other = spread_last(lg[:, t, :], E), spread(lg[:, t, :], E)
        vs.mark(dve.tensor_tensor(k["rank_eq"][:, :, :], other, mine, ALU.is_equal))
        vs.mark(dve.tensor_tensor(k["rank_gt"][:, :, :], other, mine, ALU.is_gt))
        vs.wait()
        vs.mark(dve.tensor_tensor(k["rank_eq"][:, :, :], k["rank_eq"][:, :, :], k["tie"][:, :, :], ALU.mult))
        vs.wait()
        vs.mark(dve.tensor_tensor(k["rank_gt"][:, :, :], k["rank_gt"][:, :, :], k["rank_eq"][:, :, :], ALU.add))
        vs.wait()
        vs.mark(dve.tensor_reduce(k["rank"][:, t, :], k["rank_gt"][:, :, :], AX_X, ALU.add))
        vs.wait()
    dve.wait_ge(s["router_exp"], 2)
    for t in range(TT):
        vs.mark(dve.scalar_tensor_tensor(out=k["wtok"][:, t, :], in0=k["rank"][:, t, :], scalar=TOP_K - 0.5, in1=k["wexp"][:, t, :], op0=ALU.is_lt, op1=ALU.mult))
    vs.wait()
    for t in range(TT):
        vs.mark(dve.tensor_reduce(k["stat"][:, 0, 4 + t:5 + t], k["wtok"][:, t, :], AX_X, ALU.add))
    vs.wait()
    vs.mark(dve.reciprocal(k["stat"][:, 0, 6:8], k["stat"][:, 0, 4:6]))
    vs.wait()
    for t in range(TT):
        vs.mark(dve.tensor_scalar(k["wtok"][:, t, :], k["wtok"][:, t, :], k["stat"][:, 0, 6 + t:7 + t], None, ALU.mult))
    vs.wait()
    dve.drain().then_inc(s["weights_ready"], 1)
    dve.wait_ge(s["weights_T"], 1)
    dve.tensor_copy(k["wT"][0:E, :], k["ps"][5][0:E, 0:S]).then_inc(s["weights_T_done"], 1)
    dve.wait_ge(s["y_init"], 1)
    for half in range(2):
        for t in range(TT):
            dve.tensor_copy(k["xn"][:, t, half * 512:(half + 1) * 512], k["ps"][2 * half + t][:, :]).then_inc(s["y_drained"], 1)


def router_scalar(k, act):
    s = k["sig"]
    act.wait_ge(s["router_in"], 1)
    for t in range(TT):
        act.activation(k["wexp"][:, t, :], k["logits"][:, t, :], ACT.Exp, bias=k["stat"][:, 0, 2 + t:3 + t]).then_inc(s["router_exp"], 1)




def gate_up(k, pe, n, slot, parity, landed):
    s = k["sig"]
    w = k["ring"][slot]
    pe.wait_ge(k["landed"][slot], landed)
    pe.wait_ge(s["gu_drained"], n + 1)
    for g in range(2):
        bank = k["ps"][2 * parity + g]
        for ff in range(STEP_TILES):
            for kt in range(KT):
                at = g * STEP_GATE + kt * STEP_COLS + ff * P
                mm = pe.matmul(bank[:, ff * S:(ff + 1) * S], w[:, at:at + P], k["hT"][:, kt, :], start=kt == 0, stop=kt == KT - 1)
    mm.then_inc(s["gu_ready"], 1)


def down(k, pe, n, slot, parity, first, last):
    s = k["sig"]
    w = k["ring"][slot]
    pe.wait_ge(s["act_ready"], n + 2)
    for ff in range(STEP_TILES):
        for t in range(TT):
            for half in range(2):
                at = 2 * STEP_GATE + ff * D + half * 512
                mm = pe.matmul(k["ps"][4 + 2 * half + t][:, :], k["act"][:, parity, ff, t * P:(t + 1) * P], w[:, at:at + 512],
                               start=first and ff == 0, stop=last and ff == STEP_TILES - 1)
    mm.then_inc(s["down_done"], 1)


def moe_tensor(k, pe):
    s = k["sig"]
    base = k["moe"].landed

    def gu(e, i):
        gate_up(k, pe, 4 * e + i, i, i % 2, base[i] + 16 * e)

    def dn(e, i):
        if i == 0:
            pe.wait_ge(s["y_drained"], 4 * e + 4)
        down(k, pe, 4 * e + i, i, i % 2, i == 0, i == MOE_STEPS - 1)

    pe.wait_ge(s["y_drained"], 4)
    gu(0, 0)
    with pe.Fori(0, E - 1) as e:
        for i in range(MOE_STEPS):
            if i + 1 < MOE_STEPS:
                gu(e, i + 1)
            else:
                gu(e + 1, 0)
            dn(e, i)
    for i in range(MOE_STEPS):
        if i + 1 < MOE_STEPS:
            gu(E - 1, i + 1)
        dn(E - 1, i)


def moe_vector(k, dve):
    s = k["sig"]
    lo = PARAM_AT["b_gu"][0]
    with dve.Fori(0, E) as e:
        for i in range(MOE_STEPS):
            n = 4 * e + i
            par_ = i % 2
            dve.wait_ge(s["gu_ready"], n + 1)
            dve.wait_ge(s["act_ready"], n + 1)
            for ff in range(STEP_TILES):
                b = lo + e * 16 + (i * STEP_TILES + ff) * 2
                cols = slice(ff * S, (ff + 1) * S)
                gate = dve.tensor_scalar(k["gate"][:, cols], k["ps"][2 * par_][:, cols], k["params"][:, bass.ds(b, 1)], LIMIT, ALU.add, ALU.min)
                if ff == STEP_TILES - 1:
                    gate.then_inc(s["gate_ready"], 1)
            for ff in range(STEP_TILES):
                b = lo + e * 16 + (i * STEP_TILES + ff) * 2 + 1
                cols = slice(ff * S, (ff + 1) * S)
                up = dve.tensor_scalar(k["up"][:, cols], k["ps"][2 * par_ + 1][:, cols], k["params"][:, bass.ds(b, 1)], LIMIT, ALU.add, ALU.min)
                if ff == STEP_TILES - 1:
                    up.then_inc(s["gu_drained"], 1)
            dve.wait_ge(s["gu_drained"], n + 3)
            dve.tensor_scalar(k["up"][:, :], k["up"][:, :], -LIMIT, 1.0, ALU.max, ALU.add).then_inc(s["swi_step"], 1)
            dve.wait_ge(s["sig_ready"], n + 1)
            dve.tensor_tensor(k["sg"][:, :], k["sg"][:, :], k["gate"][:, :], ALU.mult).then_inc(s["swi_step"], 1)
            dve.wait_ge(s["swi_step"], 2 * n + 2)
            dve.wait_ge(s["down_done"], n + 1)
            dve.tensor_tensor(k["act"][:, par_, :, :].rearrange("p a b -> p (a b)"), k["sg"][:, :], k["up"][:, :], ALU.mult).then_inc(s["act_ready"], 1)
        dve.wait_ge(s["down_done"], 4 * e + 6)
        dve.wait_ge(s["y_drained"], 4 * e + 4)
        for half in range(2):
            for t in range(TT):
                acc = k["xn"][:, t, half * 512:(half + 1) * 512]
                dve.scalar_tensor_tensor(out=acc, in0=k["ps"][4 + 2 * half + t][:, :], scalar=k["wtok"][:, t, bass.ds(e, 1)], in1=acc,
                                         op0=ALU.mult, op1=ALU.add).then_inc(s["y_drained"], 1)


def moe_scalar(k, act):
    s = k["sig"]
    with act.Fori(0, E * MOE_STEPS) as n:
        act.wait_ge(s["gate_ready"], n + 1)
        act.activation(k["sg"][:, :], k["gate"][:, :], ACT.Sigmoid, scale=ALPHA).then_inc(s["sig_ready"], 1)


def moe_sync(k, sp):
    s = k["sig"]

    def load(e, i):
        sp.dma_start(k["ring"][i][:, :], k["src"]["moe"][bass.ds(4 * e + i, 1), :, :].rearrange("o p n -> (o p) n")).then_inc(k["landed"][i], 16)

    for i in range(MOE_STEPS):
        if k["moe"].free[i] is not None:
            sp.wait_ge(*k["moe"].free[i])
        load(0, i)
    with sp.Fori(1, E) as e:
        for i in range(MOE_STEPS):
            sp.wait_ge(s["down_done"], 4 * e + i - 1)
            load(e, i)


def ffn_tensor(k, pe, q):
    base = E * MOE_STEPS + FFN_STEPS * q
    items = [k["plan"][f"ffn{q}_{m}"] for m in range(FFN_STEPS)]

    def gu(m):
        gate_up(k, pe, base + m, items[m].slot, (base + m) % 2, items[m].landed)

    gu(0)
    for m in range(FFN_STEPS):
        if m + 1 < FFN_STEPS:
            gu(m + 1)
        down(k, pe, base + m, items[m].slot, (base + m) % 2, m == 0, m == FFN_STEPS - 1)


def ffn_vector(k, dve, q):
    s, vs = k["sig"], k["vs"]
    base = E * MOE_STEPS + FFN_STEPS * q
    for m in range(FFN_STEPS):
        n = base + m
        par_ = n % 2
        dve.wait_ge(s["sig_ready"], n + 1)
        dve.tensor_tensor(k["sg"][:, :], k["sg"][:, :], k["ps"][2 * par_][:, :], ALU.mult).then_inc(s["swi_step"], 1)
        dve.wait_ge(s["swi_step"], 2 * E * MOE_STEPS + (n - E * MOE_STEPS) + 1)
        dve.wait_ge(s["down_done"], n + 1)
        dve.tensor_tensor(k["act"][:, par_, :, :].rearrange("p a b -> p (a b)"), k["sg"][:, :], k["ps"][2 * par_ + 1][:, :], ALU.mult).then_inc(s["act_ready"], 1)
        dve.wait_ge(s["act_ready"], n + 2)
        dve.drain().then_inc(s["gu_drained"], 1)
    dve.wait_ge(s["down_done"], 2 + base + FFN_STEPS)
    for u in range(4):
        half, t = divmod(u, 2)
        x = k["x"][:, t, half * 512:(half + 1) * 512]
        vs.mark(dve.scalar_tensor_tensor(out=x, in0=k["ps"][4 + u][:, :], scalar=0.5, in1=x, op0=ALU.mult, op1=ALU.add))
    vs.wait()
    dve.drain().then_inc(s["x_ready"], 1)


def ffn_scalar(k, act, q):
    s = k["sig"]
    base = E * MOE_STEPS + FFN_STEPS * q
    for m in range(FFN_STEPS):
        n = base + m
        act.wait_ge(s["gu_ready"], n + 1)
        if m >= 1:
            act.wait_ge(s["act_ready"], n + 1)
        act.activation(k["sg"][:, :], k["ps"][2 * (n % 2)][:, :], ACT.Sigmoid).then_inc(s["sig_ready"], 1)


def add_out_vector(k, dve, base):
    s, vs = k["sig"], k["vs"]
    for u in range(4):
        half, t = divmod(u, 2)
        dve.wait_ge(s["out_ready"], base + u + 1)
        x = k["x"][:, t, half * 512:(half + 1) * 512]
        vs.mark(dve.tensor_tensor(x, x, k["ps"][4 + u][:, :], ALU.add))
    vs.wait()
    dve.drain().then_inc(s["x_ready"], 1)




def lora_norm_scalar(k, act):
    s = k["sig"]
    n = 0
    for t in range(TT):
        act.wait_ge(s["proj_act"], 5)
        act.wait_ge(s["proj_dve"], 5)
        for c, (lo, w) in enumerate(((0, Q_LORA), (Q_LORA, KV_LORA))):
            act.activation(k["lora_n"][:, t, lo:lo + w], k["hya"][:, t, lo:lo + w], ACT.Square,
                           accum_out=k["small"][:, 2 * c + t:2 * c + t + 1]).then_inc(s["lora_sq"], 1)
    act.wait_ge(s["lora_mean"], 2)
    act.activation(k["small"][:, 4:8], k["small"][:, 4:8], ACT.Sqrt).then_inc(s["lora_root"], 1)


def lora_norm_vector(k, dve):
    s, vs = k["sig"], k["vs"]
    dve.wait_ge(s["lora_sq"], 4)
    dve.tensor_scalar(k["small"][:, 4:6], k["small"][:, 0:2], 1.0 / Q_LORA, EPS, ALU.mult, ALU.add).then_inc(s["lora_mean"], 1)
    dve.tensor_scalar(k["small"][:, 6:8], k["small"][:, 2:4], 1.0 / KV_LORA, EPS, ALU.mult, ALU.add).then_inc(s["lora_mean"], 1)
    dve.wait_ge(s["lora_root"], 1)
    vs.mark(dve.reciprocal(k["small"][:, 8:12], k["small"][:, 4:8]))
    vs.wait()
    for t in range(TT):
        for c, (lo, w) in enumerate(((0, Q_LORA), (Q_LORA, KV_LORA))):
            dve.tensor_scalar(k["lora_n"][:, t, lo:lo + w], k["hya"][:, t, lo:lo + w], k["small"][:, 8 + 2 * c + t:9 + 2 * c + t], None, ALU.mult)\
               .then_inc(s["lora_n"], 1)


def hy_turn_jobs(k):
    jobs = [[(k["lora_n"][:, t, c * P:(c + 1) * P], P, t * P) for t in range(TT)] for c in range(3)]
    jobs += [[(k["hyb"][:, t, (2 * g + c) * P:(2 * g + c + 1) * P], P, (2 * c + t) * P) for c in range(2) for t in range(TT)] for g in range(2)]
    jobs += [[(k["hya"][:, t, HYA - GLA_RANK:HYA], GLA_RANK, t * P) for t in range(TT)]]
    lo = PARAM_AT["q_norm"][0]
    kv = PARAM_AT["kv_norm"][0]
    reads = [(k["loraT"][:, 0, :], P, S, k["params"][:, lo:lo + 1]), (k["loraT"][:, 1, :], P, S, k["params"][:, lo + 1:lo + 2]),
             (k["loraT"][:, 2, :], P, S, k["params"][:, kv:kv + 1]),
             (k["gqT"][:, :, :].rearrange("p a b -> p (a b)"), P, 2 * S), (k["gkT"][:, :, :].rearrange("p a b -> p (a b)"), P, 2 * S),
             (k["gaT"][0:GLA_RANK, :], GLA_RANK, S)]
    return jobs, reads


def lora_tensor(k, pe):
    s = k["sig"]
    it = k["plan"]["lora"]
    w = k["ring"][it.slot]
    pe.wait_ge(k["landed"][it.slot], it.landed)
    for t in range(TT):
        for i in range(4):
            u = 4 * t + i
            if t == 1:
                pe.wait_ge(s["lora_act"] if i % 2 == 0 else s["lora_dve"], i // 2 + 1)
            if i < 2:
                for kt in range(2):
                    mm = pe.matmul(k["ps"][i][:, 0:384], k["loraT"][:, kt, t * P:(t + 1) * P], w[:, kt * 768 + i * 384:kt * 768 + (i + 1) * 384],
                                   start=kt == 0, stop=kt == 1)
            else:
                at = 2 * 768 + (i - 2) * 512
                mm = pe.matmul(k["ps"][i][:, :], k["loraT"][:, 2, t * P:(t + 1) * P], w[:, at:at + 512], start=True, stop=True)
            mm.then_inc(s["lora_ready"], 1)


def lora_read(k, eng, parity):
    s = k["sig"]
    for t in range(TT):
        for i in range(parity, 4, 2):
            eng.wait_ge(s["lora_ready"], 4 * t + i + 1)
            dst = k["mq"][:, t, i * 384:(i + 1) * 384] if i < 2 else k["mkv"][:, t, (i - 2) * 512:(i - 1) * 512]
            src = k["ps"][i][:, 0:dst.shape[1]]
            if parity == 0:
                eng.activation(dst, src, ACT.Copy).then_inc(s["lora_act"], 1)
            else:
                eng.tensor_copy(dst, src).then_inc(s["lora_dve"], 1)


def mla_rows(k, eng, steps, t, done, tmp):
    s = k["sig"]
    eng.wait_ge(s["lora_act"], 4)
    eng.wait_ge(s["lora_dve"], 4)
    cos, sin = angle(k, k["cos"], f"m{t}"), angle(k, k["sin"], f"m{t}")
    q = k["mq"][:, t, :].rearrange("p (h x) -> p h x", h=MLA_H)
    rope_rotate(eng, steps, q[:, :, MLA_NOPE:MLA_QK], q[:, :, MLA_NOPE:MLA_QK], MLA_H, MLA_ROPE // 2, cos, sin, tmp)
    kr = k["hya"][:, t, Q_LORA + KV_LORA:Q_LORA + KV_LORA + MLA_ROPE]
    kr1 = kr.unsqueeze(1)
    rope_rotate(eng, steps, kr1, kr1, 1, MLA_ROPE // 2, cos, sin, tmp)
    full = k["mk"][:, t, :].rearrange("p (h x) -> p h x", h=MLA_H)
    kv = k["mkv"][:, t, :].rearrange("p (h x) -> p h x", h=MLA_H)
    steps.mark(eng.tensor_copy(full[:, :, 0:MLA_NOPE], kv[:, :, 0:MLA_NOPE]))
    steps.mark(eng.tensor_copy(full[:, :, MLA_NOPE:MLA_QK], spread(kr, MLA_H)))
    steps.wait()
    eng.drain().then_inc(done, 1)


def mla_turn_jobs(k):
    jobs, reads = [], []
    for rows, dst in ((k["mq"], k["mqT"]), (k["mk"], k["mkT"])):
        for b in range(4):
            jobs.append([(rows[:, t, h * MLA_QK:(h + 1) * MLA_QK], MLA_QK, ((h - 2 * b) * 2 + t) * P) for h in (2 * b, 2 * b + 1) for t in range(TT)])
            reads.append((dst[0:MLA_QK, 2 * b:2 * b + 2, :].rearrange("p a b -> p (a b)"), MLA_QK, 2 * S))
    return jobs, reads


def gla_rows(k, t, h):
    at = (2 * t + h // 2) * P
    return k["ps"][2 + h % 2][:, at:at + P]


def gla_tensor(k, pe):
    s = k["sig"]
    wa = PARAM_AT["w_a2"][0]
    for c in range(2):
        mm = pe.matmul(k["ps"][6][:, c * S:(c + 1) * S], k["params"][0:GLA_RANK, wa + c * P:wa + (c + 1) * P], k["gaT"][0:GLA_RANK, :], start=True, stop=True)
    mm.then_inc(s["gla_pre"], 1)
    pe.wait_ge(s["gla_ready"], 3)
    for t in range(TT):
        for c in range(2):
            mm = pe.transpose(k["ps"][7][:, (2 * t + c) * P:(2 * t + c + 1) * P], k["kdecT"][:, c, t * P:(t + 1) * P], con(k, "ident"))
    mm.then_inc(s["gla_kdec"], 1)
    for hh in range(2):
        lo = 64 * hh
        for t in range(TT):
            for c in range(2):
                mm = pe.matmul(k["ps"][hh][:, (2 * t + c) * P:(2 * t + c + 1) * P], k["kdecT"][lo:lo + 64, c, t * P:(t + 1) * P],
                               k["qintraT"][lo:lo + 64, c, t * P:(t + 1) * P], start=True, stop=True)
        mm.then_inc(s["gla_A"], 1)
    pe.wait_ge(s["gla_kdec_read"], 1)
    for odd in range(2):
        for n in range(odd, NCH - 1, 2):
            for c in range(2):
                for hh in range(2):
                    h, lo, tok, at = 2 * c + hh, 64 * hh, CHUNK * odd, (n // 2 * 2 + c) * P
                    mm = pe.matmul(k["ps"][4 + odd][lo:lo + 64, at:at + P], k["kdec"][tok:tok + CHUNK, n // 2, c, lo:lo + 64],
                                   k["hyv"][tok:tok + CHUNK, n // 2, h * P:(h + 1) * P], start=True, stop=True)
        mm.then_inc(s["gla_kv"], 1)
    pe.wait_ge(s["gla_state"], 2)
    pe.wait_ge(s["gla_A_read"], 2)
    for hh in range(2):
        for n2 in range(4):
            t, c = divmod(n2, 2)
            h, lo = 2 * c + hh, 64 * hh
            pe.matmul(gla_rows(k, t, h), k["AT"][:, h % 2, 2 * t + c, :], k["hyv"][:, t, h * P:(h + 1) * P], start=True, stop=False, skip_group_check=True)
            for n in (2 * t, 2 * t + 1):
                if n == 0:
                    continue
                at = CHUNK * (n % 2)
                mm = pe.matmul(gla_rows(k, t, h)[at:at + CHUNK, :], k["qinterT"][lo:lo + 64, c, n * CHUNK:(n + 1) * CHUNK],
                               k["state"][lo:lo + 64, c, n - 1, :], start=False, stop=n == 2 * t + 1, skip_group_check=True)
        mm.then_inc(s["gla_o"], 1)


def gla_vector(k, dve):
    s, vs = k["sig"], k["vs"]
    ba = PARAM_AT["b_a"][0]
    dve.wait_ge(s["gla_pre"], 1)
    z, la = k["gz"], k["gla"]
    for c in range(2):
        vs.mark(dve.tensor_scalar(z[:, c, :], k["ps"][6][:, c * S:(c + 1) * S], k["params"][:, ba + c:ba + c + 1], None, ALU.add))
    vs.wait()
    vs.mark(dve.tensor_scalar(la[:, :, :], z[:, :, :], -1.0, None, ALU.mult))
    vs.wait()
    dve.tensor_tensor(la[:, :, :], la[:, :, :], z[:, :, :], ALU.max).then_inc(s["gla_abs"], 1)
    vs.mark(dve.tensor_scalar(z[:, :, :], z[:, :, :], 0.0, None, ALU.min))
    vs.wait()
    dve.wait_ge(s["gla_soft"], 2)
    vs.mark(dve.tensor_tensor(z[:, :, :], z[:, :, :], la[:, :, :], ALU.subtract))
    vs.wait()
    vs.mark(dve.tensor_scalar(z[:, :, :], z[:, :, :], 1.0 / GLA_TAU, None, ALU.mult))
    vs.wait()
    for c in range(2):
        vs.mark(dve.tensor_tensor_scan(k["gb"][:, c, :], con(k, "gla_keep"), z[:, c, :], 0.0, ALU.mult, ALU.add))
    vs.wait()
    for c in range(2):
        b = k["gb"][:, c, :].rearrange("p (n i) -> p n i", n=NCH)
        last = b[:, :, CHUNK - 1:CHUNK].to_broadcast([P, NCH, CHUNK])
        dve.tensor_tensor(k["gd"][:, c, :].rearrange("p (n i) -> p n i", n=NCH), last, b, ALU.subtract).then_inc(s["gla_arg"], 1)
    dve.wait_ge(s["gla_exp"], 4)
    dve.tensor_tensor(k["kdecT"][:, :, :], k["gkT"][:, :, :], k["ge"][:, 0, :, :], ALU.mult).then_inc(s["gla_ready"], 1)
    dve.scalar_tensor_tensor(out=k["qintraT"][:, :, :], in0=k["gqT"][:, :, :], scalar=GLA_DK ** -0.5, in1=k["ge"][:, 1, :, :], op0=ALU.mult, op1=ALU.mult).then_inc(s["gla_ready"], 1)
    dve.scalar_tensor_tensor(out=k["qinterT"][:, :, :], in0=k["gqT"][:, :, :], scalar=GLA_DK ** -0.5, in1=k["ge"][:, 2, :, :], op0=ALU.mult, op1=ALU.mult).then_inc(s["gla_ready"], 1)
    dve.wait_ge(s["gla_kdec"], 1)
    dve.tensor_copy(k["kdec"][:, :, :, :].rearrange("p a b c -> p (a b c)"), k["ps"][7][:, :]).then_inc(s["gla_kdec_read"], 1)
    for hh in range(2):
        dve.wait_ge(s["gla_A"], hh + 1)
        dve.tensor_tensor(k["AT"][:, hh, :, :], k["ps"][hh][:, :].rearrange("p (n i) -> p n i", n=4), spread(con(k, "gla_mask"), 4), ALU.mult).then_inc(s["gla_A_read"], 1)
    dve.wait_ge(s["gla_kv"], 2)
    for c in range(2):
        vs.mark(dve.tensor_copy(k["state"][:, c, 0, :], k["ps"][4][:, c * P:(c + 1) * P]))
        vs.wait()
        for n in (1, 2):
            ins = dve.scalar_tensor_tensor(out=k["state"][:, c, n, :], in0=k["state"][:, c, n - 1, :], scalar=k["gdec"][:, c, n:n + 1],
                                           in1=k["ps"][4 + n % 2][:, (n // 2 * 2 + c) * P:(n // 2 * 2 + c + 1) * P], op0=ALU.mult, op1=ALU.add)
            if n == 1:
                vs.mark(ins)
                vs.wait()
        ins.then_inc(s["gla_state"], 1)
    dve.wait_ge(s["gla_sq"], 8)
    dve.tensor_scalar(k["small"][:, 16:24], k["small"][:, 16:24], 1.0 / GLA_DV, EPS, ALU.mult, ALU.add).then_inc(s["gla_mean"], 1)
    dve.wait_ge(s["gla_root"], 1)
    vs.mark(dve.reciprocal(k["small"][:, 24:32], k["small"][:, 16:24]))
    vs.wait()
    dve.wait_ge(s["gla_silu"], 2)
    for t in range(TT):
        vs.mark(dve.tensor_tensor(k["hyr"][:, t, :], k["hyr"][:, t, :], k["rsig"][:, t, :], ALU.mult))
        for h in range(GLA_H):
            vs.mark(dve.scalar_tensor_tensor(out=k["rsig2"][:, t, h * P:(h + 1) * P], in0=gla_rows(k, t, h),
                                             scalar=k["small"][:, 24 + 4 * t + h:25 + 4 * t + h], in1=par(k, "out_norm"), op0=ALU.mult, op1=ALU.mult))
        vs.wait()
        dve.tensor_tensor(k["rsig2"][:, t, :], k["rsig2"][:, t, :], k["hyr"][:, t, :], ALU.mult).then_inc(s["gla_out"], 1)


def gla_scalar(k, act):
    s, acs = k["sig"], k["acs"]
    act.wait_ge(s["gla_abs"], 1)
    act.activation(k["gla"][:, :, :], k["gla"][:, :, :], ACT.Exp, scale=-1.0).then_inc(s["gla_soft"], 1)
    act.wait_ge(s["gla_soft"], 1)
    act.activation(k["gla"][:, :, :], k["gla"][:, :, :], ACT.Ln, bias=1.0).then_inc(s["gla_soft"], 1)
    act.wait_ge(s["gla_arg"], 2)
    act.activation(k["ge"][:, 0, :, :], k["gd"][:, :, :], ACT.Exp).then_inc(s["gla_exp"], 1)
    act.activation(k["ge"][:, 1, :, :], k["gd"][:, :, :], ACT.Exp, scale=-1.0).then_inc(s["gla_exp"], 1)
    act.activation(k["ge"][:, 2, :, :], k["gb"][:, :, :], ACT.Exp).then_inc(s["gla_exp"], 1)
    act.activation(k["gdec"][:, :, :], k["gb"][:, :, CHUNK - 1:S:CHUNK], ACT.Exp).then_inc(s["gla_exp"], 1)
    for t in range(TT):
        act.activation(k["rsig"][:, t, :], k["hyr"][:, t, :], ACT.Sigmoid).then_inc(s["gla_silu"], 1)
    act.wait_ge(s["gla_o"], 2)
    for t in range(TT):
        for h in range(GLA_H):
            act.activation(k["rsig2"][:, t, h * P:(h + 1) * P], gla_rows(k, t, h), ACT.Square,
                           accum_out=k["small"][:, 16 + 4 * t + h:17 + 4 * t + h]).then_inc(s["gla_sq"], 1)
    act.wait_ge(s["gla_mean"], 1)
    act.activation(k["small"][:, 16:24], k["small"][:, 16:24], ACT.Sqrt).then_inc(s["gla_root"], 1)


def gla_turn_jobs(k):
    jobs = [[(k["rsig2"][:, t, (2 * b + c) * P:(2 * b + c + 1) * P], P, (2 * c + t) * P) for c in range(2) for t in range(TT)] for b in range(2)]
    reads = [(k["catT"][:, 4 + 2 * b:6 + 2 * b, :].rearrange("p a b -> p (a b)"), P, 2 * S) for b in range(2)]
    return jobs, reads




def nsa_rows(k, eng, steps, t, done, tmp):
    cos, sin = angle(k, k["cos"], f"b{t}"), angle(k, k["sin"], f"b{t}")
    rope_rotate(eng, steps, k["xn"][:, t, :].rearrange("p (h x) -> p h x", h=NSA_H), k["nq"][:, t, :].rearrange("p (h x) -> p h x", h=NSA_H),
                NSA_H, HD // 2, cos, sin, tmp)
    for w, rows in enumerate((k["nkv"], k["nwv"])):
        kd = k["kd"][:, t, w, :, :, :]
        rope_rotate(eng, steps, kd[:, :, 0, :], rows[:, t, 0:NSA_G * HD].rearrange("p (h x) -> p h x", h=NSA_G), NSA_G, HD // 2, cos, sin, tmp)
        steps.mark(eng.tensor_copy(kd[:, :, 1, :], kd[:, :, 0, :]))
    steps.wait()
    eng.drain().then_inc(done, 1)


def nsa_turn_jobs(k):
    jobs, reads = [], []

    def four(tile, dst, tiles):
        for b in range(tiles // 2):
            jobs.append([(tile(2 * b + c, t), P, (2 * c + t) * P) for c in range(2) for t in range(TT)])
            reads.append((dst[:, 2 * b:2 * b + 2, :].rearrange("p a b -> p (a b)"), P, 2 * S))

    four(lambda c, t: k["kcv"][:, t, c * P:(c + 1) * P], k["kcvT"], 4)
    four(lambda c, t: k["xn"][:, t, c * P:(c + 1) * P], k["nqT"], 8)
    four(lambda c, t: k["kd"][:, t, 0, c, :, :].rearrange("p a b -> p (a b)"), k["ksT"], 4)
    four(lambda c, t: k["kd"][:, t, 1, c, :, :].rearrange("p a b -> p (a b)"), k["kwT"], 4)
    return jobs, reads


def cmp_tensor(k, pe):
    s = k["sig"]
    it = k["plan"]["nsa_c"]
    w = k["ring"][it.slot]
    pe.wait_ge(k["landed"][it.slot], it.landed)
    for t in range(TT):
        for kt in range(KT):
            mm = pe.matmul(k["ps"][6][:, t * 48:(t + 1) * 48], k["hT"][:, kt, t * P:(t + 1) * P], w[:, 4096 + kt * 48:4096 + (kt + 1) * 48], start=kt == 0, stop=kt == KT - 1)
    mm.then_inc(s["gate_in"], 1)
    pe.wait_ge(s["cmp_blk"], 8)
    for c in range(2):
        lo = 64 * c
        for n in range(CMP_LEN):
            mm = pe.matmul(k["ps"][4 + c][:, 0:NSA_G * N_CMP], w[lo:lo + HD, n * CMP_HID:(n + 1) * CMP_HID], k["blk"][lo:lo + HD, n, :, :].rearrange("p a b -> p (a b)"),
                           start=n == 0, stop=n == CMP_LEN - 1)
        mm.then_inc(s["cmp_h"], 1)
    pe.wait_ge(s["cmp_hid"], 2)
    for c in range(2):
        for g in range(NSA_G):
            at = 4096 + 384 + c * HD
            mm = pe.matmul(k["ps"][7][0:N_CMP, c * S + g * HD:c * S + (g + 1) * HD], k["hidT"][:, c, g * N_CMP:(g + 1) * N_CMP], w[:, at:at + HD], start=True, stop=True)
        mm.then_inc(s["cmp_kv"], 1)
    pe.wait_ge(s["cmp_k"], 1)
    for g in range(NSA_G):
        mm = pe.transpose(k["ps"][4][:, g * N_CMP:(g + 1) * N_CMP], k["kcmp"][0:N_CMP, g, :, :].rearrange("p a b -> p (a b)"), con(k, "ident")[0:N_CMP, 0:N_CMP])
    mm.then_inc(s["cmp_kT"], 1)
    pe.wait_ge(s["cmp_kT_read"], 1)
    pe.wait_ge(s["gate_sig"], 1)
    for odd in range(2):
        for n in range(NSA_H):
            t, h = n // 8, n % 8 * 2 + odd
            lo, g = HD * odd, h // (NSA_H // NSA_G)
            at = n * N_CMP
            mm = pe.matmul(k["ps"][5 + odd][:, at:at + N_CMP], k["nqT"][lo:lo + HD, h // 2, t * P:(t + 1) * P], k["kcmpT"][lo:lo + HD, g, :], start=True, stop=True)
    mm.then_inc(s["cmp_score"], 1)


def cmp_vector(k, dve):
    s, vs = k["sig"], k["vs"]
    pos = PARAM_AT["pos_kv"][0]
    turned(k, dve, 26)
    for r in range(2):
        for g in range(NSA_G):
            src = k["kcvT"][:, g, :].rearrange("p (n l) -> p l n", l=CMP_STRIDE)[:, :, r:r + N_CMP]
            add = spread_last(k["params"][:, pos + r * CMP_STRIDE:pos + (r + 1) * CMP_STRIDE], N_CMP)
            dve.tensor_tensor(k["blk"][:, r * CMP_STRIDE:(r + 1) * CMP_STRIDE, g, :], src, add, ALU.add).then_inc(s["cmp_blk"], 1)
    for c in range(2):
        dve.wait_ge(s["cmp_sig"], c + 1)
        dve.tensor_tensor(k["hidT"][:, c, :], k["hidT"][:, c, :], k["ps"][4 + c][:, 0:NSA_G * N_CMP], ALU.mult).then_inc(s["cmp_hid"], 1)
    dve.wait_ge(s["cmp_kv"], 2)
    vs.mark(dve.tensor_copy(k["kcr"][0:N_CMP, :], k["ps"][7][0:N_CMP, 0:S]))
    vs.mark(dve.tensor_copy(k["vcmp"][0:N_CMP, :, :].rearrange("p a b -> p (a b)"), k["ps"][7][0:N_CMP, S:2 * S]))
    vs.wait()
    kc = k["kcmp"][0:N_CMP, :, :, :]
    rope_rotate(dve, vs, kc[:, :, 0, :], k["kcr"][0:N_CMP, :].rearrange("p (h x) -> p h x", h=NSA_G), NSA_G, HD // 2,
                angle(k, k["cos"], "e", N_CMP), angle(k, k["sin"], "e", N_CMP), k["tmp_dve"])
    dve.tensor_copy(kc[:, :, 1, :], kc[:, :, 0, :]).then_inc(s["cmp_k"], 1)
    dve.wait_ge(s["cmp_kT"], 1)
    dve.tensor_copy(k["kcmpT"][:, :, :].rearrange("p a b -> p (a b)"), k["ps"][4][:, 0:NSA_G * N_CMP]).then_inc(s["cmp_kT_read"], 1)
    dve.wait_ge(s["cmp_score"], 1)
    add, one = con(k, "cmp_add"), con(k, "cmp_one")
    for t in range(TT):
        for odd in range(2):
            sc = k["ps"][5 + odd][:, t * 8 * N_CMP:(t + 1) * 8 * N_CMP].rearrange("p (h n) -> p h n", h=8)
            vs.mark(dve.scalar_tensor_tensor(out=k["cp"][:, t, odd:NSA_H:2, :], in0=sc, scalar=HD ** -0.5, in1=spread(add[:, t * N_CMP:(t + 1) * N_CMP], 8),
                                             op0=ALU.mult, op1=ALU.add))
    vs.wait()
    for t in range(TT):
        vs.mark(dve.tensor_reduce(k["cs"][:, t, :], k["cp"][:, t, :, :], AX_X, ALU.max))
    vs.wait()
    for t in range(TT):
        dve.tensor_tensor(k["cp"][:, t, :, :], k["cp"][:, t, :, :], spread_last(k["cs"][:, t, :], N_CMP), ALU.subtract).then_inc(s["cmp_arg"], 1)
    dve.wait_ge(s["cmp_exp"], 2)
    for t in range(TT):
        vs.mark(dve.tensor_tensor(k["cp"][:, t, :, :], k["cp"][:, t, :, :], spread(one[:, t * N_CMP:(t + 1) * N_CMP], NSA_H), ALU.mult))
    vs.wait()
    for t in range(TT):
        vs.mark(dve.tensor_reduce(k["cs"][:, t, :], k["cp"][:, t, :, :], AX_X, ALU.add))
    vs.wait()
    vs.mark(dve.tensor_scalar(k["cs"][:, :, :], k["cs"][:, :, :], TINY, None, ALU.max))
    vs.wait()
    vs.mark(dve.reciprocal(k["cs"][:, :, :], k["cs"][:, :, :]))
    vs.wait()
    dve.wait_ge(s["gate_sig"], 1)
    vs.mark(dve.tensor_tensor(k["cs"][:, :, :], k["cs"][:, :, :], k["gates"][:, :, 0:48:3], ALU.mult))
    vs.wait()
    for t in range(TT):
        dve.tensor_tensor(k["cp"][:, t, :, :], k["cp"][:, t, :, :], spread_last(k["cs"][:, t, :], N_CMP), ALU.mult).then_inc(s["cmp_p"], 1)


def cmp_scalar(k, act):
    s = k["sig"]
    act.wait_ge(s["gate_in"], 1)
    act.activation(k["gates"][:, :, :].rearrange("p a b -> p (a b)"), k["ps"][6][:, 0:96], ACT.Sigmoid).then_inc(s["gate_sig"], 1)
    for c in range(2):
        act.wait_ge(s["cmp_h"], c + 1)
        act.activation(k["hidT"][:, c, :], k["ps"][4 + c][:, 0:NSA_G * N_CMP], ACT.Sigmoid).then_inc(s["cmp_sig"], 1)
    for t in range(TT):
        act.wait_ge(s["cmp_arg"], t + 1)
        act.activation(k["cp"][:, t, :, :], k["cp"][:, t, :, :], ACT.Exp).then_inc(s["cmp_exp"], 1)




def program(nc, src, out):
    ctx = ExitStack()
    with ctx:
        def sem(name):
            return ctx.enter_context(nc.semaphore(name))

        k = {"src": src}
        k["sig"] = {n: sem(n) for n in SIGNALS}
        k["landed"] = [sem(f"landed{i}") for i in range(4)]
        k["plan"], before, k["moe"], after = plan_ring(k["sig"])
        k["ps"] = [ctx.enter_context(nc.psum_tensor(f"bank{i}", [P, 512], F32)) for i in range(8)]

        def place(stack, name, shape, dt=F32):
            t = stack.enter_context(nc.sbuf_tensor(name, shape, dt))
            k[name] = t
            return t

        ring = [place(ctx, f"slot{i}", [P, SLOT]) for i in range(3)]
        place(ctx, "x", [P, TT, D])
        place(ctx, "hT", [P, KT, S])
        place(ctx, "xn", [P, TT, D])
        place(ctx, "consts", [P, CONST_W])
        place(ctx, "params", [P, PARAM_W])
        work = place(ctx, "work", [P, 2560])
        k["act"] = work[:, 0:1024].rearrange("p (a b c) -> p a b c", a=2, b=2)
        k["gate"], k["sg"], k["up"] = work[:, 1024:1536], work[:, 1536:2048], work[:, 2048:2560]
        k["junk"], k["fold"] = work[:, 0:512], work[:, 512:1024]
        k["tmp_dve"] = work[:, 0:2048].rearrange("p (a b) -> p a b", a=4)
        place(ctx, "posi", [P, 5], I32)
        place(ctx, "posf", [P, 5])
        place(ctx, "rope", [P, 3, ANGLE_W])
        place(ctx, "sin", [P, ANGLE_W])
        place(ctx, "cos", [P, ANGLE_W])
        place(ctx, "ss", [P, 8])
        place(ctx, "ss4", [P, TT, 2])
        place(ctx, "stat", [P, 2, 8])
        place(ctx, "small", [P, 32])
        place(ctx, "quarter", [P, 1])
        place(ctx, "one_row", [P, P])
        place(ctx, "wtok", [P, TT, E])

        one = ExitStack()
        place(one, "rows", [P, 6 * D])
        k["qk"] = k["rows"][:, 0:2 * D].rearrange("p (t d) -> p t d", t=TT)
        mix = ExitStack()
        place(mix, "c_mix", [P, 4, SSM_TILES * 32])
        place(mix, "ssm_small", [P, 14 * SSM_TILES])
        a = ExitStack()
        place(a, "ada_b", [P, 6 * D])
        place(a, "cond_wide", [P, KT, P])
        place(a, "cond", [P, 2 * KT])
        place(a, "gains", [P, 4, D])
        a.close()
        place(mix, "uT", [P, 4, S])
        place(mix, "ysT", [P, 4, S])
        place(mix, "v", [P, TT, 512])
        a = ExitStack()
        place(a, "table", [P, 2, 2, SSM_Q, S])
        place(a, "trig", [P, 2, SSM_Q, S])
        place(a, "ssm_a", [P, 2, S])
        place(a, "ssm_b", [P, 2, S])
        place(a, "ssm_r", [P, 2, 2, 2, S])
        a.close()
        k["ssm_sig"] = k["trig"][:, :, :, :].rearrange("p a b c -> p a (b c)")[:, :, 0:512]
        k["tmp_pool"] = k["trig"][:, :, :, :].rearrange("p a b c -> p (a b) c").rearrange("p (x y) c -> p x (y c)", x=4)
        a = ExitStack()
        place(a, "qkT", [P, 8, S])
        place(a, "yaT", [P, 4, S])
        place(a, "masked", [P, 2, 3 * P])
        place(a, "prob", [P, 2, 3 * P])
        place(a, "probT", [P, 2, 3 * P])
        place(a, "msig", [P, 2, 512])
        place(a, "catT", [P, KT, S])
        k["qT"], k["kT"] = k["qkT"][:, 0:4, :], k["qkT"][:, 4:8, :]
        a.close()
        mix.close()
        first = dict(k)
        moe = ExitStack()
        ring.append(place(moe, "slot3", [P, SLOT]))
        place(moe, "tie", [P, E, E])
        place(moe, "b_down", [P, D])
        place(moe, "rank_eq", [P, E, E])
        place(moe, "rank_gt", [P, E, E])
        for name in ("logits", "rank", "wexp"):
            place(moe, name, [P, TT, E])
        place(moe, "wT", [P, S])
        moe.close()
        one.close()
        k["ring"] = first["ring"] = ring
        first.update({n: k[n] for n in ("tie", "b_down", "rank_eq", "rank_gt", "logits", "rank", "wexp", "wT")})
        hy = ExitStack()
        second = dict(k)

        def place2(stack, target, name, shape):
            target[name] = stack.enter_context(nc.sbuf_tensor(f"{name}_{'h' if target is second else 'n'}", shape, F32))

        for name, shape in (("hya", [P, TT, HYA]), ("hyb", [P, TT, 512]), ("hyv", [P, TT, 512]), ("hyr", [P, TT, 512]), ("lora_n", [P, TT, 384]),
                            ("loraT", [P, 3, S]), ("mq", [P, TT, 768]), ("mkv", [P, TT, 1024]), ("catT", [P, KT, S]), ("tmp_pool", [P, 4, 128])):
            place2(hy, second, name, shape)
        a = ExitStack()
        for name, shape in (("gqT", [P, 2, S]), ("gkT", [P, 2, S]), ("gaT", [P, S]), ("gz", [P, 2, S]), ("gla", [P, 2, S]), ("gb", [P, 2, S]), ("gd", [P, 2, S]),
                            ("ge", [P, 3, 2, S]), ("gdec", [P, 2, NCH]), ("kdecT", [P, 2, S]), ("qintraT", [P, 2, S]), ("qinterT", [P, 2, S]),
                            ("kdec", [P, TT, 2, P]), ("AT", [P, 2, 4, P]), ("state", [P, 2, 3, P])):
            place2(a, second, name, shape)
        second["rsig"], second["rsig2"] = k["xn"][:, :, 0:512], k["xn"][:, :, 512:1024]
        a.close()
        a = ExitStack()
        for name, shape in (("mk", [P, TT, 768]), ("mqT", [P, MLA_H, S]), ("mkT", [P, MLA_H, S]), ("masked", [P, 2, 3 * P]), ("prob", [P, 2, 3 * P]), ("probT", [P, 2, 3 * P])):
            place2(a, second, name, shape)
        a.close()
        hy.close()
        third = dict(k)
        ns = ExitStack()
        for name, shape in (("nq", [P, TT, 1024]), ("kcv", [P, TT, 512]), ("nkv", [P, TT, 512]), ("nwv", [P, TT, 512]), ("kd", [P, TT, 2, NSA_G, 2, HD]),
                            ("tmp_pool", [P, 4, 512]), ("nqT", [P, 8, S]), ("ksT", [P, 4, S]), ("kwT", [P, 4, S]), ("gates", [P, TT, 48]),
                            ("vcmp", [P, NSA_G, HD]), ("cp", [P, TT, NSA_H, N_CMP]), ("cs", [P, TT, NSA_H]), ("masked", [P, 2, 3 * P])):
            place2(ns, third, name, shape)
        a = ExitStack()
        for name, shape in (("kcvT", [P, 4, S]), ("blk", [P, CMP_LEN, NSA_G, N_CMP]), ("hidT", [P, 2, NSA_G * N_CMP]), ("kcr", [P, S]), ("kcmp", [P, NSA_G, 2, HD]),
                            ("kcmpT", [P, NSA_G, N_CMP])):
            place2(a, third, name, shape)
        a.close()
        a = ExitStack()
        for name, shape in (("catT", [P, KT, S]), ("prob", [P, 2, 3 * P]), ("probT", [P, 2, 3 * P])):
            place2(a, third, name, shape)
        a.close()
        ns.close()
        last = ExitStack()
        k["final_row"] = last.enter_context(nc.sbuf_tensor("final_row", [P, D], F32))
        last.close()

        block = ctx.enter_context(nc.Block())
        f = first
        gain = {}
        lo = PARAM_AT["ffn_g"][0]
        for q in range(4):
            gain["ffn", q] = k["params"][:, lo + q * KT:lo + (q + 1) * KT]
        lo = PARAM_AT["mix_g"][0]
        for q in range(2):
            gain["mix", q] = k["params"][:, lo + q * KT:lo + (q + 1) * KT]
        moba, mla, nsa = moba_units(f), mla_units(second), nsa_units(third)
        qk_jobs = [[(k["xn"][:, t, (2 * b + c) * P:(2 * b + c + 1) * P], P, (2 * c + t) * P) for c in range(2) for t in range(TT)] for b in range(4)]
        qk_reads = [(f["qkT"][:, 2 * b:2 * b + 2, :].rearrange("p a b -> p (a b)"), P, 2 * S) for b in range(4)]
        qkv_dst = [f["qk"][:, :, 0:512], f["qk"][:, :, 512:1024], f["v"]]
        mix_bank = lambda half, t: k["ps"][4 + 2 * half + t][:, :]
        moe_rows = lambda half, t: k["xn"][:, t, half * 512:(half + 1) * 512]

        @block.sync
        def _(sp):
            def stream(items):
                for it in items:
                    if it.free is not None:
                        sp.wait_ge(*it.free)
                    name, i = it.src
                    sp.dma_start(k["ring"][it.slot][:, 0:it.width], src[name][i, :, 0:it.width]).then_inc(k["landed"][it.slot], 16)

            stream(before)
            moe_sync(k, sp)
            stream(after)
            sp.wait_ge(k["sig"]["xn_ready"], 2 * 8 + 2)
            sp.dma_start(out.rearrange("o (t p) d -> p (o t) d", p=P), k["xn"][:, :, :]).then_inc(k["sig"]["stored"], 16)
            sp.wait_ge(k["sig"]["stored"], 16)

        @block.scalar
        def _(act):
            s = k["sig"]
            for each in (k, f, second, third):
                each["acs"] = Steps(act, s["step_act"]) if each is k else k["acs"]
            act.dma_start(k["params"][:, :], src["params"]).then_inc(s["small_loaded"], 16)
            act.dma_start(k["consts"][:, :], src["consts"]).then_inc(s["small_loaded"], 16)
            act.dma_start(k["posi"][:, :], src["pos"]).then_inc(s["small_loaded"], 16)
            act.dma_start(k["x"][:, :, :], src["x"].rearrange("o (t p) d -> p (o t) d", p=P)).then_inc(s["small_loaded"], 16)
            act.dma_start(f["ada_b"][0:1, :], src["ada_b"]).then_inc(s["rows_loaded"], 16)
            act.dma_start(f["gains"][:, :, :], src["gains"]).then_inc(s["rows_loaded"], 16)
            ada_scalar(f, act)
            angles_scalar(f, act)
            ssm_prep_scalar(f, act)
            norm_scalar(f, act, 0, None)
            end_phase(k, act, 1)
            act.wait_ge(s["proj_ready"], 1)
            act.activation(f["uT"][:, 0:2, :].rearrange("p a b -> p (a b)"), k["ps"][0][:, :], ACT.Copy).then_inc(s["proj_act"], 1)
            project_read(f, act, 0, 2, qkv_dst)
            ssm_scalar(f, act)
            end_phase(k, act, 2)
            turn_read(f, act, qk_reads, 0, 0)
            attend_scalar(f, act, moba, HD ** -0.5)
            merge_scalar(f, act)
            post_norm_scalar(f, act, s["out_ready"], (1, 2, 3, 4), mix_bank, s["mix_square"], 0)
            end_phase(k, act, 3)
            act.dma_start(f["tie"][:, :, :], src["tie"]).then_inc(s["tie_loaded"], 16)
            act.dma_start(f["b_down"][0:E, :], src["b_down"]).then_inc(s["tie_loaded"], 16)
            norm_scalar(f, act, 1, None)
            router_scalar(f, act)
            moe_scalar(f, act)
            act.wait_ge(s["y_drained"], 4 * E + 4)
            post_norm_scalar(f, act, None, None, moe_rows, s["moe_square"], 1)
            end_phase(k, act, 4)
            norm_scalar(k, act, 2, gain["ffn", 0])
            ffn_scalar(k, act, 0)
            norm_scalar(k, act, 3, gain["mix", 0])
            project_read(second, act, 0, 8, [second["hya"], second["hyb"], second["hyv"], second["hyr"]])
            lora_norm_scalar(second, act)
            turn_read(second, act, hy_turn_jobs(second)[1], 4, 0)
            lora_read(second, act, 0)
            gla_scalar(second, act)
            turn_read(second, act, gla_turn_jobs(second)[1], 10, 0)
            end_phase(k, act, 5)
            turn_read(second, act, mla_turn_jobs(second)[1], 12, 0)
            attend_scalar(second, act, mla, MLA_QK ** -0.5)
            norm_scalar(k, act, 4, gain["ffn", 1])
            ffn_scalar(k, act, 1)
            norm_scalar(k, act, 5, gain["ffn", 2])
            ffn_scalar(k, act, 2)
            norm_scalar(k, act, 6, gain["mix", 1])
            end_phase(k, act, 6)
            project_read(third, act, 0, 16, [third["nq"][:, :, 0:512], third["nq"][:, :, 512:1024], third["kcv"], third["nkv"], third["nwv"]])
            turn_read(third, act, nsa_turn_jobs(third)[1], 20, 0)
            cmp_scalar(third, act)
            end_phase(k, act, 7)
            attend_scalar(third, act, nsa, HD ** -0.5)
            norm_scalar(k, act, 7, gain["ffn", 3])
            ffn_scalar(k, act, 3)
            end_phase(k, act, 8)
            act.dma_start(k["final_row"][:, :], src["final_norm"]).then_inc(s["final_loaded"], 16)
            act.wait_ge(s["x_ready"], 9)
            for t in range(TT):
                act.activation(k["xn"][:, t, :], k["x"][:, t, :], ACT.Square, accum_out=k["ss"][:, t:t + 1]).then_inc(s["sumsq"], 1)
            act.wait_ge(s["meansq"], 9)
            act.activation(k["ss"][:, 2:4], k["ss"][:, 2:4], ACT.Sqrt).then_inc(s["root"], 1)

        @block.vector
        def _(dve):
            s = k["sig"]
            for each in (k, f, second, third):
                each["vs"] = Steps(dve, s["step_dve"]) if each is k else k["vs"]
            ada_vector(f, dve)
            angles_vector(f, dve)
            ssm_prep_vector(f, dve)
            dve.drain().then_inc(s["ssm_prep_dve"], 1)
            norm_vector(f, dve, 0, None, (f["rows"][:, D:2 * D], f["rows"][:, 0:D]))
            end_phase(k, dve, 1)
            dve.wait_ge(s["proj_ready"], 2)
            dve.tensor_copy(f["uT"][:, 2:4, :].rearrange("p a b -> p (a b)"), k["ps"][1][:, :]).then_inc(s["proj_dve"], 1)
            project_read(f, dve, 1, 2, qkv_dst)
            dve.wait_ge(s["proj_dve"], 4)
            rope_rotate(dve, k["vs"], k["xn"][:, 1, :].rearrange("p (h x) -> p h x", h=16), f["qk"][:, 1, :].rearrange("p (h x) -> p h x", h=16), 16, 32,
                        angle(k, k["cos"], "a1"), angle(k, k["sin"], "a1"), k["tmp_dve"])
            dve.drain().then_inc(s["rope_dve"], 1)
            ssm_vector(f, dve)
            ssm_gate_vector(f, dve)
            end_phase(k, dve, 2)
            turn_read(f, dve, qk_reads, 0, 1)
            attend_vector(f, dve, moba, HD ** -0.5)
            merge_vector(f, dve)
            post_norm_vector(f, dve, mix_bank, s["mix_square"], 0, 2)
            end_phase(k, dve, 3)
            dve.drain().then_inc(s["arena_free"], 1)
            norm_vector(f, dve, 1, None, (f["rows"][:, 4 * D:5 * D], f["rows"][:, 3 * D:4 * D]))
            router_vector(f, dve)
            moe_vector(f, dve)
            post_norm_vector(f, dve, moe_rows, s["moe_square"], 1, 5)
            end_phase(k, dve, 4)
            norm_vector(k, dve, 2, gain["ffn", 0])
            ffn_vector(k, dve, 0)
            norm_vector(k, dve, 3, gain["mix", 0])
            project_read(second, dve, 1, 8, [second["hya"], second["hyb"], second["hyv"], second["hyr"]])
            lora_norm_vector(second, dve)
            turn_read(second, dve, hy_turn_jobs(second)[1], 4, 1)
            lora_read(second, dve, 1)
            gla_vector(second, dve)
            turn_read(second, dve, gla_turn_jobs(second)[1], 10, 1)
            end_phase(k, dve, 5)
            mla_rows(second, dve, k["vs"], 1, s["mla_dve"], k["tmp_dve"])
            turn_read(second, dve, mla_turn_jobs(second)[1], 12, 1)
            attend_vector(second, dve, mla, MLA_QK ** -0.5)
            add_out_vector(k, dve, 4)
            norm_vector(k, dve, 4, gain["ffn", 1])
            ffn_vector(k, dve, 1)
            norm_vector(k, dve, 5, gain["ffn", 2])
            ffn_vector(k, dve, 2)
            norm_vector(k, dve, 6, gain["mix", 1])
            end_phase(k, dve, 6)
            project_read(third, dve, 1, 16, [third["nq"][:, :, 0:512], third["nq"][:, :, 512:1024], third["kcv"], third["nkv"], third["nwv"]])
            dve.wait_ge(s["proj_dve"], 13)
            nsa_rows(third, dve, k["vs"], 1, s["nsa_dve"], k["tmp_dve"])
            turn_read(third, dve, nsa_turn_jobs(third)[1], 20, 1)
            cmp_vector(third, dve)
            end_phase(k, dve, 7)
            attend_vector(third, dve, nsa, HD ** -0.5)
            add_out_vector(k, dve, 8)
            norm_vector(k, dve, 7, gain["ffn", 3])
            ffn_vector(k, dve, 3)
            end_phase(k, dve, 8)
            dve.wait_ge(s["sumsq"], 18)
            dve.tensor_scalar(k["ss"][:, 2:4], k["ss"][:, 0:2], 1.0 / D, EPS, ALU.mult, ALU.add).then_inc(s["meansq"], 1)
            dve.wait_ge(s["root"], 9)
            k["vs"].mark(dve.reciprocal(k["ss"][:, 4:6], k["ss"][:, 2:4]))
            k["vs"].wait()
            dve.wait_ge(s["final_loaded"], 16)
            for t in range(TT):
                dve.scalar_tensor_tensor(out=k["xn"][:, t, :], in0=k["x"][:, t, :], scalar=k["ss"][:, 4 + t:5 + t], in1=k["final_row"][:, :], op0=ALU.mult, op1=ALU.mult)\
                   .then_inc(s["xn_ready"], 1)

        @block.tensor
        def _(pe):
            s = k["sig"]
            pe.drain().then_inc(s["down_done"], 2)
            ada_tensor(f, pe)
            norm_tensor(k, pe, 0)
            end_phase(k, pe, 1)
            u_tensor(f, pe)
            project_tensor(f, pe, ["w_qkv0", "w_qkv1", "w_qkv2"], 2, [512] * 3, k["hT"], KT, 0)
            ssm_tensor(f, pe)
            pe.wait_ge(s["rope_dve"], 1)
            pe.wait_ge(s["rope_pool"], 1)
            end_phase(k, pe, 2)
            turn_tensor(f, pe, qk_jobs, 0)
            turned(k, pe, 4)
            attend_tensor(f, pe, moba)
            merge_tensor(f, pe)
            pe.wait_ge(s["merged"], KT)
            out_tensor(f, pe, ["w_out0", "w_out1"], 0, f["catT"])
            end_phase(k, pe, 3)
            norm_tensor(k, pe, 1)
            router_tensor(f, pe)
            moe_tensor(f, pe)
            end_phase(k, pe, 4)
            norm_tensor(k, pe, 2)
            ffn_tensor(k, pe, 0)
            norm_tensor(k, pe, 3)
            project_tensor(second, pe, [f"hy{j}" for j in range(4)], 8, [HYA, 512, 512, 512], k["hT"], KT, 8)
            pe.wait_ge(s["lora_n"], 4)
            pe.wait_ge(s["proj_act"], 8)
            pe.wait_ge(s["proj_dve"], 8)
            turn_tensor(second, pe, hy_turn_jobs(second)[0], 4)
            turned(k, pe, 10)
            lora_tensor(second, pe)
            pe.wait_ge(s["lora_act"], 4)
            pe.wait_ge(s["lora_dve"], 4)
            gla_tensor(second, pe)
            pe.wait_ge(s["gla_out"], 2)
            turn_tensor(second, pe, gla_turn_jobs(second)[0], 10)
            end_phase(k, pe, 5)
            pe.wait_ge(s["mla_dve"], 1)
            pe.wait_ge(s["mla_pool"], 1)
            turn_tensor(second, pe, mla_turn_jobs(second)[0], 12)
            turned(k, pe, 20)
            attend_tensor(second, pe, mla)
            pe.wait_ge(s["o_copied"], 16)
            out_tensor(second, pe, ["hy_out0", "hy_out1"], 4, second["catT"])
            norm_tensor(k, pe, 4)
            ffn_tensor(k, pe, 1)
            norm_tensor(k, pe, 5)
            ffn_tensor(k, pe, 2)
            norm_tensor(k, pe, 6)
            end_phase(k, pe, 6)
            project_tensor(third, pe, [f"nsa{j}" for j in range(5)], 16, [512] * 5, k["hT"], KT, 16)
            pe.wait_ge(s["nsa_dve"], 1)
            pe.wait_ge(s["nsa_pool"], 1)
            pe.wait_ge(s["proj_act"], 13)
            pe.wait_ge(s["proj_dve"], 13)
            turn_tensor(third, pe, nsa_turn_jobs(third)[0], 20)
            turned(k, pe, 30)
            cmp_tensor(third, pe)
            pe.wait_ge(s["cmp_p"], 2)
            end_phase(k, pe, 7)
            attend_tensor(third, pe, nsa)
            pe.wait_ge(s["o_copied"], 32)
            out_tensor(third, pe, ["nsa_out0", "nsa_out1"], 8, third["catT"])
            norm_tensor(k, pe, 7)
            ffn_tensor(k, pe, 3)
            end_phase(k, pe, 8)

        @block.gpsimd
        def _(pool):
            s = k["sig"]
            for each in (k, f, second, third):
                each["pos"] = Steps(pool, s["step_pool"]) if each is k else k["pos"]
            end_phase(k, pool, 1)
            ssm_tables_pool(f, pool)
            pool.wait_ge(s["trig_done"], 8)
            pool.wait_ge(s["proj_act"], 4)
            rope_rotate(pool, k["pos"], k["xn"][:, 0, :].rearrange("p (h x) -> p h x", h=16), f["qk"][:, 0, :].rearrange("p (h x) -> p h x", h=16), 16, 32,
                        angle(k, k["cos"], "a0"), angle(k, k["sin"], "a0"), f["tmp_pool"])
            pool.drain().then_inc(s["rope_pool"], 1)
            end_phase(k, pool, 2)
            end_phase(k, pool, 3)
            end_phase(k, pool, 4)
            end_phase(k, pool, 5)
            mla_rows(second, pool, k["pos"], 0, s["mla_pool"], second["tmp_pool"])
            end_phase(k, pool, 6)
            pool.wait_ge(s["proj_act"], 13)
            nsa_rows(third, pool, k["pos"], 0, s["nsa_pool"], third["tmp_pool"])
            end_phase(k, pool, 7)
            end_phase(k, pool, 8)




def by_tile(w):
    return w.reshape(w.shape[0] // P, P, w.shape[1]).transpose(1, 0, 2)


def flat(*parts):
    return np.concatenate([p.reshape(P, -1) for p in parts], axis=1)


def columns(v):
    v = v.reshape(-1, v.shape[-1] // P, P)
    return v.transpose(2, 0, 1).reshape(P, -1)


def on_rows(a, rows=P):
    out = np.zeros((P,) + a.shape[1:], a.dtype)
    out[:a.shape[0]] = a
    return out


def ffn_steps(gate, up, down_):
    n = gate.shape[1] // STEP_COLS
    out = np.empty((n, P, STEP_WIDTH), gate.dtype)
    for j, w in enumerate((gate, up)):
        out[:, :, j * STEP_GATE:(j + 1) * STEP_GATE] = w.reshape(KT, P, n, STEP_COLS).transpose(2, 1, 0, 3).reshape(n, P, -1)
    out[:, :, 2 * STEP_GATE:] = down_.reshape(n, STEP_TILES, P, D).transpose(0, 2, 1, 3).reshape(n, P, -1)
    return out


def column_items(w, cols):
    return np.stack([flat(by_tile(w[:, a:a + cols])) for a in range(0, w.shape[1], cols)])


def constants():
    c = {}
    i, j = np.arange(P)[:, None], np.arange(P)[None, :]
    c["ident"] = (i == j).astype(np.float32)
    tri = np.where(j <= i, 0.0, NEG).astype(np.float32)
    c["causal"] = np.concatenate([tri, np.zeros((P, P), np.float32), tri], axis=1)
    c["inv_freq_64"] = np.broadcast_to(np.power(np.float32(10000.0), -np.arange(32, dtype=np.float32) / np.float32(32)), (P, 32))
    c["inv_freq_32"] = np.broadcast_to(np.power(np.float32(10000.0), -np.arange(16, dtype=np.float32) / np.float32(16)), (P, 16))
    c["time"] = np.broadcast_to(np.arange(S, dtype=np.float32), (P, S))
    c["gla_mask"] = ((i <= j) & (i // CHUNK == j // CHUNK)).astype(np.float32)
    c["gla_keep"] = np.broadcast_to((np.arange(S) % CHUNK != 0).astype(np.float32), (P, S))
    tok = np.arange(TT)[None, :, None] * P + np.arange(P)[:, None, None]
    seen = (np.arange(N_CMP) * CMP_STRIDE + CMP_LEN - 1)[None, None, :] <= tok
    c["cmp_add"] = np.where(seen, 0.0, NEG).reshape(P, -1)
    c["cmp_one"] = seen.astype(np.float32).reshape(P, -1)
    packed = np.concatenate([c[n].astype(np.float32) for n, _ in CONSTS], axis=1)
    e = np.arange(E)
    tie = np.broadcast_to((e[None, :] < e[:, None]).astype(np.float32), (P, E, E))
    return np.ascontiguousarray(packed), np.ascontiguousarray(tie)


def layout(a):
    arr = {}
    w = {n: v[0] for n, v in a.items() if v.ndim > 1}
    states = lambda v: v.reshape(SSM_TILES, P).T

    def block_c(c):
        out = np.zeros((2, SSM_N, SSM_TILES, 2, SSM_C), c.dtype)
        cc = c.reshape(SSM_TILES, 2, SSM_C, SSM_N)
        for g in range(2):
            out[g, :, :, g, :] = cc[:, g].transpose(2, 0, 1)
        return out.reshape(P, -1)

    def block_b(b):
        out = np.zeros((4, 2, SSM_C, 4, 4, 2, SSM_N), b.dtype)
        bb = b.reshape(4, 4, 2, SSM_N, SSM_C)
        for jj in range(4):
            for g in range(2):
                out[jj, g, :, :, jj, g, :] = bb[:, jj, g].transpose(2, 0, 1)
        return out.reshape(P, -1)

    b_gu = np.stack([w["b_gate"].reshape(E, KT, P), w["b_up"].reshape(E, KT, P)], axis=2)
    params = {
        "c": columns(a["c"]), "lam_re": states(w["ssm_lam_re"]), "lam_im": states(w["ssm_lam_im"]),
        "log_dt": states(np.repeat(w["ssm_log_dt"], SSM_N)), "d_skip": columns(a["ssm_d"]),
        "router_b": np.broadcast_to(w["router_b"], (P, E)), "ffn_g": columns(a["ffn_norm_2"]), "mix_g": columns(a["mix_norm_2"]),
        "q_norm": columns(a["mla_q_norm_2"]), "kv_norm": columns(a["mla_kv_norm_2"]), "b_a": columns(a["gla_b_a_2"]),
        "out_norm": np.broadcast_to(w["gla_out_norm_2"], (P, GLA_DV)), "w_a2": on_rows(w["gla_w_a2_2"]),
        "pos_kv": np.concatenate([w["nsa_pos_k_2"].T, w["nsa_pos_v_2"].T]), "ct_re": block_c(w["ssm_c_re"]), "ct_im": block_c(w["ssm_c_im"]),
        "router_w": flat(by_tile(w["router_w"])), "b_gu": b_gu.transpose(3, 0, 1, 2).reshape(P, -1)}
    arr["params"] = np.concatenate([params[n] for n, _ in PARAMS], axis=1)
    arr["consts"], arr["tie"] = constants()
    p1, p2 = a["positions"][0], a["positions_2"][0]
    ends = np.zeros(P, p2.dtype)
    ends[:N_CMP] = p2[np.arange(N_CMP) * CMP_STRIDE + CMP_LEN - 1]
    arr["pos"] = np.stack([p1[:P], p1[P:], p2[:P], p2[P:], ends], axis=1).astype(np.int32)
    arr["x"] = a["x"]
    arr["ada_b"] = a["ada_b"]
    arr["gains"] = np.broadcast_to(np.stack([w[n] for n in ("mix_pre_g", "mix_post_g", "ffn_pre_g", "ffn_post_g")]), (P, 4, D))
    arr["b_down"] = w["b_down"]
    arr["final_norm"] = np.broadcast_to(a["final_norm_2"], (P, D))
    arr["ada"] = column_items(w["ada_w"], ADA_COLS)
    arr["w_in"] = column_items(w["w_in"][:, 0:2048], 512)
    arr["ssm_b"] = flat(block_b(w["ssm_b_re"]), block_b(w["ssm_b_im"]))[None]
    arr["w_glu"] = flat(by_tile(w["ssm_w_glu"]))[None]
    gs, ga = w["w_in"][:, 2048:3072], w["w_in"][:, 3072:4096]
    arr["merge"] = np.stack([flat(by_tile(gs[:, m:m + 256]), by_tile(ga[:, m:m + 256]), by_tile(w["w_ssm_branch"][:, m:m + 256]),
                                  by_tile(w["w_attn_branch"][:, m:m + 256])) for m in range(0, D, 256)])
    arr["w_out"] = column_items(w["w_out"], 512)
    arr["moe"] = np.concatenate([ffn_steps(w["w_gate"][e], w["w_up"][e], w["w_down"][e]) for e in range(E)])
    g2, u2, d2 = (a[n].reshape(4, *a[n].shape[2:]) for n in ("ffn_w_gate_2", "ffn_w_up_2", "ffn_w_down_2"))
    arr["ffn"] = np.concatenate([ffn_steps(g2[q], u2[q], d2[q]) for q in range(4)])
    hy = w["hy_w_in_2"]
    cut = np.cumsum([0, Q_LORA, KV_LORA, MLA_ROPE, 256, 256, 512, GLA_RANK, 512])
    part = [hy[:, cut[i]:cut[i + 1]] for i in range(8)]
    items = [np.concatenate([part[0], part[1], part[2], part[6]], axis=1), np.concatenate([part[3], part[4]], axis=1), part[5], part[7]]
    arr["hy_in"] = np.zeros((4, P, 4096), hy.dtype)
    for j, it in enumerate(items):
        arr["hy_in"][j, :, :it.shape[1] * KT] = flat(by_tile(it))
    arr["lora"] = flat(by_tile(w["mla_w_uq_2"]), w["mla_w_ukv_2"])[None]
    arr["hy_out"] = column_items(w["hy_w_out_2"], 512)
    ns = w["nsa_w_in_2"]
    cut = np.cumsum([0, 1024] + [256] * 6 + [48])
    part = [ns[:, cut[i]:cut[i + 1]] for i in range(8)]
    kcv = np.stack([part[1].reshape(D, NSA_G, HD), part[2].reshape(D, NSA_G, HD)], axis=2).reshape(D, 512)
    arr["nsa_in"] = np.stack([flat(by_tile(q)) for q in (part[0][:, 0:512], part[0][:, 512:1024], kcv,
                                                         np.concatenate([part[3], part[4]], axis=1), np.concatenate([part[5], part[6]], axis=1))])
    w1 = np.concatenate([w[n].reshape(CMP_LEN, HD, CMP_HID).transpose(1, 0, 2).reshape(HD, -1) for n in ("nsa_ck_w1_2", "nsa_cv_w1_2")])
    arr["nsa_c"] = flat(w1, by_tile(part[7]), w["nsa_ck_w2_2"], w["nsa_cv_w2_2"])[None]
    arr["nsa_out"] = column_items(w["nsa_w_out_2"], 512)
    return {n: np.ascontiguousarray(v) for n, v in arr.items()}


def kernel(**inputs):
    import concourse.bacc as bacc
    from concourse.bass_utils import run_bass_kernel_spmd

    arrays = layout({n: np.asarray(v) for n, v in inputs.items()})
    nc = bacc.Bacc("TRN2", target_bir_lowering=False, num_devices=1)
    src = {n: nc.dram_tensor(f"in_{n}", v.shape, mybir.dt.from_np(v.dtype), kind="ExternalInput").ap() for n, v in arrays.items()}
    out = nc.dram_tensor("out", (1, S, D), F32, kind="ExternalOutput").ap()
    program(nc, src, out)
    result = run_bass_kernel_spmd(nc, [{f"in_{n}": v for n, v in arrays.items()}], core_ids=[0])
    return result.results[0]["out"]
```

```python
from contextlib import ExitStack

import numpy as np

import concourse.bass as bass
from concourse import mybir

F32 = mybir.dt.float32
F32R = mybir.dt.float32r
I32 = mybir.dt.int32
ALU = mybir.AluOpType
ACT = mybir.ActivationFunctionType
AX_X = mybir.AxisListType.X

P = 128
S = 256
TT = S // P
D = 1024
KT = D // P
EPS = 1e-6
NEG = -1e30
TINY = 1e-30

E = 32
TOP_K = 4
DFF = 1024
DFF2 = 2816
STEP_COLS = 256
STEP_TILES = STEP_COLS // P
STEP_GATE = KT * STEP_COLS
STEP_WIDTH = 2 * STEP_GATE + STEP_TILES * D
MOE_STEPS = DFF // STEP_COLS
MOE_SLOTS = P
PIECE = STEP_GATE
FFN_STEPS = DFF2 // STEP_COLS
ALPHA = 1.702
LIMIT = 7.0

SSM_G, SSM_C, SSM_N = 32, 16, 64
SSM_W = SSM_G * SSM_C
SSM_TILES = SSM_G * SSM_N // P
SSM_Q = 4

HEADS, HD = 8, 64
MLA_H, MLA_NOPE, MLA_ROPE, MLA_V = 8, 64, 32, 64
MLA_QK = MLA_NOPE + MLA_ROPE
Q_LORA, KV_LORA = 256, 128
GLA_H, GLA_DK, GLA_DV, GLA_RANK, GLA_TAU, CHUNK = 4, 64, 128, 16, 16.0, 64
NCH = S // CHUNK
NSA_H, NSA_G = 16, 4
CMP_LEN, CMP_STRIDE, CMP_HID = 32, 16, 128
N_CMP = (S - CMP_LEN) // CMP_STRIDE + 1

SLOT = STEP_WIDTH
ROUND = 12582912.0
ROUND_12 = 3072.0
TWO_PI = 2 * np.pi
PI_HI = 6.28125
PI_MID = float(np.float32(np.round((TWO_PI - PI_HI) * 2 ** 21) / 2 ** 21))
PI_LO = float(np.float32(TWO_PI - PI_HI - PI_MID))
SIN_MAX = 3.1415925
TURN = 6.283185

PARAMS = [("lam_re", SSM_TILES), ("lam_im", SSM_TILES), ("log_dt", SSM_TILES), ("d_skip", SSM_W // P),
          ("router_b", E), ("ffn_g", 4 * KT), ("mix_g", 2 * KT), ("q_norm", Q_LORA // P), ("kv_norm", 1),
          ("b_a", 2), ("out_norm", GLA_DV), ("w_a2", GLA_H * GLA_DK), ("pos_kv", CMP_LEN),
          ("ct_re", SSM_TILES * 32), ("ct_im", SSM_TILES * 32), ("router_w", KT * E), ("b_gu", E * 16)]
CONSTS = [("ident", P), ("causal", 3 * P), ("before", P), ("inv_freq_64", 32), ("inv_freq_32", 16), ("time", S),
          ("gla_mask", P), ("gla_keep", S), ("cmp_add", TT * N_CMP), ("cmp_one", TT * N_CMP)]
ANGLES = [("a0", 0, "inv_freq_64", 32), ("a1", 1, "inv_freq_64", 32), ("b0", 2, "inv_freq_64", 32),
          ("b1", 3, "inv_freq_64", 32), ("m0", 2, "inv_freq_32", 16), ("m1", 3, "inv_freq_32", 16),
          ("e", 4, "inv_freq_64", 32)]


def offsets(table):
    at, out = 0, {}
    for name, width in table:
        out[name] = (at, at + width)
        at += width
    return out, at


PARAM_AT, PARAM_W = offsets(PARAMS)
CONST_AT, CONST_W = offsets(CONSTS)
ANGLE_AT, ANGLE_W = offsets([(n, w) for n, _, _, w in ANGLES])

ADA_COLS = 768
ADA_UNITS = 16
ADA_N = ADA_COLS // 2
HYA = Q_LORA + KV_LORA + MLA_ROPE + GLA_RANK

SIGNALS = """small_loaded rows_loaded step_dve step_act step_pool phase_end
 cond_loaded cond_sig cond_ready ada_ready ada_act ada_dve
 sumsq meansq root xn_ready xT_ready hT_act hT_dve x_ready
 proj_ready proj_act proj_dve rope_dve rope_pool
 ssm_prep_act ssm_prep_dve trig_arg trig_arg_pool trig_done table_free bu_ready bu_read rotated ssm_y_ready gelu_in gelu_done glu_ready glu_sig
 heads_T heads_T_act heads_T_dve score_ready masked negmax exp_done p_norm pT_ready pT_copied o_ready o_copied
 merge_ready merge_sig merged
 mix_square moe_square post_mean post_root
 router_ready router_exp router_in weights_ready weights_T weights_T_done y_init y_kept tie_loaded chosen places_ready flag_ready
 moe_ones moe_weighed moe_xe moe_xe_read moe_wT moe_wT_read moe_gu moe_gu_read moe_gate moe_sig moe_step moe_act moe_down moe_y_read moe_share moe_added moe_tensor_done moe_done moe_w_hi moe_w_lo moe_low
 gu_ready gu_drained sig_ready act_ready down_done ffn_w_hi ffn_w_lo ffn_down_hi ffn_down_lo actT_ready actT_hi
 angles_ready lora_ready lora_act lora_dve lora_sq lora_mean lora_root lora_n mla_dve mla_pool
 gla_pre gla_abs gla_soft gla_arg gla_exp gla_ready gla_kdec gla_kdec_read gla_kv gla_state gla_A gla_A_read gla_o gla_sq gla_mean gla_root gla_silu gla_out
 nsa_dve nsa_pool gate_in gate_sig cmp_blk cmp_h cmp_sig cmp_hid cmp_kv cmp_k cmp_kT cmp_kT_read cmp_score cmp_arg cmp_exp cmp_p
 out_ready final_loaded stored arena_free""".split()


class Steps:

    def __init__(self, engine, sem):
        self.engine, self.sem, self.n = engine, sem, 0

    def mark(self, instruction):
        instruction.then_inc(self.sem, 1)
        self.n += 1
        return instruction

    def wait(self):
        self.engine.wait_ge(self.sem, self.n)


class Item:

    def __init__(self, src, width, slot, free, landed):
        self.src, self.width, self.slot, self.free, self.landed = src, width, slot, free, landed


class Unit:

    def __init__(self, kind, first, last, at, dv, gate=None, q=None, k=None, v=None, p=None, out=None):
        self.kind, self.first, self.last, self.at, self.dv, self.gate = kind, first, last, at, dv, gate
        self.q, self.k, self.v, self.p, self.out = q, k, v, p, out
        self.all = self.full = self.head = None


def plan_ring(sig):
    freed = [None] * 3
    landed = [0] * 3
    plan, order = {}, []
    turn = 0

    def item(name, src, width, done, slot=None):
        nonlocal turn
        if slot is None:
            slot = turn % 3
            turn += 1
        landed[slot] += 16
        plan[name] = Item(src, width, slot, freed[slot], landed[slot])
        order.append(plan[name])
        freed[slot] = done

    for j in range(8):
        item(f"ada{j}", ("ada", j), SLOT, (sig["ada_ready"], 2 * j + 2))
    item("w_u", ("w_in", 0), 4096, (sig["proj_ready"], 2), slot=2)
    item("ssm_b", ("ssm_b", 0), 4096, (sig["bu_ready"], SSM_TILES), slot=0)
    for j in range(3):
        item(f"w_qkv{j}", ("w_in", 1 + j), 4096, (sig["proj_ready"], 4 + 2 * j), slot=1 + j % 2)
    item("w_glu", ("w_glu", 0), 2048, (sig["glu_ready"], 2), slot=2)
    turn = 0
    for j in range(4):
        item(f"merge{j}", ("merge", j), SLOT, (sig["merge_ready"], 2 * j + 2))
    for j in range(2):
        item(f"w_out{j}", ("w_out", j), 4096, (sig["out_ready"], 2 * j + 2))
    before = list(order)
    moe_free = [freed[0], freed[1], freed[2], (sig["arena_free"], 1)]
    freed = [(sig["moe_tensor_done"], 1)] * 4
    order.clear()
    turn = 0

    def ffn(q):
        base = FFN_STEPS * q
        for m in range(FFN_STEPS):
            item(f"ffn{q}_{m}", ("ffn", q * FFN_STEPS + m), SLOT, (sig["ffn_down_lo"], base + m + 1))

    ffn(0)
    for j in range(4):
        item(f"hy{j}", ("hy_in", j), HYA * KT if j == 0 else 4096, (sig["proj_ready"], 8 + 2 * j + 2))
    item("lora", ("lora", 0), 2 * 768 + 1024, (sig["lora_ready"], 8))
    for j in range(2):
        item(f"hy_out{j}", ("hy_out", j), 4096, (sig["out_ready"], 4 + 2 * j + 2))
    ffn(1)
    ffn(2)
    for j in range(5):
        item(f"nsa{j}", ("nsa_in", j), 4096, (sig["proj_ready"], 16 + 2 * j + 2))
    item("nsa_c", ("nsa_c", 0), 4096 + 384 + 128, (sig["cmp_kv"], 2))
    for j in range(2):
        item(f"nsa_out{j}", ("nsa_out", j), 4096, (sig["out_ready"], 8 + 2 * j + 2))
    ffn(3)
    return plan, before, moe_free, order


def par(k, name, a=None, b=None):
    lo, hi = PARAM_AT[name]
    return k["params"][:, lo + (a or 0):(lo + b if b is not None else hi)]


def con(k, name, a=None, b=None):
    lo, hi = CONST_AT[name]
    return k["consts"][:, lo + (a or 0):(lo + b if b is not None else hi)]


def spread(ap, n):
    return ap.unsqueeze(1).to_broadcast([ap.shape[0], n, ap.shape[1]])


def spread_last(ap, n):
    return ap.unsqueeze(2).to_broadcast([ap.shape[0], ap.shape[1], n])


def end_phase(k, eng, n):
    eng.drain().then_inc(k["sig"]["phase_end"], 1)
    eng.wait_ge(k["sig"]["phase_end"], 4 * n)




def ada_scalar(k, act, units):
    s = k["sig"]
    for u in units:
        act.wait_ge(s["ada_ready"], u + 1)
        act.activation(k["rows"][:, u * ADA_N:(u + 1) * ADA_N], k["ps"][u % 4][:, 0:ADA_N], ACT.Copy).then_inc(s["ada_act"], 1)


def cond_scalar(k, act):
    s = k["sig"]
    act.wait_ge(s["cond_loaded"], 32)
    act.activation(k["cond"][:, 0:KT], k["cond"][:, 2 * KT:3 * KT], ACT.Sigmoid).then_inc(s["cond_sig"], 1)


def cond_vector(k, dve):
    s = k["sig"]
    dve.wait_ge(s["cond_loaded"], 32)
    dve.wait_ge(s["cond_sig"], 1)
    k["vs"].mark(dve.tensor_tensor(k["cond"][:, KT:2 * KT], k["cond"][:, 0:KT], k["cond"][:, 2 * KT:3 * KT], ALU.mult))
    k["vs"].mark(dve.memset(k["one_row"][:, :], 1.0))
    k["vs"].mark(dve.memset(k["quarter"][:, :], float(np.float32(TURN * 0.25))))
    k["vs"].wait()
    dve.tensor_copy(k["cond_wide"][:, :, :], spread_last(k["cond"][:, KT:2 * KT], P)).then_inc(s["cond_ready"], 1)
    for name, ahead in (("gu_drained", 2), ("act_ready", 1), ("moe_gu_read", 2), ("moe_act", 1), ("moe_added", 4), ("moe_low", 2)):
        dve.drain().then_inc(s[name], ahead)


def ada_vector(k, dve, units):
    s = k["sig"]
    for u in units:
        dve.wait_ge(s["ada_ready"], u + 1)
        dve.tensor_copy(k["rows"][:, u * ADA_N:(u + 1) * ADA_N], k["ps"][u % 4][:, 0:ADA_N]).then_inc(s["ada_dve"], 1)


def scale_row(k, dve, row, gain, plus):
    s = k["sig"]
    last = ((row + 1) * D - 1) // ADA_N
    dve.wait_ge(s["ada_act"], last // 2 + 1)
    dve.wait_ge(s["ada_dve"], (last + 1) // 2)
    dve.wait_ge(s["rows_loaded"], 16)
    r = k["rows"][:, row * D:(row + 1) * D]
    g = k["gains"][:, gain, :]
    if plus:
        k["vs"].mark(dve.scalar_tensor_tensor(out=r, in0=r, scalar=1.0, in1=g, op0=ALU.add, op1=ALU.mult))
    else:
        k["vs"].mark(dve.tensor_tensor(r, r, g, ALU.mult))
    k["vs"].wait()


def ada_tensor(k, pe, units):
    s = k["sig"]
    pe.wait_ge(s["cond_ready"], 1)
    pe.wait_ge(s["cond_loaded"], 32)
    for u in units:
        j, half = divmod(u, 2)
        it = k["plan"][f"ada{j}"]
        if half == 0:
            pe.wait_ge(k["landed"][it.slot], it.landed)
        if u >= 4:
            pe.wait_ge(s["ada_act"] if u % 2 == 0 else s["ada_dve"], (u - 4) // 2 + 1)
        bank = k["ps"][u % 4][:, 0:ADA_N]
        pe.matmul(bank, k["one_row"][0:1, :], k["ada_b"][0:1, u * ADA_N:(u + 1) * ADA_N], start=True, stop=False)
        for kt in range(KT):
            at = kt * ADA_COLS + half * ADA_N
            mm = pe.matmul(bank, k["cond_wide"][:, kt, :], k["ring"][it.slot][:, at:at + ADA_N], start=False, stop=kt == KT - 1)
        mm.then_inc(s["ada_ready"], 1)




def angles_vector(k, dve):
    s = k["sig"]
    vs = k["vs"]
    vs.mark(dve.tensor_copy(k["posf"][:, :], k["posi"][:, :]))
    vs.wait()
    ang, turns, tmp = k["rope"][:, 0, :], k["rope"][:, 1, :], k["rope"][:, 2, :]
    for name, col, freq, w in ANGLES:
        lo, hi = ANGLE_AT[name]
        vs.mark(dve.tensor_scalar(ang[:, lo:hi], con(k, freq), k["posf"][:, col:col + 1], None, ALU.mult))
    vs.wait()
    reduce_angle(dve, vs, ang, turns)
    fold_quarter(dve, vs, ang, tmp, turns)
    dve.drain().then_inc(s["angles_ready"], 1)


def reduce_angle(dve, vs, ang, turns):
    vs.mark(dve.tensor_scalar(turns, ang, 1.0 / TWO_PI, ROUND, ALU.mult, ALU.add))
    vs.wait()
    vs.mark(dve.tensor_scalar(turns, turns, ROUND, None, ALU.subtract))
    vs.wait()
    for part in (PI_HI, PI_MID, PI_LO):
        vs.mark(dve.scalar_tensor_tensor(out=ang, in0=turns, scalar=-part, in1=ang, op0=ALU.mult, op1=ALU.add))
        vs.wait()


def fold_quarter(dve, vs, ang, out, tmp):
    vs.mark(dve.tensor_scalar(out, ang, float(np.pi / 2), None, ALU.add))
    vs.wait()
    vs.mark(dve.tensor_scalar(tmp, out, float(np.pi), -TWO_PI, ALU.is_gt, ALU.mult))
    vs.wait()
    vs.mark(dve.tensor_tensor(out, out, tmp, ALU.add))
    vs.wait()
    vs.mark(dve.tensor_scalar(out, out, SIN_MAX, -SIN_MAX, ALU.min, ALU.max))
    vs.mark(dve.tensor_scalar(ang, ang, SIN_MAX, -SIN_MAX, ALU.min, ALU.max))
    vs.wait()


def angles_scalar(k, act):
    act.wait_ge(k["sig"]["angles_ready"], 1)
    k["acs"].mark(act.activation(k["sin"][:, :], k["rope"][:, 0, :], ACT.Sin))
    k["acs"].mark(act.activation(k["cos"][:, :], k["rope"][:, 2, :], ACT.Sin))




def norm_stats_scalar(k, act, i):
    s = k["sig"]
    for t in range(TT):
        act.wait_ge(s["x_ready"], 2 * i + t + 1)
        act.activation(k["xn"][:, t, :], k["x"][:, t, :], ACT.Square, accum_out=k["ss"][:, t:t + 1]).then_inc(s["sumsq"], 1)
    act.wait_ge(s["meansq"], i + 1)
    act.activation(k["ss"][:, 2:4], k["ss"][:, 2:4], ACT.Sqrt).then_inc(s["root"], 1)


def norm_scalar(k, act, i, gain):
    s = k["sig"]
    norm_stats_scalar(k, act, i)
    for b in range(2):
        act.wait_ge(s["xT_ready"], 4 * i + b + 1)
        for kk in range(2):
            kt = 2 * b + kk
            src = k["ps"][b][:, kk * S:(kk + 1) * S]
            if gain is None:
                ins = act.activation(k["hT"][:, kt, :], src, ACT.Copy)
            else:
                ins = act.activation(k["hT"][:, kt, :], src, ACT.Copy, scale=gain[:, kt:kt + 1])
        ins.then_inc(s["hT_act"], 1)


def norm_split_scalar(k, act, i, gain, q):
    s = k["sig"]
    norm_stats_scalar(k, act, i)
    ffn_weights_high(k, act, q, 0, 0)
    for b in range(4):
        act.wait_ge(s["xT_ready"], 4 * i + b + 1)
        for kk in range(2):
            kt = 2 * b + kk
            ins = act.activation(k["hT_hi"][:, kt, :], k["ps"][b][:, kk * S:(kk + 1) * S], ACT.Copy, scale=gain[:, kt:kt + 1])
        if b % 2 == 1:
            ins.then_inc(s["hT_act"], 1)


def norm_split_vector(k, dve, i, gain, q):
    s = k["sig"]
    norm_rows_vector(k, dve, i)
    ffn_weights_low(k, dve, q, 0, 0)
    for b in range(4):
        dve.wait_ge(s["hT_act"], 2 * i + b // 2 + 1)
        for kk in range(2):
            kt = 2 * b + kk
            ins = dve.scalar_tensor_tensor(out=k["hT_lo"][:, kt, :], in0=k["ps"][b][:, kk * S:(kk + 1) * S], scalar=gain[:, kt:kt + 1],
                                           in1=k["hT_hi"][:, kt, :].bitcast(F32), op0=ALU.mult, op1=ALU.subtract)
        if b % 2 == 1:
            ins.then_inc(s["hT_dve"], 1)


def norm_rows_vector(k, dve, i, rows=None):
    s = k["sig"]
    vs = k["vs"]
    dve.wait_ge(s["sumsq"], 2 * i + 2)
    dve.tensor_scalar(k["ss"][:, 2:4], k["ss"][:, 0:2], 1.0 / D, EPS, ALU.mult, ALU.add).then_inc(s["meansq"], 1)
    dve.wait_ge(s["root"], i + 1)
    vs.mark(dve.reciprocal(k["ss"][:, 4:6], k["ss"][:, 2:4]))
    vs.wait()
    for t in range(TT):
        r = k["ss"][:, 4 + t:5 + t]
        if rows is None:
            dve.tensor_scalar(k["xn"][:, t, :], k["x"][:, t, :], r, None, ALU.mult).then_inc(s["xn_ready"], 1)
        else:
            g, sh = rows
            vs.mark(dve.scalar_tensor_tensor(out=k["xn"][:, t, :], in0=k["x"][:, t, :], scalar=r, in1=g, op0=ALU.mult, op1=ALU.mult))
            vs.wait()
            dve.tensor_tensor(k["xn"][:, t, :], k["xn"][:, t, :], sh, ALU.add).then_inc(s["xn_ready"], 1)


def norm_vector(k, dve, i, gain, rows=None):
    s = k["sig"]
    norm_rows_vector(k, dve, i, rows)
    for b in range(2, 4):
        dve.wait_ge(s["xT_ready"], 4 * i + b + 1)
        if gain is None:
            ins = dve.tensor_copy(k["hT"][:, 2 * b:2 * b + 2, :].rearrange("p a b -> p (a b)"), k["ps"][b][:, :])
        else:
            for kk in range(2):
                kt = 2 * b + kk
                ins = dve.tensor_scalar(k["hT"][:, kt, :], k["ps"][b][:, kk * S:(kk + 1) * S], gain[:, kt:kt + 1], None, ALU.mult)
        ins.then_inc(s["hT_dve"], 1)


def norm_tensor(k, pe, i):
    s = k["sig"]
    pe.wait_ge(s["xn_ready"], 2 * i + 2)
    for b in range(4):
        for kk in range(2):
            for t in range(TT):
                kt = 2 * b + kk
                mm = pe.transpose(k["ps"][b][:, (kk * 2 + t) * P:(kk * 2 + t + 1) * P], k["xn"][:, t, kt * P:(kt + 1) * P], con(k, "ident"))
        mm.then_inc(s["xT_ready"], 1)
    pe.wait_ge(s["hT_act"], 2 * i + 2)
    pe.wait_ge(s["hT_dve"], 2 * i + 2)




def project_tensor(k, pe, names, base, ncols, src, kts, start, part=None):
    s = k["sig"]
    for m in part or range(2 * kts * len(names)):
        (j, t), kt = divmod(m // kts, 2), m % kts
        it = k["plan"][names[j]]
        n = ncols[j]
        u = base + 2 * j + t
        if kt == 0:
            pe.wait_ge(k["landed"][it.slot], it.landed)
            if u - 4 >= start:
                pe.wait_ge(s["proj_act"] if t == 0 else s["proj_dve"], (u - 4) // 2 + 1)
        mm = pe.matmul(k["ps"][u % 4][:, 0:n], src[:, kt, t * P:(t + 1) * P], k["ring"][it.slot][:, kt * n:(kt + 1) * n], start=kt == 0, stop=kt == kts - 1)
        if kt == kts - 1:
            mm.then_inc(s["proj_ready"], 1)


def project_read(k, eng, t, base, dsts, part=None):
    s = k["sig"]
    for j in part or range(len(dsts)):
        dst = dsts[j]
        u = base + 2 * j + t
        eng.wait_ge(s["proj_ready"], u + 1)
        d = dst[:, t, :]
        bank = k["ps"][u % 4][:, 0:d.shape[1]]
        if t == 0:
            eng.activation(d, bank, ACT.Copy).then_inc(s["proj_act"], 1)
        else:
            eng.tensor_copy(d, bank).then_inc(s["proj_dve"], 1)


def u_tensor(k, pe):
    s = k["sig"]
    it = k["plan"]["w_u"]
    pe.wait_ge(k["landed"][it.slot], it.landed)
    for b in range(2):
        for ff in range(2):
            f = 2 * b + ff
            for kt in range(KT):
                at = kt * SSM_W + f * P
                mm = pe.matmul(k["ps"][b][:, ff * S:(ff + 1) * S], k["ring"][it.slot][:, at:at + P], k["hT"][:, kt, :], start=kt == 0, stop=kt == KT - 1)
        mm.then_inc(s["proj_ready"], 1)


def rope_rotate(eng, steps, dst, src, nh, half, cos, sin, tmp):
    p = cos.shape[0]
    a, b, c, d = (tmp[0:p, i, 0:nh * half].rearrange("p (h x) -> p h x", h=nh) for i in range(4))
    cb, sb = spread(cos, nh), spread(sin, nh)
    lo, hi = src[:, :, 0:half], src[:, :, half:2 * half]
    steps.mark(eng.tensor_tensor(a, lo, cb, ALU.mult))
    steps.mark(eng.tensor_tensor(b, hi, sb, ALU.mult))
    steps.mark(eng.tensor_tensor(c, hi, cb, ALU.mult))
    steps.mark(eng.tensor_tensor(d, lo, sb, ALU.mult))
    steps.wait()
    steps.mark(eng.tensor_tensor(dst[:, :, 0:half], a, b, ALU.subtract))
    steps.mark(eng.tensor_tensor(dst[:, :, half:2 * half], c, d, ALU.add))
    steps.wait()


def angle(k, table, name, p=P):
    lo, hi = ANGLE_AT[name]
    return table[0:p, lo:hi]




def ssm_prep_vector(k, dve):
    s, vs, w = k["sig"], k["vs"], k["ssm_small"]
    n = SSM_TILES

    def c(i):
        return w[:, i * n:(i + 1) * n]

    dt, re, theta, r, sn, cs, thi, tlo, t0, t1, t2, t3, sarg, carg = (c(i) for i in range(14))
    dve.wait_ge(s["ssm_prep_act"], 1)
    vs.mark(dve.tensor_tensor(re, par(k, "lam_re"), dt, ALU.mult))
    vs.mark(dve.tensor_tensor(theta, par(k, "lam_im"), dt, ALU.mult))
    vs.wait()
    reduce_angle(dve, vs, theta, t0)
    vs.mark(dve.tensor_scalar(t1, theta, 1.0 / TWO_PI, None, ALU.mult))
    vs.wait()
    vs.mark(dve.tensor_scalar(thi, t1, ROUND_12, None, ALU.add))
    vs.wait()
    vs.mark(dve.tensor_scalar(thi, thi, ROUND_12, None, ALU.subtract))
    vs.wait()
    vs.mark(dve.tensor_tensor(tlo, t1, thi, ALU.subtract))
    vs.mark(dve.tensor_copy(sarg, theta))
    vs.wait()
    fold_quarter(dve, vs, sarg, carg, t0)
    dve.drain().then_inc(s["ssm_prep_dve"], 1)
    dve.wait_ge(s["ssm_prep_act"], 4)
    lr, li = par(k, "lam_re"), par(k, "lam_im")
    vs.mark(dve.tensor_tensor(t0, r, cs, ALU.mult))
    vs.mark(dve.tensor_tensor(t1, r, sn, ALU.mult))
    vs.mark(dve.tensor_tensor(t2, lr, lr, ALU.mult))
    vs.mark(dve.tensor_tensor(t3, li, li, ALU.mult))
    vs.wait()
    vs.mark(dve.tensor_scalar(t0, t0, 1.0, None, ALU.subtract))
    vs.mark(dve.tensor_tensor(t2, t2, t3, ALU.add))
    vs.wait()
    vs.mark(dve.reciprocal(t3, t2))
    vs.mark(dve.tensor_tensor(sarg, t0, lr, ALU.mult))
    vs.mark(dve.tensor_tensor(carg, t1, li, ALU.mult))
    vs.wait()
    vs.mark(dve.tensor_tensor(sarg, sarg, carg, ALU.add))
    vs.mark(dve.tensor_tensor(t1, t1, lr, ALU.mult))
    vs.mark(dve.tensor_tensor(t0, t0, li, ALU.mult))
    vs.wait()
    vs.mark(dve.tensor_tensor(t1, t1, t0, ALU.subtract))
    vs.wait()
    vs.mark(dve.tensor_tensor(sarg, sarg, t3, ALU.mult))
    vs.mark(dve.tensor_tensor(t1, t1, t3, ALU.mult))
    vs.wait()
    cr, ci = spread_last(sarg, 32), spread_last(t1, 32)
    re3 = par(k, "ct_re").rearrange("p (j c) -> p j c", j=n)
    im3 = par(k, "ct_im").rearrange("p (j c) -> p j c", j=n)
    plus, minus, neg_im, tmp = (k["c_mix"][:, i, :].rearrange("p (j c) -> p j c", j=n) for i in range(4))
    vs.mark(dve.tensor_tensor(plus, re3, cr, ALU.mult))
    vs.mark(dve.tensor_tensor(tmp, im3, ci, ALU.mult))
    vs.mark(dve.tensor_tensor(neg_im, re3, ci, ALU.mult))
    vs.mark(dve.tensor_tensor(minus, im3, cr, ALU.mult))
    vs.wait()
    vs.mark(dve.tensor_tensor(plus, plus, tmp, ALU.subtract))
    vs.mark(dve.tensor_tensor(neg_im, neg_im, minus, ALU.add))
    vs.wait()
    vs.mark(dve.tensor_scalar(minus, plus, -1.0, None, ALU.mult))
    vs.mark(dve.tensor_scalar(neg_im, neg_im, -1.0, None, ALU.mult))
    vs.wait()


def ssm_prep_scalar(k, act):
    s = k["sig"]
    n = SSM_TILES
    act.wait_ge(s["small_loaded"], 64)
    act.activation(k["ssm_small"][:, 0:n], par(k, "log_dt"), ACT.Exp).then_inc(s["ssm_prep_act"], 1)
    act.wait_ge(s["ssm_prep_dve"], 1)
    act.activation(k["ssm_small"][:, 3 * n:4 * n], k["ssm_small"][:, n:2 * n], ACT.Exp).then_inc(s["ssm_prep_act"], 1)
    act.activation(k["ssm_small"][:, 4 * n:5 * n], k["ssm_small"][:, 12 * n:13 * n], ACT.Sin).then_inc(s["ssm_prep_act"], 1)
    act.activation(k["ssm_small"][:, 5 * n:6 * n], k["ssm_small"][:, 13 * n:14 * n], ACT.Sin).then_inc(s["ssm_prep_act"], 1)


def ssm_angles(k, eng, steps, q, a, b, done):
    n = SSM_TILES
    time = spread(con(k, "time"), SSM_Q)
    hi = spread_last(k["ssm_small"][:, 6 * n + q * SSM_Q:6 * n + (q + 1) * SSM_Q], S)
    lo = spread_last(k["ssm_small"][:, 7 * n + q * SSM_Q:7 * n + (q + 1) * SSM_Q], S)
    steps.mark(eng.tensor_tensor(a, time, hi, ALU.mult))
    steps.wait()
    steps.mark(eng.tensor_scalar(b, a, ROUND, ROUND, ALU.add, ALU.subtract))
    steps.wait()
    steps.mark(eng.tensor_tensor(a, a, b, ALU.subtract))
    steps.wait()
    steps.mark(eng.tensor_tensor(b, time, lo, ALU.mult))
    steps.wait()
    steps.mark(eng.tensor_tensor(a, a, b, ALU.add))
    steps.wait()
    steps.mark(eng.tensor_scalar(b, a, ROUND, ROUND, ALU.add, ALU.subtract))
    steps.wait()
    steps.mark(eng.tensor_tensor(a, a, b, ALU.subtract))
    steps.wait()
    steps.mark(eng.tensor_scalar(b, a, 0.25, ROUND, ALU.add, ALU.add))
    steps.wait()
    steps.mark(eng.tensor_scalar(b, b, ROUND, None, ALU.subtract))
    steps.wait()
    eng.tensor_tensor(b, a, b, ALU.subtract).then_inc(done, 1)


def angles_of(k, q):
    if q == 0:
        r = k["ssm_r"][:, :, :, :, :].rearrange("p a b c d -> p a (b c) d")
        return r[:, 0, :, :], r[:, 1, :, :]
    if q == 2:
        xn = k["xn"][:, :, :].rearrange("p a (b c) -> p a b c", b=SSM_Q)
        return xn[:, 0, :, :], xn[:, 1, :, :]
    return k["trig"][:, 0, :, :], k["trig"][:, 1, :, :]


def ssm_trig_scalar(k, act, q):
    s = k["sig"]
    act.wait_ge(s["trig_arg"] if q % 2 == 0 else s["trig_arg_pool"], q // 2 + 1)
    if q >= 2:
        act.wait_ge(s["table_free"], q - 1)
    a, b = angles_of(k, q)
    act.activation(k["table"][:, q % 2, 1, :, :], a, ACT.Sin, scale=TURN).then_inc(s["trig_done"], 1)
    act.activation(k["table"][:, q % 2, 0, :, :], b, ACT.Sin, scale=TURN, bias=k["quarter"][:, 0:1]).then_inc(s["trig_done"], 1)


def ssm_vector(k, dve, tiles):
    s, vs = k["sig"], k["vs"]
    n = SSM_TILES
    A, B = k["ssm_a"], k["ssm_b"]
    for j in tiles:
        q, jj = divmod(j, SSM_Q)
        if jj == 0:
            dve.wait_ge(s["trig_done"], 2 * q + 2)
        cosb = spread(k["table"][:, q % 2, 0, jj, :], 2)
        sinb = spread(k["table"][:, q % 2, 1, jj, :], 2)
        bu = k["ps"][4 + j % 2][:, :].rearrange("p (a b) -> p a b", a=2)
        dve.wait_ge(s["bu_ready"], j + 1)
        vs.mark(dve.tensor_tensor(A[:, :, :], bu, cosb, ALU.mult))
        dve.tensor_tensor(B[:, :, :], bu, sinb, ALU.mult).then_inc(s["bu_read"], 1)
        vs.wait()
        dve.wait_ge(s["bu_read"], j + 1)
        vs.mark(dve.tensor_tensor(A[:, 0, :], A[:, 0, :], B[:, 1, :], ALU.add))
        vs.mark(dve.tensor_tensor(A[:, 1, :], A[:, 1, :], B[:, 0, :], ALU.subtract))
        vs.wait()
        decay = k["ssm_small"][:, 3 * n + j:3 * n + j + 1].to_broadcast([P, S])
        for c in range(2):
            vs.mark(dve.tensor_tensor_scan(B[:, c, :], decay, A[:, c, :], 0.0, ALU.mult, ALU.add))
        vs.wait()
        if j >= 2:
            dve.wait_ge(s["ssm_y_ready"], j - 1)
        R = k["ssm_r"][:, j % 2, :, :, :]
        vs.mark(dve.tensor_tensor(R[:, 0, :, :], B[:, :, :], cosb, ALU.mult))
        dve.tensor_tensor(R[:, 1, :, :], B[:, :, :], sinb, ALU.mult).then_inc(s["rotated"], 1)
        vs.wait()
        dve.wait_ge(s["rotated"], j + 1)
        if jj == SSM_Q - 1:
            dve.drain().then_inc(s["table_free"], 1)
        if jj == 1 and q >= 1:
            ssm_skip(k, dve, q - 1)


def ssm_skip(k, dve, q):
    s = k["sig"]
    dve.wait_ge(s["ssm_y_ready"], 4 * q + 4)
    lo = PARAM_AT["d_skip"][0]
    dve.scalar_tensor_tensor(out=k["ysT"][:, q, :], in0=k["uT"][:, q, :], scalar=k["params"][:, lo + q:lo + q + 1],
                             in1=k["ps"][6 + q % 2][:, 0:S], op0=ALU.mult, op1=ALU.add).then_inc(s["gelu_in"], 1)


def ssm_tensor(k, pe):
    s = k["sig"]
    it = k["plan"]["ssm_b"]
    pe.wait_ge(k["landed"][it.slot], it.landed)
    pe.wait_ge(s["proj_act"], 1)
    pe.wait_ge(s["proj_dve"], 1)
    pe.wait_ge(s["ssm_prep_dve"], 2)

    def inputs(j):
        if j >= 2:
            pe.wait_ge(s["bu_read"], j - 1)
        for c in range(2):
            at = (c * SSM_TILES + j) * P
            mm = pe.matmul(k["ps"][4 + j % 2][:, c * S:(c + 1) * S], k["ring"][it.slot][:, at:at + P], k["uT"][:, j // SSM_Q, :], start=True, stop=True)
        mm.then_inc(s["bu_ready"], 1)

    def outputs(j):
        q, jj = divmod(j, SSM_Q)
        if jj == 0 and q >= 2:
            pe.wait_ge(s["gelu_in"], q - 1)
        pe.wait_ge(s["rotated"], j + 1)
        out = k["ps"][6 + q % 2][32 * jj:32 * jj + 32, 0:S]
        R = k["ssm_r"][:, j % 2, :, :, :]
        for n_, (c, trig, part) in enumerate(((0, 0, 0), (1, 1, 1), (2, 0, 1), (2, 1, 0))):
            mm = pe.matmul(out, k["c_mix"][:, c, 32 * j:32 * j + 32], R[:, trig, part, :], start=n_ == 0, stop=n_ == 3)
        mm.then_inc(s["ssm_y_ready"], 1)

    inputs(0)
    for j in range(SSM_TILES):
        if j + 1 < SSM_TILES:
            inputs(j + 1)
        share = 2 * KT * 3 // SSM_TILES
        project_tensor(k, pe, ["w_qkv0", "w_qkv1", "w_qkv2"], 2, [512] * 3, k["hT"], KT, 0, range(share * j, share * (j + 1)))
        outputs(j)
    it = k["plan"]["w_glu"]
    pe.wait_ge(k["landed"][it.slot], it.landed)
    pe.wait_ge(s["gelu_done"], 4)
    for b in range(2):
        for ff in range(2):
            f = 2 * b + ff
            for kt in range(4):
                at = kt * SSM_W + f * P
                mm = pe.matmul(k["ps"][b][:, ff * S:(ff + 1) * S], k["ring"][it.slot][:, at:at + P], k["ysT"][:, kt, :], start=kt == 0, stop=kt == 3)
        mm.then_inc(s["glu_ready"], 1)


def ssm_scalar(k, act):
    s = k["sig"]
    for q in range(4):
        act.wait_ge(s["gelu_in"], q + 1)
        act.activation(k["ysT"][:, q, :], k["ysT"][:, q, :], ACT.Gelu_apprx_tanh).then_inc(s["gelu_done"], 1)
    act.wait_ge(s["rope_pool"], 1)
    for b in range(2):
        act.wait_ge(s["glu_ready"], b + 1)
        act.activation(k["ssm_sig"][:, b, :], k["ps"][b][:, :], ACT.Sigmoid).then_inc(s["glu_sig"], 1)


def ssm_gate_vector(k, dve):
    s = k["sig"]
    dve.wait_ge(s["glu_ready"], 2)
    for b in range(2):
        dve.wait_ge(s["glu_sig"], b + 1)
        y = k["ysT"][:, 2 * b:2 * b + 2, :].rearrange("p a b -> p (a b)")
        k["vs"].mark(dve.tensor_tensor(y, y, k["ssm_sig"][:, b, :], ALU.mult))
    k["vs"].wait()




def turn_tensor(k, pe, jobs, base):
    s = k["sig"]
    for j, pieces in enumerate(jobs):
        b = base + j
        if j >= 4:
            pe.wait_ge(s["heads_T_act"] if b % 2 == 0 else s["heads_T_dve"], (b - 4) // 2 + 1)
        for src, n, col in pieces:
            p = src.shape[0]
            mm = pe.transpose(k["ps"][b % 4][0:n, col:col + p], src, con(k, "ident")[0:p, 0:p])
        mm.then_inc(s["heads_T"], 1)


def turn_read(k, eng, jobs, base, parity):
    s = k["sig"]
    for j, (dst, n, cols, *gain) in enumerate(jobs):
        b = base + j
        if b % 2 != parity:
            continue
        eng.wait_ge(s["heads_T"], b + 1)
        src = k["ps"][b % 4][0:n, 0:cols]
        if parity == 0:
            eng.activation(dst, src, ACT.Copy, scale=gain[0] if gain else 1.0).then_inc(s["heads_T_act"], 1)
        elif gain:
            eng.tensor_scalar(dst, src, gain[0], None, ALU.mult).then_inc(s["heads_T_dve"], 1)
        else:
            eng.tensor_copy(dst, src).then_inc(s["heads_T_dve"], 1)


def turned(k, eng, total):
    eng.wait_ge(k["sig"]["heads_T_act"], total // 2)
    eng.wait_ge(k["sig"]["heads_T_dve"], total // 2)




def attend_units(units, base_full, base_all, base_heads):
    full, heads = base_full, base_heads
    for n, u in enumerate(units):
        u.all = base_all + n
        u.full = None
        if u.kind == "full":
            u.full = full
            full += 1
        u.head = heads
        if u.last:
            heads += 1
    return units


def attend_tensor(k, pe, units):
    s = k["sig"]
    fulls = [u for u in units if u.full is not None]
    first_full, first_all, first_head = fulls[0].full, units[0].all, units[0].head

    def score(u):
        if u.full - first_full >= 2:
            pe.wait_ge(s["masked"], u.full - 1)
        bank = k["ps"][u.full % 2]
        pe.matmul(bank[:, 0:P], u.q(0), u.k(0, P), start=True, stop=True)
        pe.matmul(bank[:, P:3 * P], u.q(1), u.k(0, S), start=True, stop=True).then_inc(s["score_ready"], 1)

    def turn(u):
        if u.all - first_all >= 2:
            pe.wait_ge(s["pT_copied"], u.all - 1)
        bank = k["ps"][2 + u.all % 2]
        if u.kind == "full":
            pe.wait_ge(s["p_norm"], u.full + 1)
            for b in range(3):
                mm = pe.transpose(bank[:, b * P:(b + 1) * P], k["prob"][:, u.full % 2, b * P:(b + 1) * P], con(k, "ident"))
        else:
            for t in range(TT):
                mm = pe.transpose(bank[0:N_CMP, t * P:(t + 1) * P], u.p(t), con(k, "ident"))
        mm.then_inc(s["pT_ready"], 1)

    def weigh(u):
        pe.wait_ge(s["pT_copied"], u.all + 1)
        if u.first and u.head - first_head >= 2:
            pe.wait_ge(s["o_copied"], u.head - 1)
        o = k["ps"][4 + u.head % 2][u.at:u.at + u.dv, 0:S]
        pT = k["probT"][:, u.all % 2, :]
        if u.kind == "full":
            pe.matmul(o, u.v(0), pT[:, 0:S], start=u.first, stop=False)
            mm = pe.matmul(o[:, P:S], u.v(1), pT[:, S:S + P], start=False, stop=u.last)
        else:
            mm = pe.matmul(o, u.v(0), pT[0:N_CMP, 0:S], start=u.first, stop=u.last)
        if u.last:
            mm.then_inc(s["o_ready"], 1)
        return mm

    score(fulls[0])
    score(fulls[1])
    for n, u in enumerate(units):
        if u.full is not None and u.full - first_full + 2 < len(fulls):
            score(fulls[u.full - first_full + 2])
        if n >= 1:
            weigh(units[n - 1])
        turn(u)
    weigh(units[-1])


def attend_vector(k, dve, units, scale):
    s, vs = k["sig"], k["vs"]
    fulls = [u for u in units if u.full is not None]

    def mask_and_max(u):
        b = u.full % 2
        dve.wait_ge(s["score_ready"], u.full + 1)
        if u.full - fulls[0].full >= 2:
            dve.wait_ge(s["exp_done"], 2 * (u.full - 1))
        dve.tensor_tensor(k["masked"][:, b, :], k["ps"][b][:, 0:3 * P], con(k, "causal"), ALU.add).then_inc(s["masked"], 1)
        dve.wait_ge(s["masked"], u.full + 1)
        vs.mark(dve.tensor_reduce(k["stat"][:, b, 0:1], k["masked"][:, b, 0:P], AX_X, ALU.max))
        vs.mark(dve.tensor_reduce(k["stat"][:, b, 1:2], k["masked"][:, b, P:3 * P], AX_X, ALU.max))
        vs.wait()
        dve.tensor_scalar(k["stat"][:, b, 2:4], k["stat"][:, b, 0:2], -scale, None, ALU.mult).then_inc(s["negmax"], 1)

    def normalise(u):
        b = u.full % 2
        dve.wait_ge(s["exp_done"], 2 * (u.full + 1))
        vs.mark(dve.tensor_scalar(k["stat"][:, b, 4:6], k["stat"][:, b, 4:6], TINY, None, ALU.max))
        vs.wait()
        vs.mark(dve.reciprocal(k["stat"][:, b, 6:8], k["stat"][:, b, 4:6]))
        vs.wait()
        if u.gate is not None:
            vs.mark(dve.tensor_tensor(k["stat"][:, b, 6:8], k["stat"][:, b, 6:8], u.gate, ALU.mult))
            vs.wait()
        vs.mark(dve.tensor_scalar(k["prob"][:, b, 0:P], k["prob"][:, b, 0:P], k["stat"][:, b, 6:7], None, ALU.mult))
        dve.tensor_scalar(k["prob"][:, b, P:3 * P], k["prob"][:, b, P:3 * P], k["stat"][:, b, 7:8], None, ALU.mult).then_inc(s["p_norm"], 1)

    mask_and_max(fulls[0])
    for n, u in enumerate(fulls):
        if n + 1 < len(fulls):
            mask_and_max(fulls[n + 1])
        normalise(u)


def attend_scalar(k, act, units, scale):
    s = k["sig"]
    fulls = [u for u in units if u.full is not None]

    def exps(u):
        b = u.full % 2
        act.wait_ge(s["negmax"], u.full + 1)
        if u.full - fulls[0].full >= 2:
            act.wait_ge(s["pT_ready"], fulls[u.full - fulls[0].full - 2].all + 1)
        for t, (lo, hi) in enumerate(((0, P), (P, 3 * P))):
            act.activation(k["prob"][:, b, lo:hi], k["masked"][:, b, lo:hi], ACT.Exp, bias=k["stat"][:, b, 2 + t:3 + t], scale=scale,
                           accum_out=k["stat"][:, b, 4 + t:5 + t]).then_inc(s["exp_done"], 1)

    def out(u):
        act.wait_ge(s["o_ready"], u.head + 1)
        act.activation(u.out, k["ps"][4 + u.head % 2][u.at:u.at + u.dv, 0:S], ACT.Copy).then_inc(s["o_copied"], 1)

    exps(fulls[0])
    for n, u in enumerate(units):
        if u.full is not None and u.full - fulls[0].full + 1 < len(fulls):
            exps(fulls[u.full - fulls[0].full + 1])
        act.wait_ge(s["pT_ready"], u.all + 1)
        if u.kind == "full":
            act.activation(k["probT"][:, u.all % 2, :], k["ps"][2 + u.all % 2][:, 0:3 * P], ACT.Copy).then_inc(s["pT_copied"], 1)
        else:
            act.activation(k["probT"][0:N_CMP, u.all % 2, 0:S], k["ps"][2 + u.all % 2][0:N_CMP, 0:S], ACT.Copy).then_inc(s["pT_copied"], 1)
        if n >= 1 and units[n - 1].last:
            out(units[n - 1])
    out(units[-1])


def moba_units(k):
    us = []
    for h in range(HEADS):
        lo = HD * (h % 2)
        us.append(Unit(
            kind="full", first=True, last=True, at=lo, dv=HD, gate=None,
            q=lambda t, h=h, lo=lo: k["qT"][lo:lo + HD, h // 2, t * P:(t + 1) * P],
            k=lambda a, b, h=h, lo=lo: k["kT"][lo:lo + HD, h // 2, a:b],
            v=lambda t, h=h: k["v"][:, t, h * HD:(h + 1) * HD],
            out=k["yaT"][lo:lo + HD, h // 2, :]))
    return attend_units(us, 0, 0, 0)


def mla_units(k):
    us = []
    for h in range(MLA_H):
        lo = MLA_V * (h % 2)
        us.append(Unit(
            kind="full", first=True, last=True, at=lo, dv=MLA_V, gate=None,
            q=lambda t, h=h: k["mqT"][0:MLA_QK, h, t * P:(t + 1) * P],
            k=lambda a, b, h=h: k["mkT"][0:MLA_QK, h, a:b],
            v=lambda t, h=h: k["mkv"][:, t, h * P + MLA_NOPE:(h + 1) * P],
            out=k["catT"][lo:lo + MLA_V, h // 2, :]))
    return attend_units(us, 8, 8, 8)


def nsa_units(k):
    us = []
    for h in range(NSA_H):
        lo, g = HD * (h % 2), h // (NSA_H // NSA_G)
        for br, (kT, v) in enumerate(((k["ksT"], k["nkv"]), (k["kwT"], k["nwv"]))):
            us.append(Unit(
                kind="full", first=br == 0, last=False, at=lo, dv=HD, gate=k["gates"][:, :, 3 * h + 1 + br],
                q=lambda t, h=h, lo=lo: k["nqT"][lo:lo + HD, h // 2, t * P:(t + 1) * P],
                k=lambda a, b, g=g, lo=lo, kT=kT: kT[lo:lo + HD, g, a:b],
                v=lambda t, g=g, v=v: v[:, t, NSA_G * HD + g * HD:NSA_G * HD + (g + 1) * HD],
                out=k["catT"][lo:lo + HD, h // 2, :]))
        us.append(Unit(
            kind="cmp", first=False, last=True, at=lo, dv=HD, gate=None,
            p=lambda t, h=h: k["cp"][:, t, h, :],
            v=lambda t, g=g: k["vcmp"][0:N_CMP, g, :],
            out=k["catT"][lo:lo + HD, h // 2, :]))
    return attend_units(us, 16, 16, 16)




def merge_tensor(k, pe):
    s = k["sig"]
    pe.wait_ge(s["o_copied"], HEADS)
    for m in range(4):
        it = k["plan"][f"merge{m}"]
        w = k["ring"][it.slot]
        pe.wait_ge(k["landed"][it.slot], it.landed)
        for ff in range(2):
            u = 2 * m + ff
            if u >= 2:
                pe.wait_ge(s["merged"], u - 1)
            gate, branch = k["ps"][2 * (u % 2)], k["ps"][2 * (u % 2) + 1]
            for g in range(2):
                for kt in range(KT):
                    at = (g * KT + kt) * 256 + ff * P
                    pe.matmul(gate[:, g * S:(g + 1) * S], w[:, at:at + P], k["hT"][:, kt, :], start=kt == 0, stop=kt == KT - 1)
                for kt in range(4):
                    at = 4096 + (g * 4 + kt) * 256 + ff * P
                    src = k["yaT"] if g else k["ysT"]
                    mm = pe.matmul(branch[:, g * S:(g + 1) * S], w[:, at:at + P], src[:, kt, :], start=kt == 0, stop=kt == 3)
            mm.then_inc(s["merge_ready"], 1)


def merge_scalar(k, act):
    s = k["sig"]
    for u in range(KT):
        act.wait_ge(s["merge_ready"], u + 1)
        if u >= 2:
            act.wait_ge(s["merged"], u - 1)
        act.activation(k["msig"][:, u % 2, :], k["ps"][2 * (u % 2)][:, :], ACT.Sigmoid).then_inc(s["merge_sig"], 1)


def merge_vector(k, dve):
    s, vs = k["sig"], k["vs"]
    for u in range(KT):
        dve.wait_ge(s["merge_sig"], u + 1)
        m = k["msig"][:, u % 2, :]
        vs.mark(dve.tensor_tensor(m, m, k["ps"][2 * (u % 2) + 1][:, :], ALU.mult))
        vs.wait()
        dve.tensor_tensor(k["catT"][:, u, :], m[:, 0:S], m[:, S:2 * S], ALU.add).then_inc(s["merged"], 1)


def out_tensor(k, pe, names, base, src):
    s = k["sig"]
    for half, name in enumerate(names):
        it = k["plan"][name]
        pe.wait_ge(k["landed"][it.slot], it.landed)
        for t in range(TT):
            bank = k["ps"][4 + 2 * half + t]
            for kt in range(KT):
                mm = pe.matmul(bank[:, :], src[:, kt, t * P:(t + 1) * P], k["ring"][it.slot][:, kt * 512:(kt + 1) * 512], start=kt == 0, stop=kt == KT - 1)
            mm.then_inc(s["out_ready"], 1)


def post_norm_scalar(k, act, sem, sem_at, src, done, base):
    s = k["sig"]
    for u in range(4):
        if sem is not None:
            act.wait_ge(sem, sem_at[u])
        half, t = divmod(u, 2)
        act.activation(k["junk"][:, :], src(half, t), ACT.Square, accum_out=k["ss4"][:, t, half:half + 1]).then_inc(done, 1)
        act.wait_ge(done, u + 1)
    act.wait_ge(s["post_mean"], base + 1)
    act.activation(k["ss"][:, 2:4], k["ss"][:, 2:4], ACT.Sqrt).then_inc(s["post_root"], 1)


def post_norm_vector(k, dve, src, done, base, row):
    s, vs = k["sig"], k["vs"]
    dve.wait_ge(done, 4)
    vs.mark(dve.tensor_tensor(k["ss"][:, 0:2], k["ss4"][:, :, 0], k["ss4"][:, :, 1], ALU.add))
    vs.wait()
    dve.tensor_scalar(k["ss"][:, 2:4], k["ss"][:, 0:2], 1.0 / D, EPS, ALU.mult, ALU.add).then_inc(s["post_mean"], 1)
    dve.wait_ge(s["post_root"], base + 1)
    vs.mark(dve.reciprocal(k["ss"][:, 4:6], k["ss"][:, 2:4]))
    vs.wait()
    for t in range(TT):
        for half in range(2):
            g = k["rows"][:, row * D + half * 512:row * D + (half + 1) * 512]
            vs.mark(dve.scalar_tensor_tensor(out=k["xn"][:, t, half * 512:(half + 1) * 512], in0=src(half, t), scalar=k["ss"][:, 4 + t:5 + t], in1=g, op0=ALU.mult, op1=ALU.mult))
        vs.wait()
        dve.tensor_tensor(k["x"][:, t, :], k["x"][:, t, :], k["xn"][:, t, :], ALU.add).then_inc(s["x_ready"], 1)




def router_tensor(k, pe):
    s = k["sig"]
    lo = PARAM_AT["router_w"][0]
    for t in range(TT):
        for kt in range(KT):
            mm = pe.matmul(k["ps"][4][:, t * E:(t + 1) * E], k["hT"][:, kt, t * P:(t + 1) * P], k["params"][:, lo + kt * E:lo + (kt + 1) * E], start=kt == 0, stop=kt == KT - 1)
    mm.then_inc(s["router_ready"], 1)
    pe.wait_ge(s["chosen"], 1)
    bank = k["ps"][6]
    pe.matmul(bank[:, 0:E], con(k, "before"), k["chosen"][:, 0, :], start=True, stop=True)
    pe.matmul(bank[:, E:2 * E], con(k, "before"), k["chosen"][:, 1, :], start=True, stop=False)
    pe.matmul(bank[:, E:2 * E], k["one_row"][:, :], k["chosen"][:, 0, :], start=False, stop=True)
    for t in range(TT):
        mm = pe.matmul(bank[:, 2 * E:3 * E], k["one_row"][:, :], k["chosen"][:, t, :], start=t == 0, stop=t == TT - 1)
    mm.then_inc(s["places_ready"], 1)


def turn_router_weights(k, pe):
    s = k["sig"]
    pe.wait_ge(s["weights_ready"], 1)
    for t in range(TT):
        mm = pe.transpose(k["ps"][6][0:E, t * P:(t + 1) * P], k["wtok"][:, t, :], con(k, "ident"))
    mm.then_inc(s["weights_T"], 1)


def bias_tensor(k, pe):
    s = k["sig"]
    pe.wait_ge(s["weights_T_done"], 1)
    pe.wait_ge(s["tie_loaded"], 32)
    for t in range(TT):
        if t == 1:
            pe.wait_ge(s["y_kept"], 2)
        for half in range(2):
            mm = pe.matmul(k["ps"][6 + half][:, :], k["wT"][0:E, t * P:(t + 1) * P], k["b_down"][0:E, half * 512:(half + 1) * 512], start=True, stop=True)
        mm.then_inc(s["y_init"], 1)
    pe.wait_ge(s["y_kept"], 4)


def router_vector(k, dve):
    s, vs = k["sig"], k["vs"]
    dve.wait_ge(s["router_ready"], 1)
    lg = k["logits"]
    for t in range(TT):
        vs.mark(dve.tensor_tensor(lg[:, t, :], k["ps"][4][:, t * E:(t + 1) * E], par(k, "router_b"), ALU.add))
    vs.wait()
    for t in range(TT):
        vs.mark(dve.tensor_reduce(k["stat"][:, 0, t:t + 1], lg[:, t, :], AX_X, ALU.max))
    vs.wait()
    dve.tensor_scalar(k["stat"][:, 0, 2:4], k["stat"][:, 0, 0:2], -1.0, None, ALU.mult).then_inc(s["router_in"], 1)
    dve.wait_ge(s["tie_loaded"], 32)
    for t in range(TT):
        mine, other = spread_last(lg[:, t, :], E), spread(lg[:, t, :], E)
        vs.mark(dve.tensor_tensor(k["rank_eq"][:, :, :], other, mine, ALU.is_equal))
        vs.mark(dve.tensor_tensor(k["rank_gt"][:, :, :], other, mine, ALU.is_gt))
        vs.wait()
        vs.mark(dve.tensor_tensor(k["rank_eq"][:, :, :], k["rank_eq"][:, :, :], k["tie"][:, :, :], ALU.mult))
        vs.wait()
        vs.mark(dve.tensor_tensor(k["rank_gt"][:, :, :], k["rank_gt"][:, :, :], k["rank_eq"][:, :, :], ALU.add))
        vs.wait()
        vs.mark(dve.tensor_reduce(k["rank"][:, t, :], k["rank_gt"][:, :, :], AX_X, ALU.add))
        vs.wait()
    dve.tensor_scalar(k["chosen"][:, :, :], k["rank"][:, :, :], TOP_K - 0.5, None, ALU.is_lt).then_inc(s["chosen"], 1)
    dve.wait_ge(s["router_exp"], 2)
    for t in range(TT):
        vs.mark(dve.scalar_tensor_tensor(out=k["wtok"][:, t, :], in0=k["rank"][:, t, :], scalar=TOP_K - 0.5, in1=k["wexp"][:, t, :], op0=ALU.is_lt, op1=ALU.mult))
    vs.wait()
    for t in range(TT):
        vs.mark(dve.tensor_reduce(k["stat"][:, 0, 4 + t:5 + t], k["wtok"][:, t, :], AX_X, ALU.add))
    vs.wait()
    vs.mark(dve.reciprocal(k["stat"][:, 0, 6:8], k["stat"][:, 0, 4:6]))
    vs.wait()
    for t in range(TT):
        vs.mark(dve.tensor_scalar(k["wtok"][:, t, :], k["wtok"][:, t, :], k["stat"][:, 0, 6 + t:7 + t], None, ALU.mult))
    vs.wait()
    dve.drain().then_inc(s["weights_ready"], 1)
    dve.wait_ge(s["places_ready"], 1)
    for t in range(TT):
        vs.mark(dve.scalar_tensor_tensor(out=k["place"][:, t, :], in0=k["ps"][6][:, t * E:(t + 1) * E], scalar=1.0, in1=k["chosen"][:, t, :], op0=ALU.add, op1=ALU.mult))
    vs.mark(dve.tensor_reduce(k["most"][:, 0:1], k["ps"][6][:, 2 * E:3 * E], AX_X, ALU.max))
    vs.wait()
    for t in range(TT):
        vs.mark(dve.tensor_scalar(k["place"][:, t, :], k["place"][:, t, :], 1.0, None, ALU.subtract))
    dve.tensor_scalar(k["crowded"][:, :], k["most"][:, 0:1], MOE_SLOTS + 0.5, None, ALU.is_gt).then_inc(s["flag_ready"], 1)
    vs.wait()


def turn_weights_vector(k, dve):
    s = k["sig"]
    dve.wait_ge(s["weights_T"], 1)
    dve.tensor_copy(k["wT"][0:E, :], k["ps"][6][0:E, 0:S]).then_inc(s["weights_T_done"], 1)


def bias_vector(k, dve):
    s = k["sig"]
    for t in range(TT):
        dve.wait_ge(s["y_init"], t + 1)
        for half in range(2):
            dve.tensor_copy(k["total"][:, t, half * 512:(half + 1) * 512], k["ps"][6 + half][:, :]).then_inc(s["y_kept"], 1)


def router_scalar(k, act):
    s = k["sig"]
    act.wait_ge(s["router_in"], 1)
    for t in range(TT):
        act.activation(k["wexp"][:, t, :], k["logits"][:, t, :], ACT.Exp, bias=k["stat"][:, 0, 2 + t:3 + t]).then_inc(s["router_exp"], 1)




def split_product(pe, out, left, right, start, stop):
    pe.matmul(out, left[0], right[0], start=start, stop=False)
    pe.matmul(out, left[0], right[1], start=False, stop=False)
    return pe.matmul(out, left[1], right[0], start=False, stop=stop)


def low_part(dve, lo, x, hi):
    return dve.tensor_tensor(lo, x, hi.bitcast(F32), ALU.subtract)




def crowded(k, eng):
    eng.wait_ge(k["sig"]["flag_ready"], 1)
    return eng.value_load(k["crowded"][0:1, 0:1], min_val=0, max_val=1)


def sweeps(k, eng, sweep):
    sweep(k, eng, 0)
    flag = crowded(k, eng)
    with eng.If(flag > 0):
        sweep(k, eng, 1)


def moe_tensor(k, pe, again):
    s = k["sig"]

    def gather(e):
        c = e + E * again
        pe.wait_ge(s["moe_ones"], c + 1)
        pe.wait_ge(s["moe_xe_read"], 2 * c + 2)
        for kt in range(KT):
            for t in range(TT):
                mm = pe.matmul(k["ps"][4 + kt // 4][:, kt % 4 * P:(kt % 4 + 1) * P], k["xn"][:, t, kt * P:(kt + 1) * P], k["ones"][:, t, :], start=t == 0, stop=t == TT - 1)
        mm.then_inc(s["moe_xe"], 1)

    def turn_weights(e):
        c = e + E * again
        pe.wait_ge(s["moe_weighed"], c + 1)
        pe.wait_ge(s["moe_added"], 4 * c + 4)
        for t in range(TT):
            mm = pe.transpose(k["ps"][6][:, t * P:(t + 1) * P], k["share"][:, t, :], con(k, "ident"))
        mm.then_inc(s["moe_wT"], 1)

    def bring_back(e, t):
        c = e + E * again
        if t == 0:
            pe.wait_ge(s["moe_wT_read"], c + 1)
            pe.wait_ge(s["moe_y_read"], 2 * c + 4)
            pe.wait_ge(s["moe_low"], 2 * c + 4)
        pe.wait_ge(s["moe_added"], 4 * c + 4 + 2 * t)
        for half in range(2):
            mm = split_product(pe, k["ps"][6 + half][:, :], [k[part][:, t * P:(t + 1) * P] for part in ("shareT_hi", "shareT_lo")],
                               [k[part][:, half * 512:(half + 1) * 512] for part in ("y_hi", "y_lo")], True, True)
        mm.then_inc(s["moe_share"], 1)

    def gate_up_step(e, i):
        c, n = e + E * again, 4 * (e + E * again) + i
        if i == 0:
            pe.wait_ge(s["moe_xe_read"], 2 * c + 4)
        pe.wait_ge(k["moe_landed"][i], 16 * (c + 1))
        pe.wait_ge(s["moe_gu_read"], n + 1)
        for g in range(2):
            for ff in range(STEP_TILES):
                for kt in range(KT):
                    at = g * STEP_GATE + kt * STEP_COLS + ff * P
                    mm = pe.matmul(k["ps"][i % 2][:, (2 * g + ff) * P:(2 * g + ff + 1) * P], k["ring"][i][:, at:at + P], k["xeT"][:, kt, :], start=kt == 0, stop=kt == KT - 1)
        mm.then_inc(s["moe_gu"], 1)

    def down_step(e, i):
        c, n = e + E * again, 4 * (e + E * again) + i
        if i == 0:
            pe.wait_ge(s["moe_y_read"], 2 * c + 2)
            pe.wait_ge(s["moe_low"], 2 * c + 2)
        pe.wait_ge(s["moe_w_hi"], n + 1)
        pe.wait_ge(s["moe_w_lo"], n + 1)
        pe.wait_ge(s["moe_act"], n + 2)
        for ff in range(STEP_TILES):
            hidden = [k[part][:, i % 2, ff * P:(ff + 1) * P] for part in ("moe_hid_hi", "moe_hid_lo")]
            for half in range(2):
                at = ff * D + half * 512
                mm = split_product(pe, k["ps"][2 + half][:, :], hidden, [k[part][:, at:at + 512] for part in ("moe_down_hi", "moe_down_lo")],
                                   i == 0 and ff == 0, i == MOE_STEPS - 1 and ff == STEP_TILES - 1)
        mm.then_inc(s["moe_down"], 1)

    def expert(e, first=False, last=False):
        gate_up_step(e, 1)
        down_step(e, 0)
        if not first:
            bring_back(e - 1, 0)
        gate_up_step(e, 2)
        if not first:
            bring_back(e - 1, 1)
        down_step(e, 1)
        gate_up_step(e, 3)
        if not last:
            gather(e + 1)
        turn_weights(e)
        down_step(e, 2)
        if not last:
            gate_up_step(e + 1, 0)
        down_step(e, 3)

    gather(0)
    if not again:
        turn_router_weights(k, pe)
    gate_up_step(0, 0)
    if not again:
        bias_tensor(k, pe)
    expert(0, first=True)
    with pe.Fori(1, E - 1) as e:
        expert(e)
    expert(E - 1, last=True)
    bring_back(E - 1, 0)
    bring_back(E - 1, 1)


def moe_vector(k, dve, again):
    s = k["sig"]
    bias = PARAM_AT["b_gu"][0]
    slots = con(k, "time", MOE_SLOTS * again, MOE_SLOTS * again + MOE_SLOTS)

    def place_tokens(e):
        c = e + E * again
        dve.wait_ge(s["moe_xe"], c + 1)
        for t in range(TT):
            ins = dve.tensor_scalar(k["ones"][:, t, :], slots, k["place"][:, t, bass.ds(e, 1)], None, ALU.is_equal)
        ins.then_inc(s["moe_ones"], 1)

    def weigh_tokens(e):
        c = e + E * again
        dve.wait_ge(s["moe_wT"], c + 1)
        for t in range(TT):
            ins = dve.tensor_scalar(k["share"][:, t, :], slots, k["place"][:, t, bass.ds(e, 1)], k["wtok"][:, t, bass.ds(e, 1)], ALU.is_equal, ALU.mult)
        ins.then_inc(s["moe_weighed"], 1)

    def swiglu(e, i):
        n = 4 * (e + E * again) + i
        bank = k["ps"][i % 2]
        dve.wait_ge(s["moe_gu"], n + 1)
        dve.wait_ge(s["moe_act"], n + 1)
        for ff in range(STEP_TILES):
            cols, b = slice(ff * P, (ff + 1) * P), bias + e * 16 + (i * STEP_TILES + ff) * 2
            ins = dve.tensor_scalar(k["moe_gate"][:, cols], bank[:, cols], k["params"][:, bass.ds(b, 1)], LIMIT, ALU.add, ALU.min)
        ins.then_inc(s["moe_gate"], 1)
        for ff in range(STEP_TILES):
            cols, b = slice(ff * P, (ff + 1) * P), bias + e * 16 + (i * STEP_TILES + ff) * 2 + 1
            ins = dve.tensor_scalar(k["moe_up"][:, cols], bank[:, 2 * P + ff * P:2 * P + (ff + 1) * P], k["params"][:, bass.ds(b, 1)], LIMIT, ALU.add, ALU.min)
        ins.then_inc(s["moe_gu_read"], 1)
        dve.wait_ge(s["moe_gu_read"], n + 3)
        dve.tensor_scalar(k["moe_up"][:, :], k["moe_up"][:, :], -LIMIT, 1.0, ALU.max, ALU.add).then_inc(s["moe_step"], 1)
        dve.wait_ge(s["moe_sig"], n + 1)
        dve.tensor_tensor(k["moe_sg"][:, :], k["moe_sg"][:, :], k["moe_gate"][:, :], ALU.mult).then_inc(s["moe_step"], 1)
        dve.wait_ge(s["moe_step"], 4 * n + 2)
        dve.tensor_tensor(k["moe_sg"][:, :], k["moe_sg"][:, :], k["moe_up"][:, :], ALU.mult).then_inc(s["moe_step"], 1)
        hi, lo = k["moe_hid_hi"][:, i % 2, :], k["moe_hid_lo"][:, i % 2, :]
        dve.wait_ge(s["moe_step"], 4 * n + 3)
        dve.wait_ge(s["moe_down"], n + 1)
        dve.tensor_copy(hi, k["moe_sg"][:, :]).then_inc(s["moe_step"], 1)
        dve.wait_ge(s["moe_step"], 4 * n + 4)
        low_part(dve, lo, k["moe_sg"][:, :], hi).then_inc(s["moe_act"], 1)

    def down_low(e, i):
        n = 4 * (e + E * again) + i
        dve.wait_ge(s["moe_w_hi"], n + 1)
        low_part(dve, k["moe_down_lo"][:, :], k["ring"][i][:, 2 * STEP_GATE:], k["moe_down_hi"][:, :]).then_inc(s["moe_w_lo"], 1)

    def shares_low(e):
        c = e + E * again
        dve.wait_ge(s["moe_wT_read"], c + 1)
        low_part(dve, k["shareT_lo"][:, :], k["ps"][6][:, 0:S], k["shareT_hi"][:, :]).then_inc(s["moe_low"], 1)

    def results_low(e):
        c = e + E * again
        dve.wait_ge(s["moe_share"], 2 * c + 2)
        dve.wait_ge(s["moe_y_read"], 2 * c + 4)
        for half in range(2):
            cols = slice(half * 512, (half + 1) * 512)
            ins = low_part(dve, k["y_lo"][:, cols], k["ps"][2 + half][:, :], k["y_hi"][:, cols])
        ins.then_inc(s["moe_low"], 1)

    def add(e, t):
        c = e + E * again
        dve.wait_ge(s["moe_share"], 2 * c + t + 3)
        dve.wait_ge(s["moe_added"], 4 * c + 2 * t + 4)
        for half in range(2):
            total = k["total"][:, t, half * 512:(half + 1) * 512]
            dve.tensor_tensor(total, total, k["ps"][6 + half][:, :], ALU.add).then_inc(s["moe_added"], 1)

    def expert(e, first=False, last=False):
        if not first:
            results_low(e - 1)
        down_low(e, 0)
        swiglu(e, 1)
        down_low(e, 1)
        if not first:
            add(e - 1, 0)
        swiglu(e, 2)
        down_low(e, 2)
        if not first:
            add(e - 1, 1)
        if not last:
            place_tokens(e + 1)
        weigh_tokens(e)
        swiglu(e, 3)
        shares_low(e)
        down_low(e, 3)
        if not last:
            swiglu(e + 1, 0)

    place_tokens(0)
    if not again:
        turn_weights_vector(k, dve)
    swiglu(0, 0)
    if not again:
        bias_vector(k, dve)
    expert(0, first=True)
    with dve.Fori(1, E - 1) as e:
        expert(e)
    expert(E - 1, last=True)
    results_low(E - 1)
    add(E - 1, 0)
    add(E - 1, 1)


def moe_scalar(k, act, again):
    s = k["sig"]

    def gathered(e):
        c = e + E * again
        act.wait_ge(s["moe_xe"], c + 2)
        for b in range(2):
            act.activation(k["xeT"][:, 4 * b:4 * b + 4, :].rearrange("p a b -> p (a b)"), k["ps"][4 + b][:, :], ACT.Copy).then_inc(s["moe_xe_read"], 1)

    def sigmoid(e, i):
        n = 4 * (e + E * again) + i
        act.wait_ge(s["moe_gate"], n + 1)
        act.activation(k["moe_sg"][:, :], k["moe_gate"][:, :], ACT.Sigmoid, scale=ALPHA).then_inc(s["moe_sig"], 1)

    def down_high(e, i):
        n = 4 * (e + E * again) + i
        act.wait_ge(k["moe_landed"][i], 16 * (e + E * again + 1))
        act.wait_ge(s["moe_down"], n + 2)
        act.activation(k["moe_down_hi"][:, :], k["ring"][i][:, 2 * STEP_GATE:], ACT.Copy).then_inc(s["moe_w_hi"], 1)

    def results(e):
        c = e + E * again
        act.wait_ge(s["moe_down"], 4 * c + 6)
        act.wait_ge(s["moe_share"], 2 * c + 2)
        for half in range(2):
            act.activation(k["y_hi"][:, half * 512:(half + 1) * 512], k["ps"][2 + half][:, :], ACT.Copy).then_inc(s["moe_y_read"], 1)

    def expert(e, first=False, last=False):
        if not first:
            results(e - 1)
        down_high(e, 0)
        sigmoid(e, 1)
        down_high(e, 1)
        sigmoid(e, 2)
        down_high(e, 2)
        sigmoid(e, 3)
        if not last:
            gathered(e + 1)
        act.wait_ge(s["moe_wT"], e + E * again + 2)
        act.activation(k["shareT_hi"][:, :], k["ps"][6][:, 0:S], ACT.Copy).then_inc(s["moe_wT_read"], 1)
        down_high(e, 3)
        if not last:
            sigmoid(e + 1, 0)

    gathered(0)
    sigmoid(0, 0)
    act.wait_ge(s["y_kept"], 4)
    expert(0, first=True)
    with act.Fori(1, E - 1) as e:
        expert(e)
    expert(E - 1, last=True)
    results(E - 1)


def moe_sync(k, sp, again):
    s = k["sig"]

    def load(e, i):
        sp.dma_start(k["ring"][i][:, :], k["src"]["moe"][bass.ds(4 * e + i, 1), :, :].rearrange("o p n -> (o p) n")).then_inc(k["moe_landed"][i], 16)

    for i in range(MOE_STEPS):
        if again:
            sp.wait_ge(s["moe_down"], 4 * E + i - 1)
        elif k["moe_free"][i] is not None:
            sp.wait_ge(*k["moe_free"][i])
        load(0, i)
    with sp.Fori(1, E) as e:
        for i in range(MOE_STEPS):
            sp.wait_ge(s["moe_down"], 4 * (e + E * again) + i - 1)
            load(e, i)




def ffn_tensor(k, pe, q):
    s = k["sig"]
    base = FFN_STEPS * q
    half_kt = KT // 2

    def gate_up(m, piece):
        n = base + m
        pe.wait_ge(s["ffn_w_hi"], 2 * n + piece + 1)
        pe.wait_ge(s["ffn_w_lo"], 2 * n + piece + 1)
        if piece == 0 and n >= 1:
            pe.wait_ge(s["act_ready"], n)
        for kk in range(half_kt):
            kt = piece * half_kt + kk
            w = [k[part][:, piece, kk * 512:(kk + 1) * 512] for part in ("ffn_hi", "ffn_lo")]
            for t in range(TT):
                h = [k[part][:, kt, t * P:(t + 1) * P] for part in ("hT_hi", "hT_lo")]
                mm = split_product(pe, k["ps"][2 * (n % 2) + t][:, :], h, w, kt == 0, kt == KT - 1)
        mm.then_inc(s["gu_ready"], 1)

    def turn(m):
        n = base + m
        pe.wait_ge(s["gu_drained"], n + 3)
        for ff in range(STEP_TILES):
            for t in range(TT):
                mm = pe.transpose(k["ps"][2 * (n % 2)][:, (ff * TT + t) * P:(ff * TT + t + 1) * P], k["sg"][:, t * STEP_COLS + ff * P:t * STEP_COLS + (ff + 1) * P], con(k, "ident"))
        mm.then_inc(s["actT_ready"], 1)

    def down(m):
        n = base + m
        pe.wait_ge(s["ffn_down_hi"], n + 1)
        pe.wait_ge(s["ffn_down_lo"], n + 1)
        pe.wait_ge(s["actT_hi"], n + 1)
        pe.wait_ge(s["act_ready"], n + 2)
        for ff in range(STEP_TILES):
            for t in range(TT):
                acts = [k[part][:, ff, t * P:(t + 1) * P] for part in ("act_hi", "act_lo")]
                for half in range(2):
                    at = ff * D + half * 512
                    mm = split_product(pe, k["ps"][4 + 2 * half + t][:, :], acts, [k[part][:, 2, at:at + 512] for part in ("ffn_hi", "ffn_lo")],
                                       m == 0 and ff == 0, m == FFN_STEPS - 1 and ff == STEP_TILES - 1)
        mm.then_inc(s["down_done"], 1)

    gate_up(0, 0)
    gate_up(0, 1)
    for m in range(FFN_STEPS):
        if m + 1 < FFN_STEPS:
            gate_up(m + 1, 0)
        turn(m)
        if m + 1 < FFN_STEPS:
            gate_up(m + 1, 1)
        down(m)


def ffn_weights_low(k, dve, q, m, piece):
    s = k["sig"]
    n = FFN_STEPS * q + m
    dve.wait_ge(*((s["ffn_down_hi"], n + 1) if piece == 2 else (s["ffn_w_hi"], 2 * n + piece + 1)))
    w = k["ring"][k["plan"][f"ffn{q}_{m}"].slot][:, piece * PIECE:(piece + 1) * PIECE]
    low_part(dve, k["ffn_lo"][:, piece, :], w, k["ffn_hi"][:, piece, :]).then_inc(s["ffn_down_lo"] if piece == 2 else s["ffn_w_lo"], 1)


def ffn_vector(k, dve, q):
    s, vs = k["sig"], k["vs"]
    base = FFN_STEPS * q

    def weights_low(m, piece):
        ffn_weights_low(k, dve, q, m, piece)

    def swiglu(m):
        n = base + m
        banks = [k["ps"][2 * (n % 2) + t] for t in range(TT)]
        dve.wait_ge(s["sig_ready"], n + 1)
        for t in range(TT):
            sg = k["sg"][:, t * STEP_COLS:(t + 1) * STEP_COLS]
            vs.mark(dve.tensor_tensor(sg, sg, banks[t][:, 0:STEP_COLS], ALU.mult))
        vs.wait()
        for t in range(TT):
            sg = k["sg"][:, t * STEP_COLS:(t + 1) * STEP_COLS]
            ins = dve.tensor_tensor(sg, sg, banks[t][:, STEP_COLS:2 * STEP_COLS], ALU.mult)
        ins.then_inc(s["gu_drained"], 1)

    def turned_low(m):
        n = base + m
        dve.wait_ge(s["actT_hi"], n + 1)
        low_part(dve, k["act_lo"][:, :, :].rearrange("p a b -> p (a b)"), k["ps"][2 * (n % 2)][:, :], k["act_hi"][:, :, :].rearrange("p a b -> p (a b)")).then_inc(s["act_ready"], 1)

    weights_low(0, 1)
    weights_low(1, 0)
    swiglu(0)
    weights_low(1, 1)
    for m in range(FFN_STEPS):
        weights_low(m, 2)
        turned_low(m)
        if m + 2 < FFN_STEPS:
            weights_low(m + 2, 0)
        if m + 1 < FFN_STEPS:
            swiglu(m + 1)
        if m + 2 < FFN_STEPS:
            weights_low(m + 2, 1)
    dve.wait_ge(s["down_done"], 2 + base + FFN_STEPS)
    for t in range(TT):
        for half in range(2):
            x = k["x"][:, t, half * 512:(half + 1) * 512]
            ins = dve.scalar_tensor_tensor(out=x, in0=k["ps"][4 + 2 * half + t][:, :], scalar=0.5, in1=x, op0=ALU.mult, op1=ALU.add)
        ins.then_inc(s["x_ready"], 1)


def ffn_weights_high(k, act, q, m, piece):
    s = k["sig"]
    n = FFN_STEPS * q + m
    it = k["plan"][f"ffn{q}_{m}"]
    act.wait_ge(k["landed"][it.slot], it.landed)
    if piece == 2:
        act.wait_ge(s["down_done"], n + 2)
    elif n >= 1:
        act.wait_ge(s["gu_ready"], 2 * (n - 1) + piece + 1)
    act.activation(k["ffn_hi"][:, piece, :], k["ring"][it.slot][:, piece * PIECE:(piece + 1) * PIECE], ACT.Copy).then_inc(s["ffn_down_hi"] if piece == 2 else s["ffn_w_hi"], 1)


def ffn_scalar(k, act, q):
    s = k["sig"]
    base = FFN_STEPS * q

    def weights_high(m, piece):
        ffn_weights_high(k, act, q, m, piece)

    def sigmoid(m):
        n = base + m
        act.wait_ge(s["gu_ready"], 2 * n + 2)
        for t in range(TT):
            ins = act.activation(k["sg"][:, t * STEP_COLS:(t + 1) * STEP_COLS], k["ps"][2 * (n % 2) + t][:, 0:STEP_COLS], ACT.Sigmoid)
        ins.then_inc(s["sig_ready"], 1)

    def turned_high(m):
        n = base + m
        act.wait_ge(s["actT_ready"], n + 1)
        act.wait_ge(s["down_done"], n + 2)
        act.activation(k["act_hi"][:, :, :].rearrange("p a b -> p (a b)"), k["ps"][2 * (n % 2)][:, :], ACT.Copy).then_inc(s["actT_hi"], 1)

    weights_high(0, 1)
    weights_high(1, 0)
    sigmoid(0)
    weights_high(1, 1)
    for m in range(FFN_STEPS):
        weights_high(m, 2)
        turned_high(m)
        if m + 2 < FFN_STEPS:
            weights_high(m + 2, 0)
        if m + 1 < FFN_STEPS:
            sigmoid(m + 1)
        if m + 2 < FFN_STEPS:
            weights_high(m + 2, 1)


def add_out_vector(k, dve, base):
    s = k["sig"]
    for t in range(TT):
        for half in range(2):
            u = 2 * half + t
            dve.wait_ge(s["out_ready"], base + u + 1)
            x = k["x"][:, t, half * 512:(half + 1) * 512]
            ins = dve.tensor_tensor(x, x, k["ps"][4 + u][:, :], ALU.add)
        ins.then_inc(s["x_ready"], 1)




def lora_norm_scalar(k, act):
    s = k["sig"]
    n = 0
    for t in range(TT):
        act.wait_ge(s["proj_act"], 5)
        act.wait_ge(s["proj_dve"], 5)
        for c, (lo, w) in enumerate(((0, Q_LORA), (Q_LORA, KV_LORA))):
            act.activation(k["lora_n"][:, t, lo:lo + w], k["hya"][:, t, lo:lo + w], ACT.Square,
                           accum_out=k["small"][:, 2 * c + t:2 * c + t + 1]).then_inc(s["lora_sq"], 1)
    act.wait_ge(s["lora_mean"], 2)
    act.activation(k["small"][:, 4:8], k["small"][:, 4:8], ACT.Sqrt).then_inc(s["lora_root"], 1)


def lora_norm_vector(k, dve):
    s, vs = k["sig"], k["vs"]
    dve.wait_ge(s["lora_sq"], 4)
    dve.tensor_scalar(k["small"][:, 4:6], k["small"][:, 0:2], 1.0 / Q_LORA, EPS, ALU.mult, ALU.add).then_inc(s["lora_mean"], 1)
    dve.tensor_scalar(k["small"][:, 6:8], k["small"][:, 2:4], 1.0 / KV_LORA, EPS, ALU.mult, ALU.add).then_inc(s["lora_mean"], 1)
    dve.wait_ge(s["lora_root"], 1)
    vs.mark(dve.reciprocal(k["small"][:, 8:12], k["small"][:, 4:8]))
    vs.wait()
    for t in range(TT):
        for c, (lo, w) in enumerate(((0, Q_LORA), (Q_LORA, KV_LORA))):
            dve.tensor_scalar(k["lora_n"][:, t, lo:lo + w], k["hya"][:, t, lo:lo + w], k["small"][:, 8 + 2 * c + t:9 + 2 * c + t], None, ALU.mult)\
               .then_inc(s["lora_n"], 1)


def hy_turn_jobs(k):
    jobs = [[(k["lora_n"][:, t, c * P:(c + 1) * P], P, t * P) for t in range(TT)] for c in range(3)]
    jobs += [[(k["hyb"][:, t, (2 * g + c) * P:(2 * g + c + 1) * P], P, (2 * c + t) * P) for c in range(2) for t in range(TT)] for g in range(2)]
    jobs += [[(k["hya"][:, t, HYA - GLA_RANK:HYA], GLA_RANK, t * P) for t in range(TT)]]
    lo = PARAM_AT["q_norm"][0]
    kv = PARAM_AT["kv_norm"][0]
    reads = [(k["loraT"][:, 0, :], P, S, k["params"][:, lo:lo + 1]), (k["loraT"][:, 1, :], P, S, k["params"][:, lo + 1:lo + 2]),
             (k["loraT"][:, 2, :], P, S, k["params"][:, kv:kv + 1]),
             (k["gqT"][:, :, :].rearrange("p a b -> p (a b)"), P, 2 * S), (k["gkT"][:, :, :].rearrange("p a b -> p (a b)"), P, 2 * S),
             (k["gaT"][0:GLA_RANK, :], GLA_RANK, S)]
    return jobs, reads


def lora_tensor(k, pe):
    s = k["sig"]
    it = k["plan"]["lora"]
    w = k["ring"][it.slot]
    pe.wait_ge(k["landed"][it.slot], it.landed)
    for t in range(TT):
        for i in range(4):
            u = 4 * t + i
            if t == 1:
                pe.wait_ge(s["lora_act"] if i % 2 == 0 else s["lora_dve"], i // 2 + 1)
            if i < 2:
                for kt in range(2):
                    mm = pe.matmul(k["ps"][i][:, 0:384], k["loraT"][:, kt, t * P:(t + 1) * P], w[:, kt * 768 + i * 384:kt * 768 + (i + 1) * 384],
                                   start=kt == 0, stop=kt == 1)
            else:
                at = 2 * 768 + (i - 2) * 512
                mm = pe.matmul(k["ps"][i][:, :], k["loraT"][:, 2, t * P:(t + 1) * P], w[:, at:at + 512], start=True, stop=True)
            mm.then_inc(s["lora_ready"], 1)


def lora_read(k, eng, parity):
    s = k["sig"]
    for t in range(TT):
        for i in range(parity, 4, 2):
            eng.wait_ge(s["lora_ready"], 4 * t + i + 1)
            dst = k["mq"][:, t, i * 384:(i + 1) * 384] if i < 2 else k["mkv"][:, t, (i - 2) * 512:(i - 1) * 512]
            src = k["ps"][i][:, 0:dst.shape[1]]
            if parity == 0:
                eng.activation(dst, src, ACT.Copy).then_inc(s["lora_act"], 1)
            else:
                eng.tensor_copy(dst, src).then_inc(s["lora_dve"], 1)


def mla_rows(k, eng, steps, t, done, tmp):
    s = k["sig"]
    eng.wait_ge(s["lora_act"], 4)
    eng.wait_ge(s["lora_dve"], 4)
    cos, sin = angle(k, k["cos"], f"m{t}"), angle(k, k["sin"], f"m{t}")
    q = k["mq"][:, t, :].rearrange("p (h x) -> p h x", h=MLA_H)
    rope_rotate(eng, steps, q[:, :, MLA_NOPE:MLA_QK], q[:, :, MLA_NOPE:MLA_QK], MLA_H, MLA_ROPE // 2, cos, sin, tmp)
    kr = k["hya"][:, t, Q_LORA + KV_LORA:Q_LORA + KV_LORA + MLA_ROPE]
    kr1 = kr.unsqueeze(1)
    rope_rotate(eng, steps, kr1, kr1, 1, MLA_ROPE // 2, cos, sin, tmp)
    full = k["mk"][:, t, :].rearrange("p (h x) -> p h x", h=MLA_H)
    kv = k["mkv"][:, t, :].rearrange("p (h x) -> p h x", h=MLA_H)
    steps.mark(eng.tensor_copy(full[:, :, 0:MLA_NOPE], kv[:, :, 0:MLA_NOPE]))
    steps.mark(eng.tensor_copy(full[:, :, MLA_NOPE:MLA_QK], spread(kr, MLA_H)))
    steps.wait()
    eng.drain().then_inc(done, 1)


def mla_turn_jobs(k):
    jobs, reads = [], []
    for rows, dst in ((k["mq"], k["mqT"]), (k["mk"], k["mkT"])):
        for b in range(4):
            jobs.append([(rows[:, t, h * MLA_QK:(h + 1) * MLA_QK], MLA_QK, ((h - 2 * b) * 2 + t) * P) for h in (2 * b, 2 * b + 1) for t in range(TT)])
            reads.append((dst[0:MLA_QK, 2 * b:2 * b + 2, :].rearrange("p a b -> p (a b)"), MLA_QK, 2 * S))
    return jobs, reads


def gla_rows(k, t, h):
    at = (2 * t + h // 2) * P
    return k["ps"][2 + h % 2][:, at:at + P]


def gla_tensor(k, pe):
    s = k["sig"]
    wa = PARAM_AT["w_a2"][0]
    for c in range(2):
        mm = pe.matmul(k["ps"][6][:, c * S:(c + 1) * S], k["params"][0:GLA_RANK, wa + c * P:wa + (c + 1) * P], k["gaT"][0:GLA_RANK, :], start=True, stop=True)
    mm.then_inc(s["gla_pre"], 1)
    pe.wait_ge(s["gla_ready"], 3)
    for t in range(TT):
        for c in range(2):
            mm = pe.transpose(k["ps"][7][:, (2 * t + c) * P:(2 * t + c + 1) * P], k["kdecT"][:, c, t * P:(t + 1) * P], con(k, "ident"))
    mm.then_inc(s["gla_kdec"], 1)
    for hh in range(2):
        lo = 64 * hh
        for t in range(TT):
            for c in range(2):
                mm = pe.matmul(k["ps"][hh][:, (2 * t + c) * P:(2 * t + c + 1) * P], k["kdecT"][lo:lo + 64, c, t * P:(t + 1) * P],
                               k["qintraT"][lo:lo + 64, c, t * P:(t + 1) * P], start=True, stop=True)
        mm.then_inc(s["gla_A"], 1)
    pe.wait_ge(s["gla_kdec_read"], 1)
    for odd in range(2):
        for n in range(odd, NCH - 1, 2):
            for c in range(2):
                for hh in range(2):
                    h, lo, tok, at = 2 * c + hh, 64 * hh, CHUNK * odd, (n // 2 * 2 + c) * P
                    mm = pe.matmul(k["ps"][4 + odd][lo:lo + 64, at:at + P], k["kdec"][tok:tok + CHUNK, n // 2, c, lo:lo + 64],
                                   k["hyv"][tok:tok + CHUNK, n // 2, h * P:(h + 1) * P], start=True, stop=True)
        mm.then_inc(s["gla_kv"], 1)
    pe.wait_ge(s["gla_state"], 2)
    pe.wait_ge(s["gla_A_read"], 2)
    for hh in range(2):
        for n2 in range(4):
            t, c = divmod(n2, 2)
            h, lo = 2 * c + hh, 64 * hh
            pe.matmul(gla_rows(k, t, h), k["AT"][:, h % 2, 2 * t + c, :], k["hyv"][:, t, h * P:(h + 1) * P], start=True, stop=False, skip_group_check=True)
            for n in (2 * t, 2 * t + 1):
                if n == 0:
                    continue
                at = CHUNK * (n % 2)
                mm = pe.matmul(gla_rows(k, t, h)[at:at + CHUNK, :], k["qinterT"][lo:lo + 64, c, n * CHUNK:(n + 1) * CHUNK],
                               k["state"][lo:lo + 64, c, n - 1, :], start=False, stop=n == 2 * t + 1, skip_group_check=True)
        mm.then_inc(s["gla_o"], 1)


def gla_vector(k, dve):
    s, vs = k["sig"], k["vs"]
    ba = PARAM_AT["b_a"][0]
    dve.wait_ge(s["gla_pre"], 1)
    z, la = k["gz"], k["gla"]
    for c in range(2):
        vs.mark(dve.tensor_scalar(z[:, c, :], k["ps"][6][:, c * S:(c + 1) * S], k["params"][:, ba + c:ba + c + 1], None, ALU.add))
    vs.wait()
    vs.mark(dve.tensor_scalar(la[:, :, :], z[:, :, :], -1.0, None, ALU.mult))
    vs.wait()
    dve.tensor_tensor(la[:, :, :], la[:, :, :], z[:, :, :], ALU.max).then_inc(s["gla_abs"], 1)
    vs.mark(dve.tensor_scalar(z[:, :, :], z[:, :, :], 0.0, None, ALU.min))
    vs.wait()
    dve.wait_ge(s["gla_soft"], 2)
    vs.mark(dve.tensor_tensor(z[:, :, :], z[:, :, :], la[:, :, :], ALU.subtract))
    vs.wait()
    vs.mark(dve.tensor_scalar(z[:, :, :], z[:, :, :], 1.0 / GLA_TAU, None, ALU.mult))
    vs.wait()
    for c in range(2):
        vs.mark(dve.tensor_tensor_scan(k["gb"][:, c, :], con(k, "gla_keep"), z[:, c, :], 0.0, ALU.mult, ALU.add))
    vs.wait()
    for c in range(2):
        b = k["gb"][:, c, :].rearrange("p (n i) -> p n i", n=NCH)
        last = b[:, :, CHUNK - 1:CHUNK].to_broadcast([P, NCH, CHUNK])
        dve.tensor_tensor(k["gd"][:, c, :].rearrange("p (n i) -> p n i", n=NCH), last, b, ALU.subtract).then_inc(s["gla_arg"], 1)
    dve.wait_ge(s["gla_exp"], 4)
    dve.tensor_tensor(k["kdecT"][:, :, :], k["gkT"][:, :, :], k["ge"][:, 0, :, :], ALU.mult).then_inc(s["gla_ready"], 1)
    dve.scalar_tensor_tensor(out=k["qintraT"][:, :, :], in0=k["gqT"][:, :, :], scalar=GLA_DK ** -0.5, in1=k["ge"][:, 1, :, :], op0=ALU.mult, op1=ALU.mult).then_inc(s["gla_ready"], 1)
    dve.scalar_tensor_tensor(out=k["qinterT"][:, :, :], in0=k["gqT"][:, :, :], scalar=GLA_DK ** -0.5, in1=k["ge"][:, 2, :, :], op0=ALU.mult, op1=ALU.mult).then_inc(s["gla_ready"], 1)
    dve.wait_ge(s["gla_kdec"], 1)
    dve.tensor_copy(k["kdec"][:, :, :, :].rearrange("p a b c -> p (a b c)"), k["ps"][7][:, :]).then_inc(s["gla_kdec_read"], 1)
    for hh in range(2):
        dve.wait_ge(s["gla_A"], hh + 1)
        dve.tensor_tensor(k["AT"][:, hh, :, :], k["ps"][hh][:, :].rearrange("p (n i) -> p n i", n=4), spread(con(k, "gla_mask"), 4), ALU.mult).then_inc(s["gla_A_read"], 1)
    dve.wait_ge(s["gla_kv"], 2)
    for c in range(2):
        vs.mark(dve.tensor_copy(k["state"][:, c, 0, :], k["ps"][4][:, c * P:(c + 1) * P]))
        vs.wait()
        for n in (1, 2):
            ins = dve.scalar_tensor_tensor(out=k["state"][:, c, n, :], in0=k["state"][:, c, n - 1, :], scalar=k["gdec"][:, c, n:n + 1],
                                           in1=k["ps"][4 + n % 2][:, (n // 2 * 2 + c) * P:(n // 2 * 2 + c + 1) * P], op0=ALU.mult, op1=ALU.add)
            if n == 1:
                vs.mark(ins)
                vs.wait()
        ins.then_inc(s["gla_state"], 1)
    dve.wait_ge(s["gla_sq"], 8)
    dve.tensor_scalar(k["small"][:, 16:24], k["small"][:, 16:24], 1.0 / GLA_DV, EPS, ALU.mult, ALU.add).then_inc(s["gla_mean"], 1)
    dve.wait_ge(s["gla_root"], 1)
    vs.mark(dve.reciprocal(k["small"][:, 24:32], k["small"][:, 16:24]))
    vs.wait()
    dve.wait_ge(s["gla_silu"], 2)
    for t in range(TT):
        vs.mark(dve.tensor_tensor(k["hyr"][:, t, :], k["hyr"][:, t, :], k["rsig"][:, t, :], ALU.mult))
        for h in range(GLA_H):
            vs.mark(dve.scalar_tensor_tensor(out=k["rsig2"][:, t, h * P:(h + 1) * P], in0=gla_rows(k, t, h),
                                             scalar=k["small"][:, 24 + 4 * t + h:25 + 4 * t + h], in1=par(k, "out_norm"), op0=ALU.mult, op1=ALU.mult))
        vs.wait()
        dve.tensor_tensor(k["rsig2"][:, t, :], k["rsig2"][:, t, :], k["hyr"][:, t, :], ALU.mult).then_inc(s["gla_out"], 1)


def gla_scalar(k, act):
    s, acs = k["sig"], k["acs"]
    act.wait_ge(s["gla_abs"], 1)
    act.activation(k["gla"][:, :, :], k["gla"][:, :, :], ACT.Exp, scale=-1.0).then_inc(s["gla_soft"], 1)
    act.wait_ge(s["gla_soft"], 1)
    act.activation(k["gla"][:, :, :], k["gla"][:, :, :], ACT.Ln, bias=1.0).then_inc(s["gla_soft"], 1)
    act.wait_ge(s["gla_arg"], 2)
    act.activation(k["ge"][:, 0, :, :], k["gd"][:, :, :], ACT.Exp).then_inc(s["gla_exp"], 1)
    act.activation(k["ge"][:, 1, :, :], k["gd"][:, :, :], ACT.Exp, scale=-1.0).then_inc(s["gla_exp"], 1)
    act.activation(k["ge"][:, 2, :, :], k["gb"][:, :, :], ACT.Exp).then_inc(s["gla_exp"], 1)
    act.activation(k["gdec"][:, :, :], k["gb"][:, :, CHUNK - 1:S:CHUNK], ACT.Exp).then_inc(s["gla_exp"], 1)
    for t in range(TT):
        act.activation(k["rsig"][:, t, :], k["hyr"][:, t, :], ACT.Sigmoid).then_inc(s["gla_silu"], 1)
    act.wait_ge(s["gla_o"], 2)
    for t in range(TT):
        for h in range(GLA_H):
            act.activation(k["rsig2"][:, t, h * P:(h + 1) * P], gla_rows(k, t, h), ACT.Square,
                           accum_out=k["small"][:, 16 + 4 * t + h:17 + 4 * t + h]).then_inc(s["gla_sq"], 1)
    act.wait_ge(s["gla_mean"], 1)
    act.activation(k["small"][:, 16:24], k["small"][:, 16:24], ACT.Sqrt).then_inc(s["gla_root"], 1)


def gla_turn_jobs(k):
    jobs = [[(k["rsig2"][:, t, (2 * b + c) * P:(2 * b + c + 1) * P], P, (2 * c + t) * P) for c in range(2) for t in range(TT)] for b in range(2)]
    reads = [(k["catT"][:, 4 + 2 * b:6 + 2 * b, :].rearrange("p a b -> p (a b)"), P, 2 * S) for b in range(2)]
    return jobs, reads




def nsa_rows(k, eng, steps, t, done, tmp):
    cos, sin = angle(k, k["cos"], f"b{t}"), angle(k, k["sin"], f"b{t}")
    rope_rotate(eng, steps, k["xn"][:, t, :].rearrange("p (h x) -> p h x", h=NSA_H), k["nq"][:, t, :].rearrange("p (h x) -> p h x", h=NSA_H),
                NSA_H, HD // 2, cos, sin, tmp)
    for w, rows in enumerate((k["nkv"], k["nwv"])):
        kd = k["kd"][:, t, w, :, :, :]
        rope_rotate(eng, steps, kd[:, :, 0, :], rows[:, t, 0:NSA_G * HD].rearrange("p (h x) -> p h x", h=NSA_G), NSA_G, HD // 2, cos, sin, tmp)
        steps.mark(eng.tensor_copy(kd[:, :, 1, :], kd[:, :, 0, :]))
    steps.wait()
    eng.drain().then_inc(done, 1)


def nsa_turn_jobs(k):
    jobs, reads = [], []

    def four(tile, dst, tiles):
        for b in range(tiles // 2):
            jobs.append([(tile(2 * b + c, t), P, (2 * c + t) * P) for c in range(2) for t in range(TT)])
            reads.append((dst[:, 2 * b:2 * b + 2, :].rearrange("p a b -> p (a b)"), P, 2 * S))

    four(lambda c, t: k["kcv"][:, t, c * P:(c + 1) * P], k["kcvT"], 4)
    four(lambda c, t: k["xn"][:, t, c * P:(c + 1) * P], k["nqT"], 8)
    four(lambda c, t: k["kd"][:, t, 0, c, :, :].rearrange("p a b -> p (a b)"), k["ksT"], 4)
    four(lambda c, t: k["kd"][:, t, 1, c, :, :].rearrange("p a b -> p (a b)"), k["kwT"], 4)
    return jobs, reads


def cmp_tensor(k, pe):
    s = k["sig"]
    it = k["plan"]["nsa_c"]
    w = k["ring"][it.slot]
    pe.wait_ge(k["landed"][it.slot], it.landed)
    for t in range(TT):
        for kt in range(KT):
            mm = pe.matmul(k["ps"][6][:, t * 48:(t + 1) * 48], k["hT"][:, kt, t * P:(t + 1) * P], w[:, 4096 + kt * 48:4096 + (kt + 1) * 48], start=kt == 0, stop=kt == KT - 1)
    mm.then_inc(s["gate_in"], 1)
    pe.wait_ge(s["cmp_blk"], 8)
    for c in range(2):
        lo = 64 * c
        for n in range(CMP_LEN):
            mm = pe.matmul(k["ps"][4 + c][:, 0:NSA_G * N_CMP], w[lo:lo + HD, n * CMP_HID:(n + 1) * CMP_HID], k["blk"][lo:lo + HD, n, :, :].rearrange("p a b -> p (a b)"),
                           start=n == 0, stop=n == CMP_LEN - 1)
        mm.then_inc(s["cmp_h"], 1)
    pe.wait_ge(s["cmp_hid"], 2)
    for c in range(2):
        for g in range(NSA_G):
            at = 4096 + 384 + c * HD
            mm = pe.matmul(k["ps"][7][0:N_CMP, c * S + g * HD:c * S + (g + 1) * HD], k["hidT"][:, c, g * N_CMP:(g + 1) * N_CMP], w[:, at:at + HD], start=True, stop=True)
        mm.then_inc(s["cmp_kv"], 1)
    pe.wait_ge(s["cmp_k"], 1)
    for g in range(NSA_G):
        mm = pe.transpose(k["ps"][4][:, g * N_CMP:(g + 1) * N_CMP], k["kcmp"][0:N_CMP, g, :, :].rearrange("p a b -> p (a b)"), con(k, "ident")[0:N_CMP, 0:N_CMP])
    mm.then_inc(s["cmp_kT"], 1)
    pe.wait_ge(s["cmp_kT_read"], 1)
    pe.wait_ge(s["gate_sig"], 1)
    for odd in range(2):
        for n in range(NSA_H):
            t, h = n // 8, n % 8 * 2 + odd
            lo, g = HD * odd, h // (NSA_H // NSA_G)
            at = n * N_CMP
            mm = pe.matmul(k["ps"][5 + odd][:, at:at + N_CMP], k["nqT"][lo:lo + HD, h // 2, t * P:(t + 1) * P], k["kcmpT"][lo:lo + HD, g, :], start=True, stop=True)
    mm.then_inc(s["cmp_score"], 1)


def cmp_vector(k, dve):
    s, vs = k["sig"], k["vs"]
    pos = PARAM_AT["pos_kv"][0]
    turned(k, dve, 26)
    for r in range(2):
        for g in range(NSA_G):
            src = k["kcvT"][:, g, :].rearrange("p (n l) -> p l n", l=CMP_STRIDE)[:, :, r:r + N_CMP]
            add = spread_last(k["params"][:, pos + r * CMP_STRIDE:pos + (r + 1) * CMP_STRIDE], N_CMP)
            dve.tensor_tensor(k["blk"][:, r * CMP_STRIDE:(r + 1) * CMP_STRIDE, g, :], src, add, ALU.add).then_inc(s["cmp_blk"], 1)
    for c in range(2):
        dve.wait_ge(s["cmp_sig"], c + 1)
        dve.tensor_tensor(k["hidT"][:, c, :], k["hidT"][:, c, :], k["ps"][4 + c][:, 0:NSA_G * N_CMP], ALU.mult).then_inc(s["cmp_hid"], 1)
    dve.wait_ge(s["cmp_kv"], 2)
    vs.mark(dve.tensor_copy(k["kcr"][0:N_CMP, :], k["ps"][7][0:N_CMP, 0:S]))
    vs.mark(dve.tensor_copy(k["vcmp"][0:N_CMP, :, :].rearrange("p a b -> p (a b)"), k["ps"][7][0:N_CMP, S:2 * S]))
    vs.wait()
    kc = k["kcmp"][0:N_CMP, :, :, :]
    rope_rotate(dve, vs, kc[:, :, 0, :], k["kcr"][0:N_CMP, :].rearrange("p (h x) -> p h x", h=NSA_G), NSA_G, HD // 2,
                angle(k, k["cos"], "e", N_CMP), angle(k, k["sin"], "e", N_CMP), k["tmp_dve"])
    dve.tensor_copy(kc[:, :, 1, :], kc[:, :, 0, :]).then_inc(s["cmp_k"], 1)
    dve.wait_ge(s["cmp_kT"], 1)
    dve.tensor_copy(k["kcmpT"][:, :, :].rearrange("p a b -> p (a b)"), k["ps"][4][:, 0:NSA_G * N_CMP]).then_inc(s["cmp_kT_read"], 1)
    dve.wait_ge(s["cmp_score"], 1)
    add, one = con(k, "cmp_add"), con(k, "cmp_one")
    for t in range(TT):
        for odd in range(2):
            sc = k["ps"][5 + odd][:, t * 8 * N_CMP:(t + 1) * 8 * N_CMP].rearrange("p (h n) -> p h n", h=8)
            vs.mark(dve.scalar_tensor_tensor(out=k["cp"][:, t, odd:NSA_H:2, :], in0=sc, scalar=HD ** -0.5, in1=spread(add[:, t * N_CMP:(t + 1) * N_CMP], 8),
                                             op0=ALU.mult, op1=ALU.add))
    vs.wait()
    for t in range(TT):
        vs.mark(dve.tensor_reduce(k["cs"][:, t, :], k["cp"][:, t, :, :], AX_X, ALU.max))
    vs.wait()
    for t in range(TT):
        dve.tensor_tensor(k["cp"][:, t, :, :], k["cp"][:, t, :, :], spread_last(k["cs"][:, t, :], N_CMP), ALU.subtract).then_inc(s["cmp_arg"], 1)
    dve.wait_ge(s["cmp_exp"], 2)
    for t in range(TT):
        vs.mark(dve.tensor_tensor(k["cp"][:, t, :, :], k["cp"][:, t, :, :], spread(one[:, t * N_CMP:(t + 1) * N_CMP], NSA_H), ALU.mult))
    vs.wait()
    for t in range(TT):
        vs.mark(dve.tensor_reduce(k["cs"][:, t, :], k["cp"][:, t, :, :], AX_X, ALU.add))
    vs.wait()
    vs.mark(dve.tensor_scalar(k["cs"][:, :, :], k["cs"][:, :, :], TINY, None, ALU.max))
    vs.wait()
    vs.mark(dve.reciprocal(k["cs"][:, :, :], k["cs"][:, :, :]))
    vs.wait()
    dve.wait_ge(s["gate_sig"], 1)
    vs.mark(dve.tensor_tensor(k["cs"][:, :, :], k["cs"][:, :, :], k["gates"][:, :, 0:48:3], ALU.mult))
    vs.wait()
    for t in range(TT):
        dve.tensor_tensor(k["cp"][:, t, :, :], k["cp"][:, t, :, :], spread_last(k["cs"][:, t, :], N_CMP), ALU.mult).then_inc(s["cmp_p"], 1)


def cmp_scalar(k, act):
    s = k["sig"]
    act.wait_ge(s["gate_in"], 1)
    act.activation(k["gates"][:, :, :].rearrange("p a b -> p (a b)"), k["ps"][6][:, 0:96], ACT.Sigmoid).then_inc(s["gate_sig"], 1)
    for c in range(2):
        act.wait_ge(s["cmp_h"], c + 1)
        act.activation(k["hidT"][:, c, :], k["ps"][4 + c][:, 0:NSA_G * N_CMP], ACT.Sigmoid).then_inc(s["cmp_sig"], 1)
    for t in range(TT):
        act.wait_ge(s["cmp_arg"], t + 1)
        act.activation(k["cp"][:, t, :, :], k["cp"][:, t, :, :], ACT.Exp).then_inc(s["cmp_exp"], 1)




def program(nc, src, out):
    ctx = ExitStack()
    with ctx:
        def sem(name):
            return ctx.enter_context(nc.semaphore(name))

        k = {"src": src}
        k["sig"] = {n: sem(n) for n in SIGNALS}
        k["landed"] = [sem(f"landed{i}") for i in range(3)]
        k["moe_landed"] = [sem(f"moe_landed{i}") for i in range(MOE_STEPS)]
        k["plan"], before, k["moe_free"], after = plan_ring(k["sig"])
        k["ps"] = [ctx.enter_context(nc.psum_tensor(f"bank{i}", [P, 512], F32)) for i in range(8)]

        def place(stack, name, shape, dt=F32):
            t = stack.enter_context(nc.sbuf_tensor(name, shape, dt))
            k[name] = t
            return t

        ring = [place(ctx, f"slot{i}", [P, SLOT]) for i in range(3)]
        place(ctx, "x", [P, TT, D])
        place(ctx, "hT", [P, KT, S])
        place(ctx, "xn", [P, TT, D])
        place(ctx, "consts", [P, CONST_W])
        place(ctx, "params", [P, PARAM_W])
        work = place(ctx, "work", [P, 2560])
        k["gate"], k["sg"], k["up"] = work[:, 1024:1536], work[:, 1536:2048], work[:, 2048:2560]
        k["junk"] = work[:, 0:512]
        k["tmp_dve"] = work[:, 0:2048].rearrange("p (a b) -> p a b", a=4)
        place(ctx, "posi", [P, 5], I32)
        place(ctx, "posf", [P, 5])
        place(ctx, "rope", [P, 3, ANGLE_W])
        place(ctx, "sin", [P, ANGLE_W])
        place(ctx, "cos", [P, ANGLE_W])
        place(ctx, "ss", [P, 8])
        place(ctx, "ss4", [P, TT, 2])
        place(ctx, "stat", [P, 2, 8])
        place(ctx, "small", [P, 32])
        place(ctx, "quarter", [P, 1])
        place(ctx, "one_row", [P, P])
        place(ctx, "wtok", [P, TT, E])

        one = ExitStack()
        a = ExitStack()
        place(a, "y_hi", [P, D], F32R)
        place(a, "y_lo", [P, D], F32R)
        place(a, "shareT_hi", [P, S], F32R)
        place(a, "shareT_lo", [P, S], F32R)
        a.close()
        place(one, "rows", [P, 6 * D])
        k["qk"] = k["rows"][:, 0:2 * D].rearrange("p (t d) -> p t d", t=TT)
        mix = ExitStack()
        place(mix, "c_mix", [P, 4, SSM_TILES * 32])
        place(mix, "ssm_small", [P, 14 * SSM_TILES])
        a = ExitStack()
        place(a, "ada_b", [P, 6 * D])
        place(a, "cond_wide", [P, KT, P])
        place(a, "cond", [P, 3 * KT])
        place(a, "gains", [P, 4, D])
        a.close()
        place(mix, "uT", [P, 4, S])
        place(mix, "ysT", [P, 4, S])
        place(mix, "v", [P, TT, 512])
        a = ExitStack()
        place(a, "table", [P, 2, 2, SSM_Q, S])
        place(a, "trig", [P, 2, SSM_Q, S])
        place(a, "ssm_a", [P, 2, S])
        place(a, "ssm_b", [P, 2, S])
        place(a, "ssm_r", [P, 2, 2, 2, S])
        a.close()
        k["ssm_sig"] = k["trig"][:, :, :, :].rearrange("p a b c -> p a (b c)")[:, :, 0:512]
        k["tmp_pool"] = k["trig"][:, :, :, :].rearrange("p a b c -> p (a b) c").rearrange("p (x y) c -> p x (y c)", x=4)
        a = ExitStack()
        place(a, "qkT", [P, 8, S])
        place(a, "yaT", [P, 4, S])
        place(a, "masked", [P, 2, 3 * P])
        place(a, "prob", [P, 2, 3 * P])
        place(a, "probT", [P, 2, 3 * P])
        place(a, "msig", [P, 2, 512])
        place(a, "catT", [P, KT, S])
        k["qT"], k["kT"] = k["qkT"][:, 0:4, :], k["qkT"][:, 4:8, :]
        a.close()
        mix.close()
        first = dict(k)
        moe = ExitStack()
        ring.append(place(moe, "slot3", [P, SLOT]))
        tables = ExitStack()
        place(tables, "tie", [P, E, E])
        place(tables, "b_down", [P, D])
        place(tables, "rank_eq", [P, E, E])
        place(tables, "rank_gt", [P, E, E])
        tables.close()
        place(moe, "moe_down_hi", [P, STEP_TILES * D], F32R)
        place(moe, "moe_down_lo", [P, STEP_TILES * D], F32R)
        for name in ("logits", "rank", "wexp"):
            place(moe, name, [P, TT, E])
        place(moe, "wT", [P, S])
        for name in ("chosen", "place"):
            place(moe, name, [P, TT, E])
        place(moe, "most", [P, 1])
        place(moe, "crowded", [P, 1], I32)
        place(moe, "ones", [P, TT, MOE_SLOTS])
        place(moe, "share", [P, TT, MOE_SLOTS])
        place(moe, "xeT", [P, KT, MOE_SLOTS])
        place(moe, "moe_hid_hi", [P, 2, STEP_COLS], F32R)
        place(moe, "moe_hid_lo", [P, 2, STEP_COLS], F32R)
        k["moe_gate"], k["moe_sg"], k["moe_up"] = work[:, 1024:1280], work[:, 1536:1792], work[:, 2048:2304]
        k["total"] = k["hT"][:, :, :].rearrange("p a b -> p (a b)").rearrange("p (t d) -> p t d", t=TT)
        moe.close()
        one.close()
        k["ring"] = first["ring"] = ring
        first.update({n: k[n] for n in ("tie", "b_down", "rank_eq", "rank_gt", "logits", "rank", "wexp", "wT", "chosen", "place", "most", "crowded",
                                          "ones", "share", "xeT", "moe_hid_hi", "moe_hid_lo", "moe_down_hi", "moe_down_lo", "moe_gate", "moe_sg", "moe_up", "total")})
        ffn = ExitStack()
        for name in ("ffn_hi", "ffn_lo"):
            place(ffn, name, [P, 3, PIECE], F32R)
        for name in ("hT_hi", "hT_lo"):
            place(ffn, name, [P, KT, S], F32R)
        for name in ("act_hi", "act_lo"):
            place(ffn, name, [P, STEP_TILES, S], F32R)
        place(ffn, "final_row", [P, D])
        ffn.close()
        hy = ExitStack()
        second = dict(k)

        def place2(stack, target, name, shape):
            target[name] = stack.enter_context(nc.sbuf_tensor(f"{name}_{'h' if target is second else 'n'}", shape, F32))

        for name, shape in (("hya", [P, TT, HYA]), ("hyb", [P, TT, 512]), ("hyv", [P, TT, 512]), ("hyr", [P, TT, 512]), ("lora_n", [P, TT, 384]),
                            ("loraT", [P, 3, S]), ("mq", [P, TT, 768]), ("mkv", [P, TT, 1024]), ("catT", [P, KT, S]), ("tmp_pool", [P, 4, 128])):
            place2(hy, second, name, shape)
        a = ExitStack()
        for name, shape in (("gqT", [P, 2, S]), ("gkT", [P, 2, S]), ("gaT", [P, S]), ("gz", [P, 2, S]), ("gla", [P, 2, S]), ("gb", [P, 2, S]), ("gd", [P, 2, S]),
                            ("ge", [P, 3, 2, S]), ("gdec", [P, 2, NCH]), ("kdecT", [P, 2, S]), ("qintraT", [P, 2, S]), ("qinterT", [P, 2, S]),
                            ("kdec", [P, TT, 2, P]), ("AT", [P, 2, 4, P]), ("state", [P, 2, 3, P])):
            place2(a, second, name, shape)
        second["rsig"], second["rsig2"] = k["xn"][:, :, 0:512], k["xn"][:, :, 512:1024]
        a.close()
        a = ExitStack()
        for name, shape in (("mk", [P, TT, 768]), ("mqT", [P, MLA_H, S]), ("mkT", [P, MLA_H, S]), ("masked", [P, 2, 3 * P]), ("prob", [P, 2, 3 * P]), ("probT", [P, 2, 3 * P])):
            place2(a, second, name, shape)
        a.close()
        hy.close()
        third = dict(k)
        ns = ExitStack()
        for name, shape in (("nq", [P, TT, 1024]), ("kcv", [P, TT, 512]), ("nkv", [P, TT, 512]), ("nwv", [P, TT, 512]), ("kd", [P, TT, 2, NSA_G, 2, HD]),
                            ("tmp_pool", [P, 4, 512]), ("nqT", [P, 8, S]), ("ksT", [P, 4, S]), ("kwT", [P, 4, S]), ("gates", [P, TT, 48]),
                            ("vcmp", [P, NSA_G, HD]), ("cp", [P, TT, NSA_H, N_CMP]), ("cs", [P, TT, NSA_H]), ("masked", [P, 2, 3 * P])):
            place2(ns, third, name, shape)
        a = ExitStack()
        for name, shape in (("kcvT", [P, 4, S]), ("blk", [P, CMP_LEN, NSA_G, N_CMP]), ("hidT", [P, 2, NSA_G * N_CMP]), ("kcr", [P, S]), ("kcmp", [P, NSA_G, 2, HD]),
                            ("kcmpT", [P, NSA_G, N_CMP])):
            place2(a, third, name, shape)
        a.close()
        a = ExitStack()
        for name, shape in (("catT", [P, KT, S]), ("prob", [P, 2, 3 * P]), ("probT", [P, 2, 3 * P])):
            place2(a, third, name, shape)
        a.close()
        ns.close()

        block = ctx.enter_context(nc.Block())
        f = first
        gain = {}
        lo = PARAM_AT["ffn_g"][0]
        for q in range(4):
            gain["ffn", q] = k["params"][:, lo + q * KT:lo + (q + 1) * KT]
        lo = PARAM_AT["mix_g"][0]
        for q in range(2):
            gain["mix", q] = k["params"][:, lo + q * KT:lo + (q + 1) * KT]
        moba, mla, nsa = moba_units(f), mla_units(second), nsa_units(third)
        qk_jobs = [[(k["xn"][:, t, (2 * b + c) * P:(2 * b + c + 1) * P], P, (2 * c + t) * P) for c in range(2) for t in range(TT)] for b in range(4)]
        qk_reads = [(f["qkT"][:, 2 * b:2 * b + 2, :].rearrange("p a b -> p (a b)"), P, 2 * S) for b in range(4)]
        qkv_dst = [f["qk"][:, :, 0:512], f["qk"][:, :, 512:1024], f["v"]]
        mix_bank = lambda half, t: k["ps"][4 + 2 * half + t][:, :]
        moe_rows = lambda half, t: f["total"][:, t, half * 512:(half + 1) * 512]

        @block.sync
        def _(sp):
            def stream(items):
                for it in items:
                    if it.free is not None:
                        sp.wait_ge(*it.free)
                    name, i = it.src
                    sp.dma_start(k["ring"][it.slot][:, 0:it.width], src[name][i, :, 0:it.width]).then_inc(k["landed"][it.slot], 16)

            sp.dma_start(f["cond"][:, 2 * KT:3 * KT], src["c"]).then_inc(k["sig"]["cond_loaded"], 16)
            sp.dma_start(f["ada_b"][0:1, :], src["ada_b"]).then_inc(k["sig"]["cond_loaded"], 16)
            stream(before)
            sweeps(f, sp, moe_sync)
            stream(after)
            for t in range(TT):
                sp.wait_ge(k["sig"]["xn_ready"], 2 * 8 + t + 1)
                sp.dma_start(out.rearrange("o (t p) d -> p (o t) d", p=P)[:, t, :], k["xn"][:, t, :]).then_inc(k["sig"]["stored"], 16)
            sp.wait_ge(k["sig"]["stored"], 16 * TT)

        @block.scalar
        def _(act):
            s = k["sig"]
            for each in (k, f, second, third):
                each["acs"] = Steps(act, s["step_act"]) if each is k else k["acs"]
            act.dma_start(k["params"][:, :], src["params"]).then_inc(s["small_loaded"], 16)
            act.dma_start(k["consts"][:, :], src["consts"]).then_inc(s["small_loaded"], 16)
            act.dma_start(k["posi"][:, :], src["pos"]).then_inc(s["small_loaded"], 16)
            act.dma_start(k["x"][:, :, :], src["x"].rearrange("o (t p) d -> p (o t) d", p=P)).then_inc(s["small_loaded"], 16)
            act.dma_start(f["gains"][:, :, :], src["gains"]).then_inc(s["rows_loaded"], 16)
            for name in ("moe_xe_read", "moe_y_read"):
                act.drain().then_inc(s[name], 2)
            cond_scalar(f, act)
            ada_scalar(f, act, range(0, 6, 2))
            angles_scalar(f, act)
            ssm_prep_scalar(f, act)
            ada_scalar(f, act, range(6, 10, 2))
            norm_scalar(f, act, 0, None)
            ada_scalar(f, act, range(10, ADA_UNITS, 2))
            end_phase(k, act, 1)
            act.wait_ge(s["proj_ready"], 1)
            act.activation(f["uT"][:, 0:2, :].rearrange("p a b -> p (a b)"), k["ps"][0][:, :], ACT.Copy).then_inc(s["proj_act"], 1)
            ssm_trig_scalar(f, act, 0)
            ssm_trig_scalar(f, act, 1)
            project_read(f, act, 0, 2, qkv_dst, (0, 1))
            ssm_trig_scalar(f, act, 2)
            ssm_trig_scalar(f, act, 3)
            project_read(f, act, 0, 2, qkv_dst, (2,))
            ssm_scalar(f, act)
            end_phase(k, act, 2)
            turn_read(f, act, qk_reads, 0, 0)
            attend_scalar(f, act, moba, HD ** -0.5)
            merge_scalar(f, act)
            post_norm_scalar(f, act, s["out_ready"], (1, 2, 3, 4), mix_bank, s["mix_square"], 0)
            end_phase(k, act, 3)
            act.dma_start(f["tie"][:, :, :], src["tie"]).then_inc(s["tie_loaded"], 16)
            act.dma_start(f["b_down"][0:E, :], src["b_down"]).then_inc(s["tie_loaded"], 16)
            norm_scalar(f, act, 1, None)
            router_scalar(f, act)
            sweeps(f, act, moe_scalar)
            act.wait_ge(s["moe_done"], 1)
            post_norm_scalar(f, act, None, None, moe_rows, s["moe_square"], 1)
            end_phase(k, act, 4)
            norm_split_scalar(k, act, 2, gain["ffn", 0], 0)
            ffn_scalar(k, act, 0)
            norm_scalar(k, act, 3, gain["mix", 0])
            project_read(second, act, 0, 8, [second["hya"], second["hyb"], second["hyv"], second["hyr"]])
            lora_norm_scalar(second, act)
            turn_read(second, act, hy_turn_jobs(second)[1], 4, 0)
            lora_read(second, act, 0)
            gla_scalar(second, act)
            turn_read(second, act, gla_turn_jobs(second)[1], 10, 0)
            end_phase(k, act, 5)
            turn_read(second, act, mla_turn_jobs(second)[1], 12, 0)
            attend_scalar(second, act, mla, MLA_QK ** -0.5)
            norm_split_scalar(k, act, 4, gain["ffn", 1], 1)
            ffn_scalar(k, act, 1)
            norm_split_scalar(k, act, 5, gain["ffn", 2], 2)
            ffn_scalar(k, act, 2)
            norm_scalar(k, act, 6, gain["mix", 1])
            end_phase(k, act, 6)
            project_read(third, act, 0, 16, [third["nq"][:, :, 0:512], third["nq"][:, :, 512:1024], third["kcv"], third["nkv"], third["nwv"]])
            turn_read(third, act, nsa_turn_jobs(third)[1], 20, 0)
            cmp_scalar(third, act)
            end_phase(k, act, 7)
            attend_scalar(third, act, nsa, HD ** -0.5)
            norm_split_scalar(k, act, 7, gain["ffn", 3], 3)
            act.dma_start(k["final_row"][:, :], src["final_norm"]).then_inc(s["final_loaded"], 16)
            ffn_scalar(k, act, 3)
            for t in range(TT):
                act.wait_ge(s["x_ready"], 2 * 8 + t + 1)
                act.activation(k["xn"][:, t, :], k["x"][:, t, :], ACT.Square, accum_out=k["ss"][:, t:t + 1]).then_inc(s["sumsq"], 1)
            act.wait_ge(s["meansq"], 9)
            act.activation(k["ss"][:, 2:4], k["ss"][:, 2:4], ACT.Sqrt).then_inc(s["root"], 1)

        @block.vector
        def _(dve):
            s = k["sig"]
            for each in (k, f, second, third):
                each["vs"] = Steps(dve, s["step_dve"]) if each is k else k["vs"]
            cond_vector(f, dve)
            ada_vector(f, dve, range(1, 6, 2))
            dve.wait_ge(s["small_loaded"], 64)
            dve.drain().then_inc(s["x_ready"], 2)
            angles_vector(f, dve)
            ssm_prep_vector(f, dve)
            dve.drain().then_inc(s["ssm_prep_dve"], 1)
            scale_row(f, dve, 1, 0, True)
            ada_vector(f, dve, range(7, 10, 2))
            norm_vector(f, dve, 0, None, (f["rows"][:, D:2 * D], f["rows"][:, 0:D]))
            scale_row(f, dve, 2, 1, False)
            ada_vector(f, dve, range(11, ADA_UNITS, 2))
            scale_row(f, dve, 4, 2, True)
            scale_row(f, dve, 5, 3, False)
            end_phase(k, dve, 1)
            ssm_angles(f, dve, k["vs"], 0, *angles_of(f, 0), s["trig_arg"])
            ssm_angles(f, dve, k["vs"], 2, *angles_of(f, 2), s["trig_arg"])
            dve.wait_ge(s["proj_ready"], 2)
            dve.tensor_copy(f["uT"][:, 2:4, :].rearrange("p a b -> p (a b)"), k["ps"][1][:, :]).then_inc(s["proj_dve"], 1)
            ssm_vector(f, dve, range(0, 6))
            project_read(f, dve, 1, 2, qkv_dst, (0,))
            ssm_vector(f, dve, range(6, 12))
            project_read(f, dve, 1, 2, qkv_dst, (1,))
            dve.wait_ge(s["proj_dve"], 3)
            rope_rotate(dve, k["vs"], k["xn"][:, 1, :].rearrange("p (h x) -> p h x", h=16), f["qk"][:, 1, :].rearrange("p (h x) -> p h x", h=16), 16, 32,
                        angle(k, k["cos"], "a1"), angle(k, k["sin"], "a1"), k["tmp_dve"])
            dve.drain().then_inc(s["rope_dve"], 1)
            ssm_vector(f, dve, range(12, 16))
            ssm_skip(f, dve, 3)
            project_read(f, dve, 1, 2, qkv_dst, (2,))
            ssm_gate_vector(f, dve)
            end_phase(k, dve, 2)
            turn_read(f, dve, qk_reads, 0, 1)
            attend_vector(f, dve, moba, HD ** -0.5)
            merge_vector(f, dve)
            post_norm_vector(f, dve, mix_bank, s["mix_square"], 0, 2)
            end_phase(k, dve, 3)
            dve.drain().then_inc(s["arena_free"], 1)
            norm_vector(f, dve, 1, None, (f["rows"][:, 4 * D:5 * D], f["rows"][:, 3 * D:4 * D]))
            router_vector(f, dve)
            sweeps(f, dve, moe_vector)
            dve.drain().then_inc(s["moe_done"], 1)
            dve.wait_ge(s["moe_done"], 1)
            post_norm_vector(f, dve, moe_rows, s["moe_square"], 1, 5)
            end_phase(k, dve, 4)
            norm_split_vector(k, dve, 2, gain["ffn", 0], 0)
            ffn_vector(k, dve, 0)
            norm_vector(k, dve, 3, gain["mix", 0])
            project_read(second, dve, 1, 8, [second["hya"], second["hyb"], second["hyv"], second["hyr"]])
            lora_norm_vector(second, dve)
            turn_read(second, dve, hy_turn_jobs(second)[1], 4, 1)
            lora_read(second, dve, 1)
            gla_vector(second, dve)
            turn_read(second, dve, gla_turn_jobs(second)[1], 10, 1)
            end_phase(k, dve, 5)
            mla_rows(second, dve, k["vs"], 1, s["mla_dve"], k["tmp_dve"])
            turn_read(second, dve, mla_turn_jobs(second)[1], 12, 1)
            attend_vector(second, dve, mla, MLA_QK ** -0.5)
            add_out_vector(k, dve, 4)
            norm_split_vector(k, dve, 4, gain["ffn", 1], 1)
            ffn_vector(k, dve, 1)
            norm_split_vector(k, dve, 5, gain["ffn", 2], 2)
            ffn_vector(k, dve, 2)
            norm_vector(k, dve, 6, gain["mix", 1])
            end_phase(k, dve, 6)
            project_read(third, dve, 1, 16, [third["nq"][:, :, 0:512], third["nq"][:, :, 512:1024], third["kcv"], third["nkv"], third["nwv"]])
            dve.wait_ge(s["proj_dve"], 13)
            nsa_rows(third, dve, k["vs"], 1, s["nsa_dve"], k["tmp_dve"])
            turn_read(third, dve, nsa_turn_jobs(third)[1], 20, 1)
            cmp_vector(third, dve)
            end_phase(k, dve, 7)
            attend_vector(third, dve, nsa, HD ** -0.5)
            add_out_vector(k, dve, 8)
            norm_split_vector(k, dve, 7, gain["ffn", 3], 3)
            ffn_vector(k, dve, 3)
            dve.wait_ge(s["sumsq"], 18)
            dve.tensor_scalar(k["ss"][:, 2:4], k["ss"][:, 0:2], 1.0 / D, EPS, ALU.mult, ALU.add).then_inc(s["meansq"], 1)
            dve.wait_ge(s["root"], 9)
            k["vs"].mark(dve.reciprocal(k["ss"][:, 4:6], k["ss"][:, 2:4]))
            k["vs"].wait()
            dve.wait_ge(s["final_loaded"], 16)
            for t in range(TT):
                dve.scalar_tensor_tensor(out=k["xn"][:, t, :], in0=k["x"][:, t, :], scalar=k["ss"][:, 4 + t:5 + t], in1=k["final_row"][:, :], op0=ALU.mult, op1=ALU.mult)\
                   .then_inc(s["xn_ready"], 1)

        @block.tensor
        def _(pe):
            s = k["sig"]
            for name, ahead in (("down_done", 2), ("moe_down", 2), ("moe_xe", 1), ("moe_wT", 1), ("moe_share", 2)):
                pe.drain().then_inc(s[name], ahead)
            ada_tensor(f, pe, range(0, 10))
            pe.wait_ge(s["ada_act"], 5)
            pe.wait_ge(s["ada_dve"], 5)
            norm_tensor(k, pe, 0)
            ada_tensor(f, pe, range(10, ADA_UNITS))
            end_phase(k, pe, 1)
            u_tensor(f, pe)
            ssm_tensor(f, pe)
            pe.wait_ge(s["rope_dve"], 1)
            pe.wait_ge(s["rope_pool"], 1)
            end_phase(k, pe, 2)
            turn_tensor(f, pe, qk_jobs, 0)
            turned(k, pe, 4)
            attend_tensor(f, pe, moba)
            merge_tensor(f, pe)
            pe.wait_ge(s["merged"], KT)
            out_tensor(f, pe, ["w_out0", "w_out1"], 0, f["catT"])
            end_phase(k, pe, 3)
            norm_tensor(k, pe, 1)
            router_tensor(f, pe)
            sweeps(f, pe, moe_tensor)
            pe.drain().then_inc(s["moe_tensor_done"], 1)
            end_phase(k, pe, 4)
            norm_tensor(k, pe, 2)
            ffn_tensor(k, pe, 0)
            norm_tensor(k, pe, 3)
            project_tensor(second, pe, [f"hy{j}" for j in range(4)], 8, [HYA, 512, 512, 512], k["hT"], KT, 8)
            pe.wait_ge(s["lora_n"], 4)
            pe.wait_ge(s["proj_act"], 8)
            pe.wait_ge(s["proj_dve"], 8)
            turn_tensor(second, pe, hy_turn_jobs(second)[0], 4)
            turned(k, pe, 10)
            lora_tensor(second, pe)
            pe.wait_ge(s["lora_act"], 4)
            pe.wait_ge(s["lora_dve"], 4)
            gla_tensor(second, pe)
            pe.wait_ge(s["gla_out"], 2)
            turn_tensor(second, pe, gla_turn_jobs(second)[0], 10)
            end_phase(k, pe, 5)
            pe.wait_ge(s["mla_dve"], 1)
            pe.wait_ge(s["mla_pool"], 1)
            turn_tensor(second, pe, mla_turn_jobs(second)[0], 12)
            turned(k, pe, 20)
            attend_tensor(second, pe, mla)
            pe.wait_ge(s["o_copied"], 16)
            out_tensor(second, pe, ["hy_out0", "hy_out1"], 4, second["catT"])
            norm_tensor(k, pe, 4)
            ffn_tensor(k, pe, 1)
            norm_tensor(k, pe, 5)
            ffn_tensor(k, pe, 2)
            norm_tensor(k, pe, 6)
            end_phase(k, pe, 6)
            project_tensor(third, pe, [f"nsa{j}" for j in range(5)], 16, [512] * 5, k["hT"], KT, 16)
            pe.wait_ge(s["nsa_dve"], 1)
            pe.wait_ge(s["nsa_pool"], 1)
            pe.wait_ge(s["proj_act"], 13)
            pe.wait_ge(s["proj_dve"], 13)
            turn_tensor(third, pe, nsa_turn_jobs(third)[0], 20)
            turned(k, pe, 30)
            cmp_tensor(third, pe)
            pe.wait_ge(s["cmp_p"], 2)
            end_phase(k, pe, 7)
            attend_tensor(third, pe, nsa)
            pe.wait_ge(s["o_copied"], 32)
            out_tensor(third, pe, ["nsa_out0", "nsa_out1"], 8, third["catT"])
            norm_tensor(k, pe, 7)
            ffn_tensor(k, pe, 3)

        @block.gpsimd
        def _(pool):
            s = k["sig"]
            for each in (k, f, second, third):
                each["pos"] = Steps(pool, s["step_pool"]) if each is k else k["pos"]
            end_phase(k, pool, 1)
            pool.wait_ge(s["ssm_prep_dve"], 1)
            for q in (1, 3):
                if q == 3:
                    pool.wait_ge(s["trig_done"], 4)
                ssm_angles(f, pool, k["pos"], q, *angles_of(f, q), s["trig_arg_pool"])
            pool.wait_ge(s["trig_done"], 8)
            pool.wait_ge(s["proj_act"], 4)
            rope_rotate(pool, k["pos"], k["xn"][:, 0, :].rearrange("p (h x) -> p h x", h=16), f["qk"][:, 0, :].rearrange("p (h x) -> p h x", h=16), 16, 32,
                        angle(k, k["cos"], "a0"), angle(k, k["sin"], "a0"), f["tmp_pool"])
            pool.drain().then_inc(s["rope_pool"], 1)
            end_phase(k, pool, 2)
            end_phase(k, pool, 3)
            end_phase(k, pool, 4)
            end_phase(k, pool, 5)
            mla_rows(second, pool, k["pos"], 0, s["mla_pool"], second["tmp_pool"])
            end_phase(k, pool, 6)
            pool.wait_ge(s["proj_act"], 13)
            nsa_rows(third, pool, k["pos"], 0, s["nsa_pool"], third["tmp_pool"])
            end_phase(k, pool, 7)




def by_tile(w):
    return w.reshape(w.shape[0] // P, P, w.shape[1]).transpose(1, 0, 2)


def flat(*parts):
    return np.concatenate([p.reshape(P, -1) for p in parts], axis=1)


def columns(v):
    v = v.reshape(-1, v.shape[-1] // P, P)
    return v.transpose(2, 0, 1).reshape(P, -1)


def on_rows(a, rows=P):
    out = np.zeros((P,) + a.shape[1:], a.dtype)
    out[:a.shape[0]] = a
    return out


def expert_steps(gate, up, down_):
    n = gate.shape[1] // STEP_COLS
    out = np.empty((n, P, STEP_WIDTH), gate.dtype)
    for j, w in enumerate((gate, up)):
        out[:, :, j * STEP_GATE:(j + 1) * STEP_GATE] = w.reshape(KT, P, n, STEP_COLS).transpose(2, 1, 0, 3).reshape(n, P, -1)
    out[:, :, 2 * STEP_GATE:] = down_.reshape(n, STEP_TILES, P, D).transpose(0, 2, 1, 3).reshape(n, P, -1)
    return out


def ffn_pieces(gate, up, down_):
    n = gate.shape[1] // STEP_COLS
    both = np.stack([w.reshape(KT, P, n, STEP_COLS) for w in (gate, up)], axis=3)
    gate_up = both.transpose(2, 1, 0, 3, 4).reshape(n, P, -1)
    return np.concatenate([gate_up, down_.reshape(n, STEP_TILES, P, D).transpose(0, 2, 1, 3).reshape(n, P, -1)], axis=2)


def column_items(w, cols):
    return np.stack([flat(by_tile(w[:, a:a + cols])) for a in range(0, w.shape[1], cols)])


def constants():
    c = {}
    i, j = np.arange(P)[:, None], np.arange(P)[None, :]
    c["ident"] = (i == j).astype(np.float32)
    c["before"] = (i < j).astype(np.float32)
    tri = np.where(j <= i, 0.0, NEG).astype(np.float32)
    c["causal"] = np.concatenate([tri, np.zeros((P, P), np.float32), tri], axis=1)
    c["inv_freq_64"] = np.broadcast_to(np.power(np.float32(10000.0), -np.arange(32, dtype=np.float32) / np.float32(32)), (P, 32))
    c["inv_freq_32"] = np.broadcast_to(np.power(np.float32(10000.0), -np.arange(16, dtype=np.float32) / np.float32(16)), (P, 16))
    c["time"] = np.broadcast_to(np.arange(S, dtype=np.float32), (P, S))
    c["gla_mask"] = ((i <= j) & (i // CHUNK == j // CHUNK)).astype(np.float32)
    c["gla_keep"] = np.broadcast_to((np.arange(S) % CHUNK != 0).astype(np.float32), (P, S))
    tok = np.arange(TT)[None, :, None] * P + np.arange(P)[:, None, None]
    seen = (np.arange(N_CMP) * CMP_STRIDE + CMP_LEN - 1)[None, None, :] <= tok
    c["cmp_add"] = np.where(seen, 0.0, NEG).reshape(P, -1)
    c["cmp_one"] = seen.astype(np.float32).reshape(P, -1)
    packed = np.concatenate([c[n].astype(np.float32) for n, _ in CONSTS], axis=1)
    e = np.arange(E)
    tie = np.broadcast_to((e[None, :] < e[:, None]).astype(np.float32), (P, E, E))
    return np.ascontiguousarray(packed), np.ascontiguousarray(tie)


def layout(a):
    arr = {}
    w = {n: v[0] for n, v in a.items() if v.ndim > 1}
    states = lambda v: v.reshape(SSM_TILES, P).T

    def block_c(c):
        out = np.zeros((2, SSM_N, SSM_TILES, 2, SSM_C), c.dtype)
        cc = c.reshape(SSM_TILES, 2, SSM_C, SSM_N)
        for g in range(2):
            out[g, :, :, g, :] = cc[:, g].transpose(2, 0, 1)
        return out.reshape(P, -1)

    def block_b(b):
        out = np.zeros((4, 2, SSM_C, 4, 4, 2, SSM_N), b.dtype)
        bb = b.reshape(4, 4, 2, SSM_N, SSM_C)
        for jj in range(4):
            for g in range(2):
                out[jj, g, :, :, jj, g, :] = bb[:, jj, g].transpose(2, 0, 1)
        return out.reshape(P, -1)

    b_gu = np.stack([w["b_gate"].reshape(E, KT, P), w["b_up"].reshape(E, KT, P)], axis=2)
    params = {
        "lam_re": states(w["ssm_lam_re"]), "lam_im": states(w["ssm_lam_im"]),
        "log_dt": states(np.repeat(w["ssm_log_dt"], SSM_N)), "d_skip": columns(a["ssm_d"]),
        "router_b": np.broadcast_to(w["router_b"], (P, E)), "ffn_g": columns(a["ffn_norm_2"]), "mix_g": columns(a["mix_norm_2"]),
        "q_norm": columns(a["mla_q_norm_2"]), "kv_norm": columns(a["mla_kv_norm_2"]), "b_a": columns(a["gla_b_a_2"]),
        "out_norm": np.broadcast_to(w["gla_out_norm_2"], (P, GLA_DV)), "w_a2": on_rows(w["gla_w_a2_2"]),
        "pos_kv": np.concatenate([w["nsa_pos_k_2"].T, w["nsa_pos_v_2"].T]), "ct_re": block_c(w["ssm_c_re"]), "ct_im": block_c(w["ssm_c_im"]),
        "router_w": flat(by_tile(w["router_w"])), "b_gu": b_gu.transpose(3, 0, 1, 2).reshape(P, -1)}
    arr["params"] = np.concatenate([params[n] for n, _ in PARAMS], axis=1)
    arr["consts"], arr["tie"] = constants()
    p1, p2 = a["positions"][0], a["positions_2"][0]
    ends = np.zeros(P, p2.dtype)
    ends[:N_CMP] = p2[np.arange(N_CMP) * CMP_STRIDE + CMP_LEN - 1]
    arr["pos"] = np.stack([p1[:P], p1[P:], p2[:P], p2[P:], ends], axis=1).astype(np.int32)
    arr["x"] = a["x"]
    arr["c"] = columns(a["c"])
    arr["ada_b"] = a["ada_b"]
    arr["gains"] = np.broadcast_to(np.stack([w[n] for n in ("mix_pre_g", "mix_post_g", "ffn_pre_g", "ffn_post_g")]), (P, 4, D))
    arr["b_down"] = w["b_down"]
    arr["final_norm"] = np.broadcast_to(a["final_norm_2"], (P, D))
    arr["ada"] = column_items(w["ada_w"], ADA_COLS)
    arr["w_in"] = column_items(w["w_in"][:, 0:2048], 512)
    arr["ssm_b"] = flat(block_b(w["ssm_b_re"]), block_b(w["ssm_b_im"]))[None]
    arr["w_glu"] = flat(by_tile(w["ssm_w_glu"]))[None]
    gs, ga = w["w_in"][:, 2048:3072], w["w_in"][:, 3072:4096]
    arr["merge"] = np.stack([flat(by_tile(gs[:, m:m + 256]), by_tile(ga[:, m:m + 256]), by_tile(w["w_ssm_branch"][:, m:m + 256]),
                                  by_tile(w["w_attn_branch"][:, m:m + 256])) for m in range(0, D, 256)])
    arr["w_out"] = column_items(w["w_out"], 512)
    arr["moe"] = np.concatenate([expert_steps(w["w_gate"][e], w["w_up"][e], w["w_down"][e]) for e in range(E)])
    g2, u2, d2 = (a[n].reshape(4, *a[n].shape[2:]) for n in ("ffn_w_gate_2", "ffn_w_up_2", "ffn_w_down_2"))
    arr["ffn"] = np.concatenate([ffn_pieces(g2[q], u2[q], d2[q]) for q in range(4)])
    hy = w["hy_w_in_2"]
    cut = np.cumsum([0, Q_LORA, KV_LORA, MLA_ROPE, 256, 256, 512, GLA_RANK, 512])
    part = [hy[:, cut[i]:cut[i + 1]] for i in range(8)]
    items = [np.concatenate([part[0], part[1], part[2], part[6]], axis=1), np.concatenate([part[3], part[4]], axis=1), part[5], part[7]]
    arr["hy_in"] = np.zeros((4, P, 4096), hy.dtype)
    for j, it in enumerate(items):
        arr["hy_in"][j, :, :it.shape[1] * KT] = flat(by_tile(it))
    arr["lora"] = flat(by_tile(w["mla_w_uq_2"]), w["mla_w_ukv_2"])[None]
    arr["hy_out"] = column_items(w["hy_w_out_2"], 512)
    ns = w["nsa_w_in_2"]
    cut = np.cumsum([0, 1024] + [256] * 6 + [48])
    part = [ns[:, cut[i]:cut[i + 1]] for i in range(8)]
    kcv = np.stack([part[1].reshape(D, NSA_G, HD), part[2].reshape(D, NSA_G, HD)], axis=2).reshape(D, 512)
    arr["nsa_in"] = np.stack([flat(by_tile(q)) for q in (part[0][:, 0:512], part[0][:, 512:1024], kcv,
                                                         np.concatenate([part[3], part[4]], axis=1), np.concatenate([part[5], part[6]], axis=1))])
    w1 = np.concatenate([w[n].reshape(CMP_LEN, HD, CMP_HID).transpose(1, 0, 2).reshape(HD, -1) for n in ("nsa_ck_w1_2", "nsa_cv_w1_2")])
    arr["nsa_c"] = flat(w1, by_tile(part[7]), w["nsa_ck_w2_2"], w["nsa_cv_w2_2"])[None]
    arr["nsa_out"] = column_items(w["nsa_w_out_2"], 512)
    return {n: np.ascontiguousarray(v) for n, v in arr.items()}


def kernel(**inputs):
    import concourse.bacc as bacc
    from concourse.bass_utils import run_bass_kernel_spmd

    arrays = layout({n: np.asarray(v) for n, v in inputs.items()})
    nc = bacc.Bacc("TRN2", target_bir_lowering=False, num_devices=1)
    src = {n: nc.dram_tensor(f"in_{n}", v.shape, mybir.dt.from_np(v.dtype), kind="ExternalInput").ap() for n, v in arrays.items()}
    out = nc.dram_tensor("out", (1, S, D), F32, kind="ExternalOutput").ap()
    program(nc, src, out)
    result = run_bass_kernel_spmd(nc, [{f"in_{n}": v for n, v in arrays.items()}], core_ids=[0])
    return result.results[0]["out"]
```
